# Optimizing a Trainium2 kernel written in Bass

```python
import math
import jax
import jax.numpy as jnp
from jax import lax
import numpy as np

D_MODEL = 2048
BATCH = 1
SEQ = 512
DEPTH = 1

MIX_WIDTH = D_MODEL
SB_HEAD_DIM = 128
SB_WIDTH = MIX_WIDTH // 2
SB_HEADS = SB_WIDTH // SB_HEAD_DIM
RW_HEAD_DIM = 64
RW_WIDTH = MIX_WIDTH - SB_WIDTH
RW_HEADS = RW_WIDTH // RW_HEAD_DIM
LORA_W = 64
LORA_A = 64
LORA_G = 160
RW_SHIFT_COLS = 3 * RW_WIDTH + LORA_W + LORA_A + LORA_G
IN_COLS = 3 * SB_WIDTH + RW_SHIFT_COLS
Q_BLOCK = 128
PLE_DIM = 256
N_GROUPS = 4
EXPERTS_PER_GROUP = 8
N_EXPERTS = N_GROUPS * EXPERTS_PER_GROUP
TOP_K_IN_GROUP = 2
EXPERT_FF = 512
MOE_BLOCK = 128
RMS_EPS = 1e-6
GN_EPS = 64e-5

kernel_name = "hymba_sb_rwkv7_hmoe_trunk"

def rms_norm(x, g=None, eps=RMS_EPS):
    xf = x.astype(jnp.float32)
    y = xf * lax.rsqrt(jnp.mean(xf * xf, axis=-1, keepdims=True) + eps)
    if g is not None:
        y = y * g.astype(jnp.float32)
    return y.astype(x.dtype)

def token_shift(u, mu):
    prev = jnp.pad(u[:, :-1], ((0, 0), (1, 0), (0, 0)))
    return u + mu * (prev - u)

def stick_breaking_attention(q, k, v):
    B, H, S, hd = q.shape
    n_blocks = S // Q_BLOCK
    scale = 1.0 / math.sqrt(hd)
    kf = k.astype(jnp.float32)
    vf = v.astype(jnp.float32)
    q_blocks = q.astype(jnp.float32).reshape(B, H, n_blocks, Q_BLOCK, hd).transpose(2, 0, 1, 3, 4)
    key_pos = jnp.arange(S)

    def one_block(args):
        q_blk, b_idx = args
        z = jnp.einsum("bhqd,bhkd->bhqk", q_blk, kf) * scale
        q_pos = b_idx * Q_BLOCK + jnp.arange(Q_BLOCK)
        causal = key_pos[None, :] < q_pos[:, None]
        log_keep = jnp.where(causal, jax.nn.log_sigmoid(-z), 0.0)
        later = lax.cumsum(log_keep, axis=3, reverse=True) - log_keep
        weights = jnp.where(causal, jnp.exp(jax.nn.log_sigmoid(z) + later), 0.0)
        return jnp.einsum("bhqk,bhkd->bhqd", weights, vf)

    out = lax.map(one_block, (q_blocks, jnp.arange(n_blocks)))
    return out.transpose(1, 2, 0, 3, 4).reshape(B, H, S, hd)

def rwkv7_scan(r, decay, k, v, a_in, b_in):
    B, S, H, N = r.shape

    def step(state, inp):
        r_t, w_t, k_t, v_t, a_t, b_t = inp
        sa = jnp.einsum("bhvk,bhk->bhv", state, a_t)
        state = (state * w_t[:, :, None, :]
                 + sa[..., None] * b_t[:, :, None, :]
                 + v_t[..., None] * k_t[:, :, None, :])
        return state, jnp.einsum("bhvk,bhk->bhv", state, r_t)

    xs = tuple(t.transpose(1, 0, 2, 3) for t in (r, decay, k, v, a_in, b_in))
    state0 = jnp.zeros((B, H, N, N), jnp.float32)
    _, ys = lax.scan(step, state0, xs)
    return ys.transpose(1, 0, 2, 3)

def rwkv7_time_mix(u, w0, w2, a0, a2, g2, k_k, k_a, r_k, ln_g, ln_b):
    f32 = lambda t: t.astype(jnp.float32)
    uf = f32(u)
    B, S, _ = u.shape
    r = uf[..., :RW_WIDTH]
    k = uf[..., RW_WIDTH:2 * RW_WIDTH]
    v = uf[..., 2 * RW_WIDTH:3 * RW_WIDTH]
    o = 3 * RW_WIDTH
    w_lo = uf[..., o:o + LORA_W]
    a_lo = uf[..., o + LORA_W:o + LORA_W + LORA_A]
    g_lo = uf[..., o + LORA_W + LORA_A:]
    w = -jax.nn.softplus(-(f32(w0) + jnp.tanh(w_lo) @ f32(w2))) - 0.5
    decay = jnp.exp(-jnp.exp(w))
    a = jax.nn.sigmoid(f32(a0) + a_lo @ f32(a2))
    g = jax.nn.sigmoid(g_lo) @ f32(g2)
    heads = lambda t: t.reshape(B, S, RW_HEADS, RW_HEAD_DIM)
    kk = heads(k * f32(k_k))
    kk = kk * lax.rsqrt(jnp.sum(kk * kk, axis=-1, keepdims=True) + 1e-12)
    k = heads(k * (1.0 + (a - 1.0) * f32(k_a)))
    r, v, decay, a = heads(r), heads(v), heads(decay), heads(a)
    y = rwkv7_scan(r, decay, k, v, -kk, kk * a)
    mean = jnp.mean(y, axis=-1, keepdims=True)
    var = jnp.mean(jnp.square(y - mean), axis=-1, keepdims=True)
    y = ((y - mean) * lax.rsqrt(var + GN_EPS)).reshape(B, S, RW_WIDTH) * f32(ln_g) + f32(ln_b)
    bonus = jnp.sum(r * k * f32(r_k), axis=-1, keepdims=True) * v
    y = y + bonus.reshape(B, S, RW_WIDTH)
    return (y * g).astype(u.dtype)

def hier_moe(h, router_g, router_g_b, router_e, router_e_b, w_up, w_down):
    T, D = h.shape
    TK = T * TOP_K_IN_GROUP
    hf = h.astype(jnp.float32)
    g_prob = jax.nn.softmax(hf @ router_g.astype(jnp.float32) + router_g_b.astype(jnp.float32), axis=-1)
    g_w, grp = lax.top_k(g_prob, 1)
    e_logits = (hf @ router_e.astype(jnp.float32) + router_e_b.astype(jnp.float32)).reshape(T, N_GROUPS, EXPERTS_PER_GROUP)
    e_sel = e_logits[jnp.arange(T), grp[:, 0]]
    e_w, e_idx = lax.top_k(jax.nn.softmax(e_sel, axis=-1), TOP_K_IN_GROUP)
    e_w = e_w / jnp.sum(e_w, axis=-1, keepdims=True)
    weights = (g_w * e_w).reshape(-1)
    expert_id = (grp * EXPERTS_PER_GROUP + e_idx).reshape(-1)
    token_id = jnp.repeat(jnp.arange(T), TOP_K_IN_GROUP)
    order = jnp.argsort(expert_id)
    sorted_ids = expert_id[order]
    tok_sorted = token_id[order]
    w_sorted = weights[order]
    counts = jnp.bincount(expert_id, length=N_EXPERTS)
    starts = jnp.cumsum(counts) - counts
    padded = ((counts + MOE_BLOCK - 1) // MOE_BLOCK) * MOE_BLOCK
    pad_ends = jnp.cumsum(padded)
    pad_starts = pad_ends - padded
    dest = pad_starts[sorted_ids] + (jnp.arange(TK) - starts[sorted_ids])
    n_blocks = (TK + MOE_BLOCK - 1) // MOE_BLOCK + N_EXPERTS
    x_pad = jnp.zeros((n_blocks * MOE_BLOCK, D), h.dtype).at[dest].set(h[tok_sorted])
    blk_expert = jnp.minimum(jnp.searchsorted(pad_ends, jnp.arange(n_blocks) * MOE_BLOCK, side="right"), N_EXPERTS - 1)

    def expert_block(args):
        xb, e = args
        gate, up = jnp.split(xb @ w_up[e], 2, axis=-1)
        return (jax.nn.silu(gate) * up) @ w_down[e]

    y_pad = lax.map(expert_block, (x_pad.reshape(n_blocks, MOE_BLOCK, D), blk_expert)).reshape(-1, D)
    y = y_pad[dest] * w_sorted[:, None].astype(y_pad.dtype)
    return jax.ops.segment_sum(y, tok_sorted, num_segments=T)

def setup_inputs(seed: int = 0) -> dict:
    key = jax.random.key(seed)
    counter = [0]

    def nk():
        counter[0] += 1
        return jax.random.fold_in(key, counter[0])

    def normal(shape, scale):
        return jax.random.normal(nk(), shape, jnp.float32) * scale

    def gain(shape):
        return 1.0 + 0.05 * jax.random.normal(nk(), shape, jnp.float32)

    def uniform(shape, lo, hi):
        return jax.random.uniform(nk(), shape, jnp.float32, lo, hi)

    L, D = DEPTH, D_MODEL
    return {
        "x": normal((BATCH, SEQ, D), 1.0),
        "p": normal((L, BATCH, SEQ, PLE_DIM), 1.0),
        "ln1_g": gain((L, D)),
        "w_in": normal((L, D, IN_COLS), D ** -0.5),
        "sb_q_g": gain((L, SB_HEAD_DIM)),
        "sb_k_g": gain((L, SB_HEAD_DIM)),
        "sb_out_g": gain((L, SB_HEAD_DIM)),
        "rw_mu": uniform((L, RW_SHIFT_COLS), 0.0, 1.0),
        "rw_w0": uniform((L, RW_WIDTH), -5.0, 1.0),
        "rw_w2": normal((L, LORA_W, RW_WIDTH), 0.5 * LORA_W ** -0.5),
        "rw_a0": normal((L, RW_WIDTH), 0.5),
        "rw_a2": normal((L, LORA_A, RW_WIDTH), 0.5 * LORA_A ** -0.5),
        "rw_g2": normal((L, LORA_G, RW_WIDTH), LORA_G ** -0.5),
        "rw_k_k": 0.85 + normal((L, RW_WIDTH), 0.05),
        "rw_k_a": gain((L, RW_WIDTH)),
        "rw_r_k": normal((L, RW_HEADS, RW_HEAD_DIM), 0.1),
        "rw_ln_g": gain((L, RW_WIDTH)),
        "rw_ln_b": normal((L, RW_WIDTH), 0.01),
        "w_out": normal((L, D, D), D ** -0.5),
        "ln2_g": gain((L, D)),
        "router_g": normal((L, D, N_GROUPS), D ** -0.5),
        "router_g_b": normal((L, N_GROUPS), 0.01),
        "router_e": normal((L, D, N_EXPERTS), D ** -0.5),
        "router_e_b": normal((L, N_EXPERTS), 0.01),
        "w_up": normal((L, N_EXPERTS, D, 2 * EXPERT_FF), D ** -0.5),
        "w_down": normal((L, N_EXPERTS, EXPERT_FF, D), EXPERT_FF ** -0.5),
        "ple_proj": normal((L, PLE_DIM, D), PLE_DIM ** -0.5),
        "ple_gate": normal((L, D, D), D ** -0.5),
        "ple_norm_g": gain((L, D)),
    }

def reference(x, p, ln1_g, w_in, sb_q_g, sb_k_g, sb_out_g, rw_mu, rw_w0, rw_w2, rw_a0, rw_a2, rw_g2,
              rw_k_k, rw_k_a, rw_r_k, rw_ln_g, rw_ln_b, w_out, ln2_g, router_g, router_g_b, router_e,
              router_e_b, w_up, w_down, ple_proj, ple_gate, ple_norm_g):
    B, S, D = x.shape
    heads_sb = lambda t: t.reshape(B, S, SB_HEADS, SB_HEAD_DIM)
    for i in range(DEPTH):
        xn = rms_norm(x, ln1_g[i])
        proj = xn @ w_in[i]
        q = rms_norm(heads_sb(proj[..., :SB_WIDTH]), sb_q_g[i])
        k = rms_norm(heads_sb(proj[..., SB_WIDTH:2 * SB_WIDTH]), sb_k_g[i])
        v = heads_sb(proj[..., 2 * SB_WIDTH:3 * SB_WIDTH])
        sb = stick_breaking_attention(q.transpose(0, 2, 1, 3), k.transpose(0, 2, 1, 3), v.transpose(0, 2, 1, 3))
        sb = rms_norm(sb.transpose(0, 2, 1, 3), sb_out_g[i]).reshape(B, S, SB_WIDTH).astype(x.dtype)
        u = token_shift(proj[..., 3 * SB_WIDTH:], rw_mu[i])
        rw = rwkv7_time_mix(u, rw_w0[i], rw_w2[i], rw_a0[i], rw_a2[i], rw_g2[i], rw_k_k[i], rw_k_a[i],
                            rw_r_k[i], rw_ln_g[i], rw_ln_b[i])
        x = x + jnp.concatenate([sb, rw], axis=-1) @ w_out[i]
        hn = rms_norm(x, ln2_g[i])
        x = x + hier_moe(hn.reshape(B * S, D), router_g[i], router_g_b[i], router_e[i], router_e_b[i],
                         w_up[i], w_down[i]).reshape(B, S, D)
        gate = jax.nn.sigmoid(rms_norm(x) @ ple_gate[i])
        x = x + rms_norm((p[i] @ ple_proj[i]) * gate, ple_norm_g[i])
    return x


_drawn_inputs = setup_inputs


def setup_inputs(seed=0):
    import zlib

    import numpy as np

    out = dict(_drawn_inputs(seed))
    spreads = {}
    factors = {'sb_k_g': 2.827,
     'rw_w2': 3.648,
     'rw_k_k': 3.616,
     'rw_k_a': 2.858,
     'rw_ln_g': 2.855,
     'rw_ln_b': 8.0,
     'router_g_b': 5.668,
     'router_e_b': 13.244}
    for name, (base, spread) in spreads.items():
        noise = np.random.default_rng([zlib.crc32(name.encode()), seed]).standard_normal(out[name].shape)
        drawn = base * np.exp(spread * noise) if base else spread * noise
        out[name] = jnp.asarray(drawn.astype(out[name].dtype))
    for name, factor in factors.items():
        out[name] = (out[name] * factor).astype(out[name].dtype)
    return out
```

```python
from contextlib import ExitStack
import math

import concourse.bass as bass
from concourse import mybir

F32 = mybir.dt.float32
I32 = mybir.dt.int32
ALU = mybir.AluOpType
ACT = mybir.ActivationFunctionType
AX_X = mybir.AxisListType.X
ds = bass.ds

P = 128
RMS_EPS = 1e-6
GN_EPS = 64e-5
CHUNK = 64
SLOTS = 64
BANK = 512


class Stage:

    def __init__(self, nc, tag):
        self.nc, self.tag, self.stack, self.sems = nc, tag, ExitStack(), []

    def __enter__(self):
        self.stack.__enter__()
        return self

    def __exit__(self, *exc):
        self.stack.__exit__(*exc)
        if exc[0] is None:
            self.nc.clear_and_free_semaphores(self.sems)
            self.nc.all_engine_barrier()

    def sb(self, name, shape, dt=F32):
        return self.stack.enter_context(self.nc.sbuf_tensor(f"{self.tag}_{name}", list(shape), dt))

    def psum(self):
        return self.stack.enter_context(self.nc.psum_tensor(f"{self.tag}_ps", [P, 8, BANK], F32))

    def sem(self, name):
        self.sems.append(self.nc.alloc_semaphore(f"{self.tag}_{name}"))
        return self.sems[-1]

    def block(self):
        return self.stack.enter_context(self.nc.Block())


class Chain:

    def __init__(self, eng, sem, base=0):
        self.eng, self.sem, self.base, self.n = eng, sem, base, 0

    def go(self, ins):
        self.n += 1
        ins.then_inc(self.sem, 1)

    def wait(self):
        self.eng.wait_ge(self.sem, self.base + self.n)

    def __call__(self, ins):
        self.go(ins)
        self.wait()


def signal(eng, ins, sem, value):
    ins.then_inc(sem, 1)
    eng.wait_ge(sem, value)


def wait_apart(eng, sem, value):
    eng.wait_ge(sem, value)
    eng.nop(nofuse=True)


def constants(nc, keep):
    def sb(name, shape, dt=F32):
        return keep.enter_context(nc.sbuf_tensor(f"const_{name}", shape, dt))

    C = {}
    for name in ("ident", "ones", "neg_ones", "later_neg", "after", "head_sum", "head_mean", "tmp", "first_down",
                 "first_up"):
        C[name] = sb(name, [P, P])
    C["levels"] = sb("levels", [P, 5, P])
    C["seen"] = sb("seen", [P, 2, P])
    C["blocks"] = sb("blocks", [P, 6, P])
    C["no_carry"] = sb("no_carry", [P, 512])
    with Stage(nc, "const") as st:
        steps, vsteps, pool_done = st.sem("pool_steps"), st.sem("vector_steps"), st.sem("pool_done")
        block = st.block()

        @block.gpsimd
        def _(pool):
            do = Chain(pool, steps)
            do(pool.memset(C["ident"][:], 0.0))
            do(pool.affine_select(C["ident"][:], C["ident"][:], [[-1, P]], ALU.not_equal, 1.0, base=0,
                                  channel_multiplier=1))
            for name, value in (("ones", 1.0), ("neg_ones", -1.0), ("after", 1.0), ("later_neg", -1.0),
                                ("head_sum", 0.0), ("head_mean", 0.0), ("no_carry", 1.0), ("blocks", 1.0)):
                do(pool.memset(C[name][:], value))
            do(pool.affine_select(C["after"][:], C["after"][:], [[1, P]], ALU.is_gt, 0.0, base=0,
                                  channel_multiplier=-1))
            do(pool.affine_select(C["later_neg"][:], C["later_neg"][:], [[-1, P]], ALU.is_ge, 0.0, base=0,
                                  channel_multiplier=1))
            for h in range(2):
                half = slice(64 * h, 64 * h + 64)
                do(pool.memset(C["head_sum"][half, half], 1.0))
                do(pool.memset(C["head_mean"][half, half], 1.0 / 64))
            do(pool.memset(C["no_carry"][:].rearrange("p (c t) -> p c t", t=CHUNK)[:, :, 0:1], 0.0))
            for n in range(6):
                w = 2 << n
                blk = C["blocks"][:, n, :].rearrange("p (b w) -> p b w", w=w)
                do(pool.affine_select(blk, blk, [[-w, P // w], [0, w]], ALU.is_ge, 0.0, base=0,
                                      channel_multiplier=1))
                do(pool.affine_select(blk, blk, [[w, P // w], [0, w]], ALU.is_ge, 0.0, base=w - 1,
                                      channel_multiplier=-1))
            pool.nop().then_inc(pool_done, 1)

        @block.vector
        def _(v):
            v.wait_ge(pool_done, 1)
            do = Chain(v, vsteps)
            do(v.tensor_tensor(C["seen"][:, 0, :], C["blocks"][:, 5, :], C["after"][:], ALU.mult))
            do(v.tensor_tensor(C["seen"][:, 1, :], C["seen"][:, 0, :], C["ident"][:], ALU.add))
            do(v.tensor_tensor(C["tmp"][:], C["blocks"][:, 0, :], C["ident"][:], ALU.subtract))
            do(v.tensor_tensor(C["first_up"][:], C["tmp"][:], C["after"][:], ALU.mult))
            do(v.tensor_tensor(C["first_down"][:], C["tmp"][:], C["first_up"][:], ALU.subtract))
            for n in range(5):
                do(v.tensor_tensor(C["tmp"][:], C["blocks"][:, n + 1, :], C["blocks"][:, n, :], ALU.subtract))
                do(v.tensor_tensor(C["levels"][:, n, :], C["tmp"][:], C["after"][:], ALU.mult))
    return C


def norm_transpose(nc, tag, C, rows, out_T, gain=None, rows_dram=None, load=None):
    TT, D = rows.shape[1], rows.shape[2]
    KT = D // P
    with Stage(nc, tag) as st:
        sq = st.sb("squares", [P, D])
        normed = st.sb("normed", [P, TT, D])
        ss = st.sb("ss", [P, 3, TT])
        g = st.sb("gain", [P, KT]) if gain is not None else None
        ps = st.psum()
        landed = [st.sem(f"landed{t}") for t in range(TT)]
        gain_in, stored, squared, inverse, rooted = (st.sem(n) for n in ("gain", "stored", "squared", "inverse",
                                                                           "rooted"))
        scaled, turned, vsteps = st.sem("scaled"), st.sem("turned"), st.sem("vector_steps")
        kept = st.sem("kept_vector"), st.sem("kept_scalar")
        block = st.block()

        @block.sync
        def _(sp):
            if load is not None:
                for t in range(TT):
                    sp.dma_start(rows[:, t, :], load[t * P:(t + 1) * P, :]).then_inc(landed[t], 16)
            if g is not None:
                with nc.allow_non_contiguous_dma("a gain per partition"):
                    sp.dma_start(g[:], gain.rearrange("(k p) -> p k", p=P)).then_inc(gain_in, 16)
            if rows_dram is not None:
                for t in range(TT):
                    sp.wait_ge(scaled, t + 1)
                    sp.dma_start(rows_dram[t * P:(t + 1) * P, :], normed[:, t, :]).then_inc(stored, 16)
                sp.wait_ge(stored, 16 * TT)

        @block.scalar
        def _(act):
            for t in range(TT):
                if load is not None:
                    act.wait_ge(landed[t], 16)
                signal(act, act.activation(sq[:], rows[:, t, :], ACT.Square, accum_out=ss[:, 0, t:t + 1]),
                       squared, t + 1)
            act.wait_ge(inverse, 1)
            signal(act, act.activation(ss[:, 2, :], ss[:, 1, :], ACT.Sqrt), rooted, 1)
            if g is not None:
                act.wait_ge(gain_in, 16)
            for k in range(1, KT, 2):
                act.wait_ge(turned, k + 1)
                act.activation(out_T[:, k, :], ps[:, k % 4, :], ACT.Copy,
                               scale=g[:, k:k + 1] if g is not None else 1.0).then_inc(kept[1], 1)

        @block.vector
        def _(v):
            do = Chain(v, vsteps)
            v.wait_ge(squared, TT)
            do(v.tensor_scalar(ss[:, 1, :], ss[:, 0, :], 1.0 / D, RMS_EPS, ALU.mult, ALU.add))
            signal(v, v.reciprocal(ss[:, 1, :], ss[:, 1, :]), inverse, 1)
            v.wait_ge(rooted, 1)
            for t in range(TT):
                v.tensor_scalar(normed[:, t, :], rows[:, t, :], ss[:, 2, t:t + 1], None,
                                ALU.mult).then_inc(scaled, 1)
            if g is not None:
                v.wait_ge(gain_in, 16)
            for k in range(0, KT, 2):
                v.wait_ge(turned, k + 1)
                if g is not None:
                    ins = v.tensor_scalar(out_T[:, k, :], ps[:, k % 4, :], g[:, k:k + 1], None, ALU.mult)
                else:
                    ins = v.tensor_copy(out_T[:, k, :], ps[:, k % 4, :])
                ins.then_inc(kept[0], 1)

        @block.tensor
        def _(pe):
            pe.wait_ge(scaled, TT)
            for k in range(KT):
                if k >= 4:
                    pe.wait_ge(kept[k % 2], (k - 4) // 2 + 1)
                for t in range(TT):
                    ins = pe.transpose(ps[:, k % 4, t * P:(t + 1) * P], normed[:, t, k * P:(k + 1) * P],
                                       C["ident"][:])
                ins.then_inc(turned, 1)


def project_rows(nc, tag, act_T, weights, halves, vector, scalar=None, setup=None, sync=None, finish=None,
                 scalar_first=None):
    KT = act_T.shape[1]
    SLOT, RING = 2, 4
    LOADS = KT // SLOT
    with Stage(nc, tag) as st:
        ring = st.sb("weights", [P, RING, SLOT, 1024])
        ps = st.psum()
        landed = [st.sem(f"landed{r}") for r in range(RING)]
        used, product, taken_v, taken_s = (st.sem(n) for n in ("used", "product", "taken_v", "taken_s"))
        extra = setup(st) if setup else {}
        block = st.block()
        src = weights.rearrange("(k p) n -> p k n", p=P)
        loads = [(half, n) for half in range(halves) for n in range(LOADS)]
        n_s = 4 if scalar else 0
        n_v = 8 - n_s

        @block.sync
        def _(sp):
            if sync:
                sync(sp, extra)
            for i, (half, n) in enumerate(loads):
                r = i % RING
                if i >= RING:
                    before, m = loads[i - RING]
                    if m == LOADS - 1:
                        sp.wait_ge(product, 8 * (before + 1))
                    else:
                        sp.wait_ge(used, before * (LOADS - 1) + m + 1)
                sp.dma_start(ring[:, r, :, :], src[:, n * SLOT:(n + 1) * SLOT, half * 1024:(half + 1) * 1024]
                             ).then_inc(landed[r], 16)

        @block.tensor
        def _(pe):
            for i, (half, n) in enumerate(loads):
                r = i % RING
                pe.wait_ge(landed[r], 16 * (i // RING + 1))
                if n == 0 and half:
                    pe.wait_ge(taken_v, half * n_v)
                    if n_s:
                        pe.wait_ge(taken_s, half * n_s)
                for s in range(SLOT):
                    k = n * SLOT + s
                    for t in range(4):
                        for c in range(2):
                            ins = pe.matmul(ps[:, 2 * t + c, :], act_T[:, k, t * P:(t + 1) * P],
                                            ring[:, r, s, c * BANK:(c + 1) * BANK],
                                            start=(k == 0), stop=(k == KT - 1))
                            if k == KT - 1:
                                ins.then_inc(product, 1)
                if n < LOADS - 1:
                    ins.then_inc(used, 1)

        @block.vector
        def _(v):
            for half in range(halves):
                for b in range(0, 8, 2 if scalar else 1):
                    v.wait_ge(product, half * 8 + b + 1)
                    vector(v, half, b, ps, extra, taken_v)
            if finish:
                finish[0](v, extra, taken_v, taken_s)

        @block.scalar
        def _(act):
            if scalar_first:
                for half in range(halves):
                    for b in range(8):
                        act.wait_ge(product, half * 8 + b + 1)
                        scalar_first(act, half, b, ps, extra, taken_v)
            if scalar:
                for half in range(halves):
                    for b in range(1, 8, 2):
                        act.wait_ge(product, half * 8 + b + 1)
                        scalar(act, half, b, ps, extra, taken_s)
            if finish:
                finish[1](act, extra, taken_v, taken_s)


def value_projection(nc, norm_T, w_v, v_rows):
    def vector(v, half, b, ps, extra, done):
        v.tensor_copy(v_rows[:, b // 2, (b % 2) * BANK:(b % 2 + 1) * BANK], ps[:, b, :]).then_inc(done, 1)

    def scalar(act, half, b, ps, extra, done):
        act.activation(v_rows[:, b // 2, (b % 2) * BANK:(b % 2 + 1) * BANK], ps[:, b, :], ACT.Copy).then_inc(done, 1)

    project_rows(nc, "values", norm_T, w_v, 1, vector, scalar)


def attention(nc, C, norm_T, w_in, v_rows, q_gain, k_gain, out_gain, mixed_T, heads, width):
    KT, S = norm_T.shape[1], norm_T.shape[2]
    HD, NB = P, S // P
    V_STEPS, S_STEPS = 2, 8
    with Stage(nc, "attn") as st:
        w_qk = st.sb("w_qk", [P, 2, KT, HD])
        gains = st.sb("gains", [P, 3])
        square = st.sb("square", [P, 2, S])
        root = st.sb("root", [P, 2, S])
        qk_T = st.sb("qk_T", [P, 2, S])
        log1p = st.sb("log1p", [P, NB, S])
        softplus = st.sb("softplus", [P, NB, S])
        weight = st.sb("weight", [P, NB, S])
        v_head = st.sb("v_head", [P, NB, HD])
        out_raw = st.sb("out_raw", [P, S])
        ps = st.psum()
        BQ, BO, BN, BZ = 0, 2, 3, 4
        sem = {n: st.sem(n) for n in (
            "gain_in", "wq_in", "wk_in", "projected", "squared", "summed", "inverse", "rooted", "qk_ready", "scored",
            "soft_in", "soft", "masked", "exponent", "weighted", "weight_ready", "v_ready", "output", "out_copied",
            "out_square", "out_summed", "out_mean", "gain_scaled", "out_inverse", "out_rooted", "mixed", "v_steps", "s_steps")}
        block = st.block()
        src = w_in.rearrange("(k p) n -> p k n", p=P)

        @block.sync
        def _(sp):
            with nc.allow_non_contiguous_dma("a gain per partition"):
                for n, g in enumerate((q_gain, k_gain, out_gain)):
                    sp.dma_start(gains[:, n:n + 1], g.rearrange("(p o) -> p o", o=1)).then_inc(sem["gain_in"], 16)

            def load(h, first):
                for n, s in ((0, "wq_in"), (1, "wk_in")):
                    if not first:
                        sp.wait_ge(sem["projected"], 2 * (h - 1) + n + 1)
                    sp.dma_start(w_qk[:, n, :, :], src[:, :, ds(h * HD + n * width, HD)]).then_inc(sem[s], 16)
            load(0, True)
            with sp.Fori(1, heads) as h:
                load(h, False)

        @block.tensor
        def _(pe):
            def project(h, n):
                pe.wait_ge(sem["wq_in" if n == 0 else "wk_in"], (h + 1) * 16)
                for k in range(KT):
                    ins = pe.matmul(ps[:, BQ + n, :], w_qk[:, n, k, :], norm_T[:, k, :], start=(k == 0),
                                    stop=(k == KT - 1))
                ins.then_inc(sem["projected"], 1)

            def norms(h):
                for n in range(2):
                    pe.wait_ge(sem["squared"], 2 * h + n + 1)
                    pe.matmul(ps[:, BO + n, :], C["ones"][:], square[:, n, :], start=True, stop=True
                              ).then_inc(sem["summed"], 1)

            def scores(h):
                pe.wait_ge(sem["qk_ready"], 2 * h + 2)
                for b in range(NB):
                    pe.matmul(ps[:, BZ + b, b * P:], qk_T[:, 1, b * P:(b + 1) * P], qk_T[:, 0, b * P:],
                              start=True, stop=True).then_inc(sem["scored"], 1)

            def exponents(h):
                pe.wait_ge(sem["masked"], NB * h + NB)
                for b in range(NB):
                    for j in range(b, NB):
                        ins = pe.matmul(ps[:, BZ + b, j * P:], C["later_neg" if j == b else "neg_ones"][:],
                                        softplus[:, j, j * P:], start=False, stop=(j == NB - 1),
                                        skip_group_check=True)
                    ins.then_inc(sem["exponent"], 1)

            def output(h):
                pe.wait_ge(sem["v_ready"], h + 1)
                for b in range(NB):
                    pe.wait_ge(sem["weight_ready"], NB * h + b + 1)
                    ins = pe.matmul(ps[:, BO, b * P:], v_head[:, b, :], weight[:, b, b * P:], start=(b == 0),
                                    stop=(b == NB - 1))
                ins.then_inc(sem["output"], 1)
                pe.wait_ge(sem["out_square"], h + 1)
                pe.matmul(ps[:, BN, :], C["ones"][:], square[:, 0, :], start=True, stop=True
                          ).then_inc(sem["out_summed"], 1)

            def head(h, last):
                scores(h)
                if not last:
                    project(h + 1, 0)
                exponents(h)
                if not last:
                    project(h + 1, 1)
                output(h)
                if not last:
                    pe.wait_ge(sem["mixed"], h + 1)
                    norms(h + 1)

            project(0, 0)
            project(0, 1)
            norms(0)
            with pe.Fori(0, heads - 1) as h:
                head(h, False)
            head(heads - 1, True)

        @block.scalar
        def _(act):
            def squares(h):
                for n in range(2):
                    act.wait_ge(sem["projected"], 2 * h + n + 1)
                    act.activation(square[:, n, :], ps[:, BQ + n, :], ACT.Square).then_inc(sem["squared"], 1)
                for n in range(2):
                    act.wait_ge(sem["inverse"], 2 * h + n + 1)
                    act.activation(root[:, n, :], root[:, n, :], ACT.Sqrt).then_inc(sem["rooted"], 1)

            def head(h, last):
                do = Chain(act, sem["s_steps"], h * S_STEPS)
                act.activation(v_head[:], v_rows[:, :, ds(h * HD, HD)], ACT.Copy).then_inc(sem["v_ready"], 1)
                for b in range(NB):
                    act.wait_ge(sem["scored"], NB * h + b + 1)
                    do.go(act.activation(log1p[:, b, b * P:], ps[:, BZ + b, b * P:], ACT.Abs))
                do.wait()
                for b in range(NB):
                    do.go(act.activation(log1p[:, b, b * P:], log1p[:, b, b * P:], ACT.Exp, scale=-1.0))
                do.wait()
                for b in range(NB):
                    act.activation(log1p[:, b, b * P:], log1p[:, b, b * P:], ACT.Ln, bias=1.0
                                   ).then_inc(sem["soft_in"], 1)
                assert do.n == S_STEPS
                for b in range(NB):
                    act.wait_ge(sem["exponent"], NB * h + b + 1)
                    act.activation(weight[:, b, b * P:], ps[:, BZ + b, b * P:], ACT.Exp).then_inc(sem["weighted"], 1)
                act.wait_ge(sem["output"], h + 1)
                signal(act, act.activation(out_raw[:], ps[:, BO, :], ACT.Copy), sem["out_copied"], h + 1)
                act.activation(square[:, 0, :], out_raw[:], ACT.Square).then_inc(sem["out_square"], 1)
                act.wait_ge(sem["out_inverse"], h + 1)
                act.activation(root[:, 0, :], root[:, 0, :], ACT.Sqrt).then_inc(sem["out_rooted"], 1)
                if not last:
                    act.wait_ge(sem["mixed"], h + 1)
                    squares(h + 1)

            squares(0)
            with act.Fori(0, heads - 1) as h:
                head(h, False)
            head(heads - 1, True)

        @block.vector
        def _(v):
            def normalise(h):
                do = Chain(v, sem["v_steps"], h * V_STEPS)
                for n in range(2):
                    v.wait_ge(sem["summed"], 2 * h + n + 1)
                    do(v.tensor_scalar(root[:, n, :], ps[:, BO + n, :], 1.0 / HD, RMS_EPS, ALU.mult, ALU.add))
                    v.reciprocal(root[:, n, :], root[:, n, :]).then_inc(sem["inverse"], 1)
                assert do.n == V_STEPS
                for n in range(2):
                    v.wait_ge(sem["rooted"], 2 * h + n + 1)
                    v.scalar_tensor_tensor(qk_T[:, n, :], ps[:, BQ + n, :], gains[:, n:n + 1], root[:, n, :],
                                           ALU.mult, ALU.mult).then_inc(sem["qk_ready"], 1)

            def head(h, last):
                for b in range(NB):
                    v.wait_ge(sem["soft_in"], NB * h + b + 1)
                    v.scalar_tensor_tensor(softplus[:, b, b * P:], ps[:, BZ + b, b * P:], 0.0,
                                           log1p[:, b, b * P:], ALU.max, ALU.add).then_inc(sem["soft"], 1)
                v.wait_ge(sem["out_summed"], h + 1)
                signal(v, v.tensor_scalar(root[:, 0, :], ps[:, BN, :], 1.0 / HD, RMS_EPS, ALU.mult, ALU.add),
                       sem["out_mean"], h + 1)
                v.reciprocal(root[:, 0, :], root[:, 0, :]).then_inc(sem["out_inverse"], 1)
                v.wait_ge(sem["out_rooted"], h + 1)
                v.scalar_tensor_tensor(mixed_T[:, ds(h, 1), :].rearrange("p o s -> p (o s)"), out_raw[:],
                                       gains[:, 2:3], root[:, 0, :], ALU.mult, ALU.mult).then_inc(sem["mixed"], 1)
                if not last:
                    normalise(h + 1)

            v.wait_ge(sem["gain_in"], 48)
            signal(v, v.tensor_scalar(gains[:, 0:1], gains[:, 0:1], 1.0 / math.sqrt(HD), None, ALU.mult),
                   sem["gain_scaled"], 1)
            normalise(0)
            with v.Fori(0, heads - 1) as h:
                head(h, False)
            head(heads - 1, True)

        @block.gpsimd
        def _(pool):
            def head(h):
                for source, tile, done in (("soft", softplus, "masked"), ("weighted", weight, "weight_ready")):
                    for b in range(NB):
                        wait_apart(pool, sem[source], NB * h + b + 1)
                        own = tile[:, b, b * P:(b + 1) * P]
                        pool.affine_select(own, own, [[1, P]], ALU.is_gt, 0.0, base=0,
                                           channel_multiplier=-1).then_inc(sem[done], 1)
            with pool.Fori(0, heads) as h:
                head(h)


def time_mix(nc, C, norm_T, w_u, mu, w0, w2, a0, a2, g2, k_k, k_a, r_k, ln_g, ln_b, mixed_T, first_out, width):
    KT, S = norm_T.shape[1], norm_T.shape[2]
    PAIRS, NT, NC = width // P, S // P, S // CHUNK
    LW = w2.shape[0]
    GA = P
    GB = g2.shape[0] - P
    N_PAR = 10
    MU_R, MU_K, MU_V, W0, A0, KK, KA, RK, LG, LB = range(N_PAR)
    with Stage(nc, "mix") as st:
        w_rkv = st.sb("w_rkv", [P, 3, KT, P])
        w2_s = st.sb("w2", [P, P])
        g2_s = st.sb("g2", [P, 2, P])
        params = st.sb("params", [P, N_PAR, PAIRS])
        par = st.sb("par", [P, N_PAR])
        lora_mu = st.sb("lora_mu", [P, 3])
        raw = st.sb("raw", [P, 3, S + 1])
        step = st.sb("step", [P, 3, S])
        lora = st.sb("lora", [P, 3, S])
        rkv = st.sb("rkv", [P, 3, S])
        a_t, logw, kk, kmix, cum, e_in, e_out, t1, t2 = (st.sb(n, [P, S]) for n in (
            "a", "logw", "kk", "kmix", "cum", "e_in", "e_out", "t1", "t2"))
        ar = st.sb("ar", [P, NT, 2, P])
        b_in, k_in = st.sb("b_in", [P, S]), st.sb("k_in", [P, S])
        b_end, k_end = st.sb("b_end", [P, S]), st.sb("k_end", [P, S])
        d_end = st.sb("d_end", [P, NC])
        rows = st.sb("rows", [P, 3, NT, P])
        from_b = st.sb("from_b", [P, 2, NT, 2, P])
        from_k = st.sb("from_k", [P, 2, NT, 2, P])
        inv = st.sb("inv", [P, 2, NT, P])
        inv_T = st.sb("inv_T", [P, 2, NT, P])
        join = st.sb("join", [P, 2, NT, P])
        joined = st.sb("joined", [P, 2, NT, P])
        lv = st.sb("lv", [P, NT, P])
        x_rows = st.sb("x_rows", [P, P])
        u_rows = st.sb("u_rows", [P, NT, P])
        state = st.sb("state", [P, NC + 1, P])
        ps = st.psum()
        names = ("par_in", "lora_w_in", "rkv_w_in", "small_w_in", "lora_mu_in", "zeroed", "lora_product", "lora_raw",
                 "lora_step", "lora_ready", "free", "product", "raw_ready", "par_ready", "lora_wa",
                 "wa_ready", "kk_ready", "kk_square", "kk_sum", "kk_inverse", "kk_root", "decays", "exps", "factors",
                 "turned", "rows_kept", "gram", "gram_kept", "first_gram", "first_kept", "inv_start", "join_ready",
                 "join_product", "joined_kept", "level", "level_kept", "lv_product", "lv_kept", "x_product", "x_kept",
                 "u_product", "u_kept", "s_product", "s_kept", "y_product", "y_kept", "mean", "centred", "y_square",
                 "var", "var_inverse", "var_root", "bonus_in", "bonus_sum", "gate", "v_steps", "end_steps",
                 "inv_kept", "s_half", "pool_steps")
        sem = {n: st.sem(n) for n in names}
        block = st.block()
        src = w_u.rearrange("(k p) n -> p k n", p=P)
        half = lambda c: slice((c % 2) * CHUNK, (c % 2) * CHUNK + CHUNK)

        @block.sync
        def _(sp):
            lo = 3 * width
            sp.dma_start(w_rkv[:, 0, :, :], src[:, :, lo:lo + P]).then_inc(sem["lora_w_in"], 16)
            sp.dma_start(w_rkv[:, 1, :, :], src[:, :, lo + P:lo + 2 * P]).then_inc(sem["lora_w_in"], 16)
            sp.dma_start(w_rkv[:, 2, :, 0:GB], src[:, :, lo + 2 * P:lo + 2 * P + GB]).then_inc(sem["lora_w_in"], 16)
            with nc.allow_non_contiguous_dma("a parameter per partition"):
                for n in range(2):
                    sp.dma_start(lora_mu[:, n:n + 1], mu[lo + n * P:lo + (n + 1) * P].rearrange("(p o) -> p o", o=1)
                                 ).then_inc(sem["lora_mu_in"], 16)
                sp.dma_start(lora_mu[0:GB, 2:3], mu[lo + 2 * P:lo + 2 * P + GB].rearrange("(p o) -> p o", o=1)
                             ).then_inc(sem["lora_mu_in"], 16)
                for n, a in enumerate((mu[0:width], mu[width:2 * width], mu[2 * width:3 * width], w0, a0, k_k, k_a,
                                       r_k, ln_g, ln_b)):
                    sp.dma_start(params[:, n, :], a.rearrange("(g p) -> p g", p=P)).then_inc(sem["par_in"], 16)

            def load(g, first):
                if first:
                    sp.wait_ge(sem["lora_product"], 3)
                else:
                    sp.wait_ge(sem["product"], 3 * g)
                for n in range(3):
                    sp.dma_start(w_rkv[:, n, :, :], src[:, :, ds(g * P + n * width, P)]).then_inc(sem["rkv_w_in"], 16)
                if not first:
                    wait_apart(sp, sem["gate"], g)
                sp.dma_start(w2_s[0:LW, :], w2[:, ds(g * P, P)]).then_inc(sem["small_w_in"], 16)
                sp.dma_start(w2_s[LW:2 * LW, :], a2[:, ds(g * P, P)]).then_inc(sem["small_w_in"], 16)
                sp.dma_start(g2_s[:, 0, :], g2[0:GA, ds(g * P, P)]).then_inc(sem["small_w_in"], 16)
                sp.dma_start(g2_s[0:GB, 1, :], g2[GA:GA + GB, ds(g * P, P)]).then_inc(sem["small_w_in"], 16)
            load(0, True)
            with sp.Fori(1, PAIRS) as g:
                load(g, False)

        @block.tensor
        def _(pe):
            pe.wait_ge(sem["lora_w_in"], 48)
            for n, m in ((0, P), (1, P), (2, GB)):
                for k in range(KT):
                    ins = pe.matmul(ps[0:m, n, :], w_rkv[:, n, k, 0:m], norm_T[:, k, :], start=(k == 0),
                                    stop=(k == KT - 1))
                ins.then_inc(sem["lora_product"], 1)
            pe.wait_ge(sem["lora_ready"], 3)

            def pair(g):
                pe.wait_ge(sem["free"], g + 1)
                pe.wait_ge(sem["rkv_w_in"], (g + 1) * 48)
                for n in range(3):
                    for k in range(KT):
                        ins = pe.matmul(ps[:, n, :], w_rkv[:, n, k, :], norm_T[:, k, :], start=(k == 0),
                                        stop=(k == KT - 1))
                    ins.then_inc(sem["product"], 1)
                pe.wait_ge(sem["small_w_in"], (g + 1) * 64)
                pe.matmul(ps[:, 3, :], w2_s[0:LW, :], lora[0:LW, 0, :], start=True, stop=True
                          ).then_inc(sem["lora_wa"], 1)
                pe.matmul(ps[:, 4, :], w2_s[LW:2 * LW, :], lora[LW:2 * LW, 0, :], start=True, stop=True
                          ).then_inc(sem["lora_wa"], 1)
                pe.wait_ge(sem["kk_square"], g + 1)
                pe.matmul(ps[:, 5, :], C["head_sum"][:], t2[:], start=True, stop=True).then_inc(sem["kk_sum"], 1)
                pe.wait_ge(sem["factors"], g + 1)
                for n, source in enumerate((rkv[:, 2, :], b_end[:], k_end[:])):
                    for t in range(NT):
                        ins = pe.transpose(ps[:, n, t * P:(t + 1) * P], source[:, t * P:(t + 1) * P], C["ident"][:])
                    ins.then_inc(sem["turned"], 1)
                for h in range(2):
                    f = slice(64 * h, 64 * h + 64)
                    if h:
                        pe.wait_ge(sem["gram_kept"], 8 * g + 4)
                        pe.wait_ge(sem["first_kept"], 2 * g + 1)
                    for t in range(NT):
                        cols = slice(t * P, (t + 1) * P)
                        for n, source in enumerate((b_in, k_in)):
                            ins = pe.matmul(ps[:, 3 + 2 * n + t // 2, (t % 2) * 2 * P:(t % 2 + 1) * 2 * P],
                                            source[f, cols], ar[f, t, :, :].rearrange("p a t -> p (a t)"),
                                            start=True, stop=True)
                            if t % 2:
                                ins.then_inc(sem["gram"], 1)
                        ins = pe.matmul(ps[:, 7, cols], ar[f, t, 0, :], b_in[f, cols], start=True, stop=True)
                    ins.then_inc(sem["first_gram"], 1)
                pe.wait_ge(sem["gram_kept"], 8 * g + 8)
                pe.wait_ge(sem["rows_kept"], 3 * g + 3)
                pe.wait_ge(sem["inv_start"], 2 * g + 2)
                for n in range(5):
                    for h in range(2):
                        b0 = 3 - 3 * h
                        pe.wait_ge(sem["join_ready"], 10 * g + 2 * n + h + 1)
                        if n:
                            pe.wait_ge(sem["level_kept"], 10 * g + 2 * (n - 1) + h + 1)
                        for t in range(NT):
                            ins = pe.matmul(ps[:, b0, t * P:(t + 1) * P], join[:, h, t, :], inv[:, h, t, :],
                                            start=True, stop=True)
                        ins.then_inc(sem["join_product"], 1)
                    for h in range(2):
                        b0 = 3 - 3 * h
                        pe.wait_ge(sem["joined_kept"], 10 * g + 2 * n + h + 1)
                        for t in range(NT):
                            cols = slice(t * P, (t + 1) * P)
                            if n < 4:
                                pe.matmul(ps[:, b0 + 1, cols], inv_T[:, h, t, :], joined[:, h, t, :], start=True,
                                          stop=True)
                            ins = pe.matmul(ps[:, b0 + 2, cols], joined[:, h, t, :], inv_T[:, h, t, :], start=True,
                                            stop=True)
                        ins.then_inc(sem["level"], 1)
                pe.wait_ge(sem["level_kept"], 10 * g + 10)
                for t in range(NT):
                    for h in range(2):
                        v_cols = slice(64 * h, 64 * h + 64)
                        ins = pe.matmul(ps[:, 3, t * P + 64 * h:t * P + 64 * h + 64], from_k[:, h, t, 0, :],
                                        rows[:, 0, t, v_cols], start=True, stop=True)
                ins.then_inc(sem["lv_product"], 1)
                for c in range(NC):
                    t, rr = c // 2, half(c)
                    if c:
                        pe.wait_ge(sem["s_kept"], (NC - 1) * g + c)
                    pe.matmul(ps[rr, 4, 0:P], ar[:, t, 0, rr], state[:, c, :], start=True, stop=True
                              ).then_inc(sem["x_product"], 1)
                    pe.matmul(ps[:, 7, c * CHUNK:(c + 1) * CHUNK], state[:, c, :], ar[:, t, 1, rr], start=(c == 0),
                              stop=False, skip_group_check=True)
                    pe.wait_ge(sem["x_kept"], NC * g + c + 1)
                    for h in range(2):
                        v_cols = slice(64 * h, 64 * h + 64)
                        ins = pe.matmul(ps[rr, 5, v_cols], inv_T[:, h, t, rr], x_rows[:, v_cols], start=True, stop=True)
                    ins.then_inc(sem["u_product"], 1)
                    pe.wait_ge(sem["u_kept"], NC * g + c + 1)
                    if c < NC - 1:
                        pe.matmul(ps[:, 6, 0:P], rows[rr, 1, t, :], u_rows[rr, t, :], start=True, stop=False)
                        pe.matmul(ps[:, 6, 0:P], rows[rr, 2, t, :], rows[rr, 0, t, :], start=False, stop=True
                                  ).then_inc(sem["s_product"], 1)
                    if c % 2:
                        for h in range(2):
                            f = slice(64 * h, 64 * h + 64)
                            pe.matmul(ps[f, 7, t * P:(t + 1) * P], u_rows[:, t, f], from_b[:, h, t, 1, :],
                                      start=False, stop=False, skip_group_check=True)
                            ins = pe.matmul(ps[f, 7, t * P:(t + 1) * P], rows[:, 0, t, f], from_k[:, h, t, 1, :],
                                            start=False, stop=(c == NC - 1), skip_group_check=True)
                ins.then_inc(sem["y_product"], 1)
                pe.matmul(ps[:, 5, :], g2_s[:, 0, :], lora[:, 1, :], start=True, stop=False)
                pe.matmul(ps[:, 5, :], g2_s[0:GB, 1, :], lora[0:GB, 2, :], start=False, stop=True
                          ).then_inc(sem["gate"], 1)
                pe.wait_ge(sem["bonus_in"], g + 1)
                pe.matmul(ps[:, 2, :], C["head_sum"][:], b_in[:], start=True, stop=True).then_inc(sem["bonus_sum"], 1)
                pe.wait_ge(sem["y_kept"], g + 1)
                pe.matmul(ps[:, 0, :], C["head_mean"][:], e_out[:], start=True, stop=True).then_inc(sem["mean"], 1)
                pe.wait_ge(sem["y_square"], g + 1)
                pe.matmul(ps[:, 1, :], C["head_mean"][:], t2[:], start=True, stop=True).then_inc(sem["var"], 1)

            with pe.Fori(0, PAIRS) as g:
                pair(g)

        @block.scalar
        def _(act):
            act.wait_ge(sem["zeroed"], 1)
            for n, m in ((0, P), (1, P), (2, GB)):
                act.wait_ge(sem["lora_product"], n + 1)
                act.activation(raw[0:m, n, 1:], ps[0:m, n, :], ACT.Copy).then_inc(sem["lora_raw"], 1)
            for n, m, f in ((0, LW, ACT.Tanh), (1, P, ACT.Sigmoid), (2, GB, ACT.Sigmoid)):
                act.wait_ge(sem["lora_step"], n + 1)
                act.activation(lora[0:m, n, :], lora[0:m, n, :], f).then_inc(sem["lora_ready"], 1)

            def pair(g):
                for n in range(3):
                    act.wait_ge(sem["product"], 3 * g + n + 1)
                    act.activation(raw[:, n, 1:], ps[:, n, :], ACT.Copy).then_inc(sem["raw_ready"], 1)
                act.wait_ge(sem["par_ready"], g + 1)
                for n, (out, bias) in enumerate(((logw, W0), (a_t, A0))):
                    act.wait_ge(sem["lora_wa"], 2 * g + n + 1)
                    act.activation(out[:], ps[:, 3 + n, :], ACT.Sigmoid, bias=par[:, bias:bias + 1]
                                   ).then_inc(sem["wa_ready"], 1)
                act.wait_ge(sem["kk_ready"], g + 1)
                act.activation(t2[:], kk[:], ACT.Square).then_inc(sem["kk_square"], 1)
                act.wait_ge(sem["kk_inverse"], g + 1)
                act.activation(t1[:], t1[:], ACT.Sqrt).then_inc(sem["kk_root"], 1)
                act.wait_ge(sem["decays"], g + 1)
                act.activation(e_in[:], e_in[:], ACT.Exp).then_inc(sem["exps"], 1)
                signal(act, act.activation(e_out[:], cum[:], ACT.Exp, scale=-1.0), sem["exps"], 3 * g + 2)
                act.activation(cum[:], cum[:], ACT.Exp).then_inc(sem["exps"], 1)
                for n in range(3):
                    act.wait_ge(sem["turned"], 3 * g + n + 1)
                    act.activation(rows[:, n, :, :].rearrange("p t f -> p (t f)"), ps[:, n, :], ACT.Copy
                                   ).then_inc(sem["rows_kept"], 1)
                for n in range(5):
                    for h in range(2):
                        act.wait_ge(sem["join_product"], 10 * g + 2 * n + h + 1)
                        act.activation(joined[:, h, :, :].rearrange("p t f -> p (t f)"), ps[:, 3 - 3 * h, :], ACT.Copy
                                       ).then_inc(sem["joined_kept"], 1)
                act.wait_ge(sem["lv_product"], g + 1)
                act.activation(lv[:].rearrange("p t f -> p (t f)"), ps[:, 3, :], ACT.Copy).then_inc(sem["lv_kept"], 1)
                for c in range(NC):
                    act.wait_ge(sem["u_product"], NC * g + c + 1)
                    act.activation(u_rows[half(c), c // 2, :], ps[half(c), 5, 0:P], ACT.Copy).then_inc(sem["u_kept"], 1)
                act.wait_ge(sem["y_product"], g + 1)
                act.activation(e_out[:], ps[:, 7, :], ACT.Copy).then_inc(sem["y_kept"], 1)
                act.wait_ge(sem["centred"], g + 1)
                act.activation(t2[:], e_in[:], ACT.Square).then_inc(sem["y_square"], 1)
                act.wait_ge(sem["var_inverse"], g + 1)
                act.activation(t1[:], t1[:], ACT.Sqrt).then_inc(sem["var_root"], 1)

            with act.Fori(0, PAIRS) as g:
                pair(g)

        @block.vector
        def _(v):
            do = Chain(v, sem["v_steps"])
            do.go(v.memset(raw[:, :, 0:1], 0.0))
            do.go(v.memset(state[:], 0.0))
            do(v.memset(x_rows[:], 0.0))
            v.nop().then_inc(sem["zeroed"], 1)
            v.wait_ge(sem["lora_mu_in"], 48)
            v.wait_ge(sem["par_in"], 160)
            for n, m in ((0, P), (1, P), (2, GB)):
                v.wait_ge(sem["lora_raw"], n + 1)
                do(v.tensor_tensor(step[0:m, n, :], raw[0:m, n, 0:S], raw[0:m, n, 1:], ALU.subtract))
                v.scalar_tensor_tensor(lora[0:m, n, :], step[0:m, n, :], lora_mu[0:m, n:n + 1], raw[0:m, n, 1:],
                                       ALU.mult, ALU.add).then_inc(sem["lora_step"], 1)
            v.wait_ge(sem["lora_step"], 3)
            v.nop().then_inc(sem["free"], 1)
            before, V_STEPS = do.n, 19

            def pair(g):
                do = Chain(v, sem["v_steps"], before + g * V_STEPS)
                signal(v, v.tensor_copy(par[:], params[:, :, ds(g, 1)].rearrange("p n o -> p (n o)")),
                       sem["par_ready"], g + 1)
                for n in range(3):
                    v.wait_ge(sem["raw_ready"], 3 * g + n + 1)
                    do(v.tensor_tensor(step[:, n, :], raw[:, n, 0:S], raw[:, n, 1:], ALU.subtract))
                    do(v.scalar_tensor_tensor(rkv[:, n, :], step[:, n, :], par[:, MU_R + n:MU_R + n + 1],
                                              raw[:, n, 1:], ALU.mult, ALU.add))
                r, k, val = (rkv[:, n, :] for n in range(3))
                signal(v, v.tensor_scalar(kk[:], k, par[:, KK:KK + 1], None, ALU.mult), sem["kk_ready"], g + 1)
                v.wait_ge(sem["wa_ready"], 2 * g + 2)
                do(v.tensor_scalar(logw[:], logw[:], -math.exp(-0.5), None, ALU.mult))
                do(v.tensor_tensor_scan(cum[:], C["no_carry"][:], logw[:], 0.0, ALU.mult, ALU.add))
                signal(v, v.tensor_tensor(e_in[:], cum[:], logw[:], ALU.subtract), sem["decays"], g + 1)
                do(v.tensor_scalar(kmix[:], a_t[:], 1.0, par[:, KA:KA + 1], ALU.subtract, ALU.mult))
                do(v.scalar_tensor_tensor(kmix[:], kmix[:], 1.0, k, ALU.add, ALU.mult))
                v.wait_ge(sem["kk_sum"], g + 1)
                do(v.tensor_scalar(t1[:], ps[:, 5, :], 1e-12, None, ALU.add))
                v.reciprocal(t1[:], t1[:]).then_inc(sem["kk_inverse"], 1)
                v.wait_ge(sem["kk_root"], g + 1)
                do(v.tensor_tensor(kk[:], kk[:], t1[:], ALU.mult))
                do(v.tensor_tensor(t2[:], kk[:], a_t[:], ALU.mult))
                v.wait_ge(sem["exps"], 3 * g + 3)
                tiles = lambda x: x[:].rearrange("p (t s) -> p t s", s=P)
                chunks = lambda x: x[:].rearrange("p (c s) -> p c s", s=CHUNK)
                do.go(v.scalar_tensor_tensor(ar[:, :, 0, :], tiles(kk), -1.0, tiles(e_in), ALU.mult, ALU.mult))
                do.go(v.tensor_tensor(ar[:, :, 1, :], r.rearrange("p (t s) -> p t s", s=P), tiles(cum), ALU.mult))
                do.go(v.tensor_tensor(b_in[:], t2[:], e_out[:], ALU.mult))
                do.go(v.tensor_tensor(k_in[:], kmix[:], e_out[:], ALU.mult))
                do(v.tensor_copy(d_end[:], chunks(cum)[:, :, CHUNK - 1]))
                end = d_end[:].unsqueeze(2).to_broadcast([P, NC, CHUNK])
                do.go(v.tensor_tensor(chunks(b_end), chunks(b_in), end, ALU.mult))
                v.tensor_tensor(chunks(k_end), chunks(k_in), end, ALU.mult).then_inc(sem["factors"], 1)
                assert do.n == V_STEPS, do.n
                for h in range(2):
                    for i, (bank, kept, t0) in enumerate(((3, from_b, 0), (5, from_k, 0), (4, from_b, 2),
                                                          (6, from_k, 2))):
                        v.wait_ge(sem["gram"], 8 * g + 4 * h + i + 1)
                        v.tensor_tensor(kept[:, h, t0:t0 + 2, :, :].rearrange("p t a s -> p t (a s)"),
                                        ps[:, bank, :].rearrange("p (t s) -> p t s", t=2),
                                        C["seen"][:].rearrange("p a s -> p (a s)").unsqueeze(1
                                                               ).to_broadcast([P, 2, 2 * P]),
                                        ALU.mult).then_inc(sem["gram_kept"], 1)
                    v.wait_ge(sem["first_gram"], 2 * g + h + 1)
                    signal(v, v.tensor_tensor(inv[:, h, :, :], ps[:, 7, :].rearrange("p (t s) -> p t s", s=P),
                                              C["first_down"][:].unsqueeze(1).to_broadcast([P, NT, P]), ALU.mult),
                           sem["first_kept"], 2 * g + h + 1)
                    v.tensor_tensor(inv[:, h, :, :], inv[:, h, :, :],
                                    C["ident"][:].unsqueeze(1).to_broadcast([P, NT, P]),
                                    ALU.add).then_inc(sem["inv_start"], 1)
                v.scalar_tensor_tensor(b_in[:], r, par[:, RK:RK + 1], kmix[:], ALU.mult, ALU.mult
                                       ).then_inc(sem["bonus_in"], 1)
                for n in range(5):
                    for h in range(2):
                        flat = lambda x: x[:, h, :, :].rearrange("p t s -> p (t s)")
                        v.wait_ge(sem["level"], 10 * g + 2 * n + h + 1)
                        if n < 4:
                            v.tensor_tensor(flat(inv), flat(inv), ps[:, 4 - 3 * h, :], ALU.add
                                            ).then_inc(sem["inv_kept"], 1)
                        v.tensor_tensor(flat(inv_T), flat(inv_T), ps[:, 5 - 3 * h, :], ALU.add
                                        ).then_inc(sem["level_kept"], 1)
                v.wait_ge(sem["lv_kept"], g + 1)
                for c in range(NC):
                    rr = half(c)
                    v.wait_ge(sem["x_product"], NC * g + c + 1)
                    v.tensor_tensor(x_rows[rr, :], ps[rr, 4, 0:P], lv[rr, c // 2, :], ALU.add
                                    ).then_inc(sem["x_kept"], 1)
                    if c < NC - 1:
                        v.wait_ge(sem["s_product"], (NC - 1) * g + c + 1)
                        for h in range(2):
                            f = slice(64 * h, 64 * h + 64)
                            ins = v.scalar_tensor_tensor(state[f, c + 1, f], state[f, c, f], d_end[f, c:c + 1],
                                                         ps[f, 6, f], ALU.mult, ALU.add)
                            ins.then_inc(sem["s_half" if h == 0 else "s_kept"], 1)
                do = Chain(v, sem["end_steps"], 5 * g)
                v.wait_ge(sem["y_kept"], g + 1)
                v.wait_ge(sem["mean"], g + 1)
                signal(v, v.tensor_tensor(e_in[:], e_out[:], ps[:, 0, :], ALU.subtract), sem["centred"], g + 1)
                v.wait_ge(sem["bonus_sum"], g + 1)
                do(v.tensor_tensor(k_in[:], val, ps[:, 2, :], ALU.mult))
                v.wait_ge(sem["var"], g + 1)
                do(v.tensor_scalar(t1[:], ps[:, 1, :], GN_EPS, None, ALU.add))
                signal(v, v.reciprocal(t1[:], t1[:]), sem["var_inverse"], g + 1)
                v.wait_ge(sem["var_root"], g + 1)
                do(v.tensor_tensor(e_in[:], e_in[:], t1[:], ALU.mult))
                do(v.tensor_scalar(e_in[:], e_in[:], par[:, LG:LG + 1], par[:, LB:LB + 1], ALU.mult, ALU.add))
                do(v.tensor_tensor(e_in[:], e_in[:], k_in[:], ALU.add))
                assert do.n == 5
                v.wait_ge(sem["gate"], g + 1)
                signal(v, v.tensor_tensor(mixed_T[:, ds(first_out + g, 1), :].rearrange("p o s -> p (o s)"), e_in[:],
                                          ps[:, 5, :], ALU.mult), sem["free"], g + 2)

            with v.Fori(0, PAIRS) as g:
                pair(g)

        @block.gpsimd
        def _(pool):
            def pair(g):
                bc = lambda m: m.unsqueeze(1).to_broadcast([P, NT, P])
                do = Chain(pool, sem["pool_steps"], 4 * g)
                for h in range(2):
                    pool.wait_ge(sem["gram_kept"], 8 * g + 4 * h + 4)
                    do(pool.tensor_tensor(inv_T[:, h, :, :], from_b[:, h, :, 0, :], bc(C["first_up"][:]), ALU.mult))
                    do(pool.tensor_tensor(inv_T[:, h, :, :], inv_T[:, h, :, :], bc(C["ident"][:]), ALU.add))
                for n in range(5):
                    for h in range(2):
                        if n:
                            pool.wait_ge(sem["join_product"], 10 * g + 2 * (n - 1) + h + 1)
                        pool.tensor_tensor(join[:, h, :, :], from_b[:, h, :, 0, :], bc(C["levels"][:, n, :]),
                                           ALU.mult).then_inc(sem["join_ready"], 1)
            with pool.Fori(0, PAIRS) as g:
                pair(g)


def output_projection(nc, mixed_T, w_out, x, x_rows):
    def setup(st):
        return {"x_in": [st.sem(f"x_in{t}") for t in range(4)]}

    def sync(sp, extra):
        for t in range(4):
            sp.dma_start(x_rows[:, t, :], x[t * P:(t + 1) * P, :]).then_inc(extra["x_in"][t], 16)

    def vector(v, half, b, ps, extra, done):
        t, cols = b // 2, slice(half * 1024 + (b % 2) * BANK, half * 1024 + (b % 2 + 1) * BANK)
        v.wait_ge(extra["x_in"][t], 16)
        v.tensor_tensor(x_rows[:, t, cols], x_rows[:, t, cols], ps[:, b, :], ALU.add).then_inc(done, 1)

    project_rows(nc, "out", mixed_T, w_out, x_rows.shape[2] // 1024, vector, setup=setup, sync=sync)


def route(nc, C, hn_T, router_g, router_g_b, router_e, router_e_b, R, token_table, items_dram):
    KT = hn_T.shape[1]
    G, E = router_g.shape[1], router_e.shape[1]
    EG, NT = E // G, 4
    NB = hn_T.shape[2] // SLOTS - 1
    NL = G + E
    with Stage(nc, "route") as st:
        w = st.sb("w", [P, KT, NL])
        bias = st.sb("bias", [NL, 1])
        logits_T = st.sb("logits_T", [NL, 512])
        lg = st.sb("logits", [P, NT, NL])
        group_at, expert_at = st.sb("group_at", [P, G]), st.sb("expert_at", [P, EG])
        first_at = st.sb("first_at", [P, NB + 1, E])
        later_at = st.sb("later_at", [P, NB, E])
        expert_no = st.sb("expert_no", [P, NB, E])
        edges = st.sb("edges", [P, NB + 2])
        block_min = st.sb("block_min", [P, NB, E])
        own_index = st.sb("own_index", [P, 1])
        token_id = st.sb("token_id", [P, NT, 16], I32)
        g4, g4b = st.sb("g4", [P, NT, G]), st.sb("g4b", [P, NT, G])
        pick = st.sb("pick", [P, NT, G, EG])
        e8, e8b, cand = (st.sb(n, [P, NT, EG]) for n in ("e8", "e8b", "cand"))
        chosen = st.sb("chosen", [P, 2, NT, EG])
        hot = st.sb("hot", [P, 2, NT, G, EG])
        both = st.sb("both", [P, NT, E])
        rank = st.sb("rank", [P, NT, E])
        picked = st.sb("picked", [P, NT, NB + 1, E])
        own_rank = st.sb("own_rank", [P, NT, 1])
        reached = st.sb("reached", [P, NT, NB + 2])
        candidate = st.sb("candidate", [P, NT, NB + 1])
        c1, c2, c3, c4, c5 = (st.sb(n, [P, NT, 1]) for n in ("c1", "c2", "c3", "c4", "c5"))
        slot_f = st.sb("slot_f", [P, 2, NT])
        count = st.sb("count", [P, E])
        over = st.sb("over", [P, NB * E])
        order = st.sb("order", [P, NB * E])
        ones_row = st.sb("ones_row", [P, NB * E])
        item = st.sb("item", [P, 1])
        ps = st.psum()
        sem = {n: st.sem(n) for n in ("w_in", "iota", "logits", "biased", "turned", "v_steps", "difference",
                                      "exp_g", "top", "exp_e", "both_ready", "ranked", "slots_ready", "scattered",
                                      "item_ready", "item_turned", "pool_steps", "items_ready")}
        block = st.block()

        @block.sync
        def _(sp):
            with nc.allow_non_contiguous_dma("router weights"):
                sp.dma_start(w[:, :, 0:G], router_g.rearrange("(k p) n -> p k n", p=P)).then_inc(sem["w_in"], 16)
                sp.dma_start(w[:, :, G:NL], router_e.rearrange("(k p) n -> p k n", p=P)).then_inc(sem["w_in"], 16)
                sp.dma_start(bias[0:G, :], router_g_b.rearrange("(p o) -> p o", o=1)).then_inc(sem["w_in"], 16)
                sp.dma_start(bias[G:NL, :], router_e_b.rearrange("(p o) -> p o", o=1)).then_inc(sem["w_in"], 16)

        @block.tensor
        def _(pe):
            pe.wait_ge(sem["w_in"], 64)
            for k in range(KT):
                ins = pe.matmul(ps[0:NL, 0, :], w[:, k, :], hn_T[:, k, :], start=(k == 0), stop=(k == KT - 1))
            ins.then_inc(sem["logits"], 1)
            pe.wait_ge(sem["biased"], 1)
            for t in range(NT):
                ins = pe.transpose(ps[:, 1, t * NL:(t + 1) * NL], logits_T[:, t * P:(t + 1) * P],
                                   C["ident"][0:NL, 0:NL])
            ins.then_inc(sem["turned"], 1)
            pe.wait_ge(sem["both_ready"], 1)
            for t in range(NT + 1):
                for j in range(min(t, NT - 1) + 1):
                    ins = pe.matmul(ps[:, 2, t * E:(t + 1) * E], C["after" if j == t else "ones"][:], both[:, j, :],
                                    start=(j == 0), stop=(j == min(t, NT - 1)))
            ins.then_inc(sem["ranked"], 1)
            pe.wait_ge(sem["item_ready"], 1)
            pe.matmul(ps[0:1, 3, 0:P], item[:], C["ident"][:], start=True, stop=True).then_inc(sem["item_turned"], 1)

        @block.scalar
        def _(act):
            act.wait_ge(sem["logits"], 1)
            act.wait_ge(sem["w_in"], 64)
            act.activation(logits_T[:], ps[0:NL, 0, :], ACT.Identity, bias=bias[:]).then_inc(sem["biased"], 1)
            act.wait_ge(sem["difference"], 1)
            act.activation(g4b[:], g4b[:], ACT.Exp).then_inc(sem["exp_g"], 1)
            act.wait_ge(sem["top"], 1)
            act.activation(c4[:], c4[:], ACT.Exp).then_inc(sem["exp_e"], 1)

        @block.gpsimd
        def _(pool):
            do = Chain(pool, sem["pool_steps"])
            kw = dict(allow_small_or_imprecise_dtypes=True)
            do.go(pool.iota(group_at[:], [[1, G]], base=-G, channel_multiplier=0, **kw))
            do.go(pool.iota(expert_at[:], [[1, EG]], base=-EG, channel_multiplier=0, **kw))
            do.go(pool.iota(first_at[:, 0, :], [[SLOTS, E]], base=0, channel_multiplier=0, **kw))
            do.go(pool.iota(later_at[:], [[-SLOTS, NB], [0, E]], base=(E - 1) * SLOTS, channel_multiplier=0, **kw))
            do.go(pool.iota(expert_no[:], [[0, NB], [1, E]], base=0, channel_multiplier=0, **kw))
            do.go(pool.iota(edges[:], [[SLOTS, NB + 2]], base=0, channel_multiplier=0, **kw))
            do.go(pool.iota(block_min[:], [[SLOTS, NB], [0, E]], base=SLOTS, channel_multiplier=0, **kw))
            do.go(pool.iota(own_index[:], [[0, 1]], base=0, channel_multiplier=1, **kw))
            do.go(pool.iota(token_id[:], [[P, NT], [0, 16]], base=0, channel_multiplier=1))
            do(pool.memset(ones_row[:], 1.0))
            pool.nop().then_inc(sem["iota"], 1)
            pool.wait_ge(sem["slots_ready"], 2)
            for n in range(2):
                for t in range(NT):
                    pool.indirect_dma_start(
                        out=token_table, out_offset=bass.IndirectOffsetOnAxis(ap=R["slot"][:, n, t:t + 1], axis=0),
                        in_=token_id[:, t, :], in_offset=None).then_inc(sem["scattered"], 16)
            pool.wait_ge(sem["scattered"], 16 * 2 * NT)

        @block.vector
        def _(v):
            do = Chain(v, sem["v_steps"])
            v.wait_ge(sem["iota"], 1)
            v.wait_ge(sem["turned"], 1)
            wide = lambda x, n: x.to_broadcast([P, NT, n])
            do(v.tensor_copy(lg[:], ps[:, 1, 0:NT * NL].rearrange("p (t n) -> p t n", n=NL)))

            def first_top(values, at, n, best, mark, cand):
                do(v.tensor_reduce(best, values, AX_X, ALU.max))
                do(v.tensor_tensor(mark, values, wide(best, n), ALU.is_equal))
                do(v.tensor_tensor(cand, mark, at[:].unsqueeze(1).to_broadcast([P, NT, n]), ALU.mult))
                do(v.tensor_reduce(c5[:], cand, AX_X, ALU.min))
                do(v.tensor_tensor(mark, at[:].unsqueeze(1).to_broadcast([P, NT, n]), wide(c5[:], n), ALU.is_equal))

            first_top(lg[:, :, 0:G], group_at, G, c1[:], g4[:], g4b[:])
            signal(v, v.tensor_tensor(g4b[:], lg[:, :, 0:G], wide(c1[:], G), ALU.subtract), sem["difference"], 1)
            do(v.tensor_tensor(pick[:], lg[:, :, G:NL].rearrange("p t (g e) -> p t g e", g=G),
                               g4[:].unsqueeze(3).to_broadcast([P, NT, G, EG]), ALU.mult))
            do(v.tensor_tensor(e8[:], pick[:, :, 0, :], pick[:, :, 1, :], ALU.add))
            for g in range(2, G):
                do(v.tensor_tensor(e8[:], e8[:], pick[:, :, g, :], ALU.add))
            first_top(e8[:], expert_at, EG, c2[:], chosen[:, 0, :, :], cand[:])
            do(v.scalar_tensor_tensor(e8b[:], chosen[:, 0, :, :], -1e30, e8[:], ALU.mult, ALU.add))
            first_top(e8b[:], expert_at, EG, c3[:], chosen[:, 1, :, :], cand[:])
            signal(v, v.tensor_tensor(c4[:], c3[:], c2[:], ALU.subtract), sem["top"], 1)
            for n in range(2):
                do(v.tensor_tensor(hot[:, n, :, :, :], g4[:].unsqueeze(3).to_broadcast([P, NT, G, EG]),
                                   chosen[:, n, :, :].unsqueeze(2).to_broadcast([P, NT, G, EG]), ALU.mult))
            flat = lambda n: hot[:, n, :, :, :].rearrange("p t g e -> p t (g e)")
            signal(v, v.tensor_tensor(both[:], flat(0), flat(1), ALU.add), sem["both_ready"], 1)
            v.wait_ge(sem["exp_g"], 1)
            do(v.tensor_reduce(c1[:], g4b[:], AX_X, ALU.add))
            v.wait_ge(sem["exp_e"], 1)
            do(v.tensor_scalar(c2[:], c4[:], 1.0, None, ALU.add))
            do(v.tensor_tensor(c2[:], c2[:], c1[:], ALU.mult))
            do(v.reciprocal(R["weight"][:, 0, :].unsqueeze(2), c2[:]))
            do(v.tensor_tensor(R["weight"][:, 1, :].unsqueeze(2), R["weight"][:, 0, :].unsqueeze(2), c4[:], ALU.mult))
            v.wait_ge(sem["ranked"], 1)
            do(v.tensor_copy(rank[:], ps[:, 2, 0:NT * E].rearrange("p (t e) -> p t e", e=E)))
            do(v.tensor_copy(count[:], ps[:, 2, NT * E:(NT + 1) * E]))
            over3 = over[:].rearrange("p (b e) -> p b e", e=E)
            do(v.tensor_tensor(over3, count[:].unsqueeze(1).to_broadcast([P, NB, E]), block_min[:], ALU.is_gt))
            do(v.tensor_tensor_scan(order[:], ones_row[:], over[:], 0.0, ALU.mult, ALU.add))
            do(v.tensor_copy(R["n_items"][:], order[:, NB * E - 1:NB * E]))
            do(v.scalar_tensor_tensor(first_at[:, 1:, :], order[:].rearrange("p (b e) -> p b e", e=E), float(SLOTS),
                                      later_at[:], ALU.mult, ALU.add))
            for n in range(2):
                do(v.tensor_tensor(picked[:, :, 0, :], rank[:], flat(n), ALU.mult))
                do(v.tensor_reduce(own_rank[:], picked[:, :, 0, :], AX_X, ALU.add))
                do(v.tensor_tensor(reached[:], own_rank[:].to_broadcast([P, NT, NB + 2]),
                                   edges[:].unsqueeze(1).to_broadcast([P, NT, NB + 2]), ALU.is_ge))
                do(v.tensor_tensor(reached[:, :, 0:NB + 1], reached[:, :, 0:NB + 1], reached[:, :, 1:NB + 2],
                                   ALU.subtract))
                do(v.tensor_tensor(picked[:], first_at[:].unsqueeze(1).to_broadcast([P, NT, NB + 1, E]),
                                   flat(n).unsqueeze(2).to_broadcast([P, NT, NB + 1, E]), ALU.mult))
                do(v.tensor_reduce(candidate[:].unsqueeze(3), picked[:], AX_X, ALU.add))
                do(v.tensor_tensor(candidate[:], candidate[:], reached[:, :, 0:NB + 1], ALU.mult))
                do(v.tensor_reduce(slot_f[:, n, :].unsqueeze(2), candidate[:], AX_X, ALU.add))
                do(v.tensor_tensor(slot_f[:, n, :].unsqueeze(2), slot_f[:, n, :].unsqueeze(2), own_rank[:], ALU.add))
                signal(v, v.tensor_copy(R["slot"][:, n, :], slot_f[:, n, :]), sem["slots_ready"], n + 1)
            do(v.tensor_tensor(order[:], order[:], over[:], ALU.mult))
            do(v.tensor_scalar(own_index[:], own_index[:], 1.0, None, ALU.add))
            do(v.tensor_scalar(order[:], order[:], own_index[:, 0:1], None, ALU.is_equal))
            do(v.tensor_tensor(over[:], order[:], expert_no[:].rearrange("p b e -> p (b e)"), ALU.mult))
            signal(v, v.tensor_reduce(item[:], over[:], AX_X, ALU.add), sem["item_ready"], 1)
            v.wait_ge(sem["item_turned"], 1)
            do(v.tensor_copy(R["item_expert"][:], ps[0:1, 3, 0:P]))


def experts(nc, C, gain, w_up, w_down, R, token_table, rows_dram, y_dram):
    E, D, F2 = w_up.shape
    F = F2 // 2
    KT, FT, ITEMS = D // P, F // P, R["max_items"]
    UP, DOWN = KT // 4, FT // 2
    with Stage(nc, "moe") as st:
        w_u = st.sb("w_up", [P, UP, 4, F2])
        w_d = st.sb("w_down", [P, DOWN, 2, D])
        g = st.sb("gain", [P, KT])
        ids = st.sb("ids", [SLOTS, 16], I32)
        x_in = st.sb("x_in", [SLOTS, D])
        x_T = st.sb("x_T", [P, KT, SLOTS])
        sig = st.sb("sig", [P, F // 2])
        hid = st.sb("hid", [P, F // 2])
        hid_T = st.sb("hid_T", [P, 2, 2, SLOTS])
        y = st.sb("y", [P, 2, BANK])
        ps = st.psum()
        up_in = [st.sem(f"up_in{n}") for n in range(UP)]
        down_in = [st.sem(f"down_in{n}") for n in range(DOWN)]
        sem = {n: st.sem(n) for n in ("gain_in", "ids_in", "x_in", "x_turned", "x_scaled", "up_used", "up_done",
                                      "sigmoid", "gated", "hidden", "hid_turned", "hid_kept", "down_used",
                                      "y_kept_v", "y_kept_s", "stored")}
        block = st.block()

        def turns(eng, turn):
            turn(0, 0, 0, True)
            with eng.Fori(1, E) as i:
                turn(i, i, i * SLOTS, False)
            n_items = eng.value_load(R["n_items"][0:1, 0:1], min_val=0, max_val=ITEMS)
            with eng.If(n_items > 0):
                with eng.Fori(0, ITEMS) as i:
                    with eng.If(n_items > i):
                        expert = eng.value_load(R["item_expert"][0:1, ds(i, 1)], min_val=0, max_val=E - 1)
                        turn(i + E, expert, (i + E) * SLOTS, False)
                    eng.nop()
            eng.nop()

        @block.sync
        def _(sp):
            with nc.allow_non_contiguous_dma("a gain per partition"):
                sp.dma_start(g[:], gain.rearrange("(k p) -> p k", p=P)).then_inc(sem["gain_in"], 16)
            up = w_up.rearrange("e (n k p) f -> e p n k f", p=P, k=4)
            down = w_down.rearrange("e (n k p) f -> e p n k f", p=P, k=2)

            def turn(i, expert, row, first):
                for n in range(UP):
                    if not first:
                        sp.wait_ge(sem["up_used"], (i - 1) * UP + n + 1)
                    sp.dma_start(w_u[:, n, :, :], up[ds(expert, 1), :, n, :, :].rearrange("e p k f -> (e p) k f")
                                 ).then_inc(up_in[n], 16)
                for n in range(DOWN):
                    if not first:
                        sp.wait_ge(sem["down_used"], (i - 1) * DOWN + n + 1)
                    sp.dma_start(w_d[:, n, :, :], down[ds(expert, 1), :, n, :, :].rearrange("e p k f -> (e p) k f")
                                 ).then_inc(down_in[n], 16)
            turns(sp, turn)

        @block.gpsimd
        def _(pool):
            def turn(i, expert, row, first):
                if not first:
                    pool.wait_ge(sem["x_turned"], i * 2)
                pool.dma_start(ids[:], token_table[ds(row, SLOTS), :]).then_inc(sem["ids_in"], 16)
                wait_apart(pool, sem["ids_in"], (i + 1) * 16)
                pool.indirect_dma_start(out=x_in[:], out_offset=None, in_=rows_dram,
                                        in_offset=bass.IndirectOffsetOnAxis(ap=ids[:, 0:1], axis=0)
                                        ).then_inc(sem["x_in"], 16)
            turns(pool, turn)

        @block.tensor
        def _(pe):
            def turn(i, expert, row, first):
                wait_apart(pe, sem["x_in"], (i + 1) * 16)
                for b in range(2):
                    for k in range(KT // 2):
                        kk = b * KT // 2 + k
                        ins = pe.transpose(ps[:, b, k * SLOTS:(k + 1) * SLOTS], x_in[:, kk * P:(kk + 1) * P],
                                           C["ident"][0:SLOTS, 0:SLOTS])
                    ins.then_inc(sem["x_turned"], 1)
                for n in range(UP):
                    pe.wait_ge(up_in[n], (i + 1) * 16)
                    for s in range(4):
                        k = 4 * n + s
                        if k % (KT // 2) == 0:
                            pe.wait_ge(sem["x_scaled"], i * 2 + k // (KT // 2) + 1)
                        cols = w_u[:, n, s, :].rearrange("p (a c f) -> p a c f", a=2, c=2)
                        for c in range(2):
                            ins = pe.matmul(ps[64 * c:64 * c + 64, 2, :].rearrange("p (a f) -> p a f", a=2),
                                            x_T[:, k, :], cols[:, :, c, :], start=(k == 0), stop=(k == KT - 1))
                            if c == 0 and k == KT - 1:
                                ins.then_inc(sem["up_done"], 1)
                    ins.then_inc(sem["up_used"], 1)
                pe.wait_ge(sem["hidden"], i + 1)
                for c in range(2):
                    ins = pe.transpose(ps[:, 3, c * P:(c + 1) * P], hid[:, c * P:(c + 1) * P], C["ident"][:])
                ins.then_inc(sem["hid_turned"], 1)
                pe.wait_ge(sem["hid_kept"], i + 1)
                if not first:
                    pe.wait_ge(sem["y_kept_v"], i)
                    pe.wait_ge(sem["y_kept_s"], i)
                for n in range(DOWN):
                    pe.wait_ge(down_in[n], (i + 1) * 16)
                    for s in range(2):
                        f = 2 * n + s
                        for b in range(2):
                            for c in range(2):
                                ins = pe.matmul(ps[64 * c:64 * c + 64, 4 + b, :], hid_T[:, f % 2, f // 2, :],
                                                w_d[:, n, s, (2 * c + b) * BANK:(2 * c + b + 1) * BANK],
                                                start=(f == 0), stop=(f == FT - 1))
                    ins.then_inc(sem["down_used"], 1)
            turns(pe, turn)

        @block.scalar
        def _(act):
            def turn(i, expert, row, first):
                act.wait_ge(sem["up_used"], (i + 1) * UP)
                act.activation(sig[:], ps[:, 2, 0:F // 2], ACT.Sigmoid).then_inc(sem["sigmoid"], 1)
                act.wait_ge(sem["down_used"], (i + 1) * DOWN)
                if not first:
                    act.wait_ge(sem["stored"], i * 32)
                signal(act, act.activation(y[:, 1, :], ps[:, 5, :], ACT.Copy), sem["y_kept_s"], i + 1)
                act.wait_ge(sem["y_kept_v"], i + 1)
                for c in range(2):
                    act.dma_start(y_dram[ds(row, SLOTS), c * 1024:(c + 1) * 1024],
                                  y[64 * c:64 * c + 64, :, :].rearrange("p b n -> p (b n)")
                                  ).then_inc(sem["stored"], 16)
            turns(act, turn)
            n_items = act.value_load(R["n_items"][0:1, 0:1], min_val=0, max_val=ITEMS)
            wait_apart(act, sem["stored"], (n_items + E) * 32)

        @block.vector
        def _(v):
            v.wait_ge(sem["gain_in"], 16)

            def turn(i, expert, row, first):
                for b in range(2):
                    v.wait_ge(sem["x_turned"], i * 2 + b + 1)
                    k = slice(b * KT // 2, (b + 1) * KT // 2)
                    v.tensor_tensor(x_T[:, k, :], ps[:, b, :].rearrange("p (k s) -> p k s", s=SLOTS),
                                    g[:, k].unsqueeze(2).to_broadcast([P, KT // 2, SLOTS]),
                                    ALU.mult).then_inc(sem["x_scaled"], 1)
                v.wait_ge(sem["sigmoid"], i + 1)
                signal(v, v.tensor_tensor(hid[:], sig[:], ps[:, 2, 0:F // 2], ALU.mult), sem["gated"], i + 1)
                v.tensor_tensor(hid[:], hid[:], ps[:, 2, F // 2:F], ALU.mult).then_inc(sem["hidden"], 1)
                v.wait_ge(sem["hid_turned"], i + 1)
                v.tensor_copy(hid_T[:].rearrange("p a c s -> p (a c s)"), ps[:, 3, 0:4 * SLOTS]
                              ).then_inc(sem["hid_kept"], 1)
                v.wait_ge(sem["down_used"], (i + 1) * DOWN)
                if not first:
                    v.wait_ge(sem["stored"], i * 32)
                v.tensor_copy(y[:, 0, :], ps[:, 4, :]).then_inc(sem["y_kept_v"], 1)
            turns(v, turn)


def combine(nc, R, y_dram, x_rows):
    NT, D = x_rows.shape[1], x_rows.shape[2]
    with Stage(nc, "combine") as st:
        y = st.sb("y", [P, 4, D])
        landed = [st.sem(f"landed{n}") for n in range(4)]
        added = st.sem("added")
        block = st.block()

        @block.gpsimd
        def _(pool):
            for i in range(2 * NT):
                t, n = i // 2, i % 2
                if i >= 4:
                    pool.wait_ge(added, i - 3)
                pool.indirect_dma_start(out=y[:, i % 4, :], out_offset=None, in_=y_dram,
                                        in_offset=bass.IndirectOffsetOnAxis(ap=R["slot"][:, n, t:t + 1], axis=0)
                                        ).then_inc(landed[i % 4], 16)

        @block.vector
        def _(v):
            for i in range(2 * NT):
                t, n = i // 2, i % 2
                v.wait_ge(landed[i % 4], 16 * (i // 4 + 1))
                signal(v, v.scalar_tensor_tensor(x_rows[:, t, :], y[:, i % 4, :], R["weight"][:, n, t:t + 1],
                                                 x_rows[:, t, :], ALU.mult, ALU.add), added, i + 1)


def layer_embedding(nc, C, p, ple_proj, ple_gate, ple_norm_g, x_rows, x_T, out):
    NT, D, PD = x_rows.shape[1], x_rows.shape[2], p.shape[1]
    KP = PD // P
    with ExitStack() as keep:
        emb = keep.enter_context(nc.sbuf_tensor("embedding", [P, NT, D], F32))
        p_T = keep.enter_context(nc.sbuf_tensor("p_T", [P, KP, 512], F32))
        with Stage(nc, "p_turn") as st:
            rows = st.sb("rows", [P, NT, PD])
            ps = st.psum()
            landed, turned, kept = st.sem("landed"), st.sem("turned"), st.sem("kept")
            block = st.block()

            @block.sync
            def _(sp):
                sp.dma_start(rows[:], p.rearrange("(t q) n -> q t n", q=P)).then_inc(landed, 16)

            @block.tensor
            def _(pe):
                pe.wait_ge(landed, 16)
                for k in range(KP):
                    for t in range(NT):
                        ins = pe.transpose(ps[:, k, t * P:(t + 1) * P], rows[:, t, k * P:(k + 1) * P], C["ident"][:])
                    ins.then_inc(turned, 1)

            @block.vector
            def _(v):
                for k in range(KP):
                    v.wait_ge(turned, k + 1)
                    v.tensor_copy(p_T[:, k, :], ps[:, k, :]).then_inc(kept, 1)

        cols = lambda half, b: slice(half * 1024 + (b % 2) * BANK, half * 1024 + (b % 2 + 1) * BANK)

        def keep_vector(v, half, b, ps, extra, done):
            v.tensor_copy(emb[:, b // 2, cols(half, b)], ps[:, b, :]).then_inc(done, 1)

        def keep_scalar(act, half, b, ps, extra, done):
            act.activation(emb[:, b // 2, cols(half, b)], ps[:, b, :], ACT.Copy).then_inc(done, 1)

        project_rows(nc, "embed", p_T, ple_proj, D // 1024, keep_vector, keep_scalar)

        def setup(st):
            extra = {n: st.sem(n) for n in ("gate", "gated", "g_in", "squared", "inverse", "rooted", "stored",
                                            "steps")}
            extra["sig"] = st.sb("sig", [P, 2, BANK])
            extra["ss"] = st.sb("ss", [P, 2, NT])
            extra["gain_rows"] = st.sb("gain_rows", [P, D])
            extra["square"] = st.sb("square", [P, D])
            return extra

        def sync(sp, X):
            sp.dma_start(X["gain_rows"][:], ple_norm_g.rearrange("(o n) -> o n", o=1).to_broadcast([P, D])
                         ).then_inc(X["g_in"], 16)

        def vector(v, half, b, ps, X, done):
            i = half * 8 + b
            v.wait_ge(X["gate"], i + 1)
            v.tensor_tensor(emb[:, b // 2, cols(half, b)], emb[:, b // 2, cols(half, b)], X["sig"][:, i % 2, :],
                            ALU.mult).then_inc(done, 1)

        def finish_vector(v, X, taken_v, taken_s):
            v.wait_ge(X["squared"], NT)
            do = Chain(v, X["steps"])
            do(v.tensor_scalar(X["ss"][:, 1, :], X["ss"][:, 0, :], 1.0 / D, RMS_EPS, ALU.mult, ALU.add))
            signal(v, v.reciprocal(X["ss"][:, 1, :], X["ss"][:, 1, :]), X["inverse"], 1)
            v.wait_ge(X["rooted"], 1)
            v.wait_ge(X["g_in"], 16)
            for t in range(NT):
                do(v.scalar_tensor_tensor(emb[:, t, :], emb[:, t, :], X["ss"][:, 1, t:t + 1], X["gain_rows"][:],
                                          ALU.mult, ALU.mult))
                signal(v, v.tensor_tensor(emb[:, t, :], emb[:, t, :], x_rows[:, t, :], ALU.add), X["gated"], t + 1)

        def finish_scalar(act, X, taken_v, taken_s):
            act.wait_ge(taken_v, 16)
            for t in range(NT):
                signal(act, act.activation(X["square"][:], emb[:, t, :], ACT.Square,
                                           accum_out=X["ss"][:, 0, t:t + 1]), X["squared"], t + 1)
            act.wait_ge(X["inverse"], 1)
            act.activation(X["ss"][:, 1, :], X["ss"][:, 1, :], ACT.Sqrt).then_inc(X["rooted"], 1)
            for t in range(NT):
                act.wait_ge(X["gated"], t + 1)
                act.dma_start(out[t * P:(t + 1) * P, :], emb[:, t, :]).then_inc(X["stored"], 16)
            act.wait_ge(X["stored"], 16 * NT)

        def gate_scalar(act, half, b, ps, X, taken_v):
            i = half * 8 + b
            if i >= 2:
                act.wait_ge(taken_v, i - 1)
            act.activation(X["sig"][:, i % 2, :], ps[:, b, :], ACT.Sigmoid).then_inc(X["gate"], 1)

        project_rows(nc, "gate", x_T, ple_gate, D // 1024, vector, setup=setup, sync=sync,
                     finish=(finish_vector, finish_scalar), scalar_first=gate_scalar)


def layer(nc, x, p, ln1_g, w_in, sb_q_g, sb_k_g, sb_out_g, rw_mu, rw_w0, rw_w2, rw_a0, rw_a2, rw_g2, rw_k_k,
          rw_k_a, rw_r_k, rw_ln_g, rw_ln_b, w_out, ln2_g, router_g, router_g_b, router_e, router_e_b, w_up, w_down,
          ple_proj, ple_gate, ple_norm_g, out):
    S, D = x.shape
    KT, NT = D // P, S // P
    SB = D // 2
    E = w_up.shape[0]
    max_items = (2 * S - 1) // SLOTS
    slots = (E + max_items) * SLOTS
    rows_dram = nc.dram_tensor("normed_rows", (S, D), F32, kind="Internal").ap()
    y_dram = nc.dram_tensor("expert_rows", (slots, D), F32, kind="Internal").ap()
    token_table = nc.dram_tensor("token_table", (slots, 16), I32, kind="Internal").ap()
    with ExitStack() as keep:
        C = constants(nc, keep)
        hold = lambda stack, name, shape, dt=F32: stack.enter_context(nc.sbuf_tensor(name, shape, dt))
        clear_tables(nc, token_table, y_dram, E * SLOTS)
        with ExitStack() as mixed_life:
            mixed_T = hold(mixed_life, "mixed_T", [P, KT, S])
            with ExitStack() as norm_life:
                norm_T = hold(norm_life, "norm_T", [P, KT, S])
                with ExitStack() as rows_life:
                    rows = hold(rows_life, "rows", [P, NT, D])
                    norm_transpose(nc, "norm1", C, rows, norm_T, gain=ln1_g, load=x)
                with ExitStack() as v_life:
                    v_rows = hold(v_life, "v_rows", [P, NT, SB])
                    value_projection(nc, norm_T, w_in[:, 2 * SB:3 * SB], v_rows)
                    attention(nc, C, norm_T, w_in, v_rows, sb_q_g, sb_k_g, sb_out_g, mixed_T, SB // P, SB)
                time_mix(nc, C, norm_T, w_in[:, 3 * SB:], rw_mu, rw_w0, rw_w2, rw_a0, rw_a2, rw_g2, rw_k_k, rw_k_a,
                         rw_r_k, rw_ln_g, rw_ln_b, mixed_T, SB // P, D - SB)
            x_rows = keep.enter_context(nc.sbuf_tensor("x_rows", [P, NT, D], F32, side="right"))
            output_projection(nc, mixed_T, w_out, x, x_rows)
        R = {"max_items": max_items,
             "slot": hold(keep, "slot", [P, 2, NT], I32), "weight": hold(keep, "weight", [P, 2, NT]),
             "n_items": hold(keep, "n_items", [P, 1], I32),
             "item_expert": hold(keep, "item_expert", [1, P], I32)}
        with ExitStack() as hn_life:
            hn_T = hold(hn_life, "hn_T", [P, KT, S])
            norm_transpose(nc, "norm2", C, x_rows, hn_T, gain=ln2_g, rows_dram=rows_dram)
            route(nc, C, hn_T, router_g, router_g_b, router_e, router_e_b, R, token_table, None)
        experts(nc, C, ln2_g, w_up, w_down, R, token_table, rows_dram, y_dram)
        combine(nc, R, y_dram, x_rows)
        x_T = hold(keep, "x_T", [P, KT, S])
        norm_transpose(nc, "norm3", C, x_rows, x_T)
        layer_embedding(nc, C, p, ple_proj, ple_gate, ple_norm_g, x_rows, x_T, out)


def clear_tables(nc, token_table, y_dram, further):
    (n, w), D, ZR = token_table.shape, y_dram.shape[1], 2
    n_further = n - further
    Q = n_further // 8
    with Stage(nc, "clear") as st:
        zeros = st.sb("zeros", [P, max(n // 64 * w, ZR * D)], I32)
        zeroed, stored = st.sem("zeroed"), st.sem("stored")
        block = st.block()

        @block.vector
        def _(v):
            v.memset(zeros[:], 0).then_inc(zeroed, 1)

        @block.sync
        def _(sp):
            sp.wait_ge(zeroed, 1)
            sp.dma_start(token_table.rearrange("(q r) w -> q (r w)", q=64), zeros[0:64, 0:n // 64 * w]
                         ).then_inc(stored, 16)
            rows = y_dram[further:n, :].rearrange("(q r) n -> q (r n)", r=8)
            for i in range(8 // ZR):
                sp.dma_start(rows[:, i * ZR * D:(i + 1) * ZR * D], zeros[0:Q, 0:ZR * D].bitcast(F32)
                             ).then_inc(stored, 16)
            sp.wait_ge(stored, 16 * (8 // ZR + 1))


def kernel(**inputs):
    import numpy as np
    import concourse.bacc as bacc
    from concourse.bass_utils import run_bass_kernel_spmd

    names = ["x", "p", "ln1_g", "w_in", "sb_q_g", "sb_k_g", "sb_out_g", "rw_mu", "rw_w0", "rw_w2", "rw_a0", "rw_a2",
             "rw_g2", "rw_k_k", "rw_k_a", "rw_r_k", "rw_ln_g", "rw_ln_b", "w_out", "ln2_g", "router_g", "router_g_b",
             "router_e", "router_e_b", "w_up", "w_down", "ple_proj", "ple_gate", "ple_norm_g"]
    shape = inputs["x"].shape
    nc = bacc.Bacc("TRN2", target_bir_lowering=False, num_devices=1)
    arrays, args = {}, []
    for name in names:
        a = np.ascontiguousarray(inputs[name])[0]
        if name == "p":
            a = a[0]
        if name == "rw_r_k":
            a = a.reshape(-1)
        a = np.ascontiguousarray(a)
        arrays[f"in_{name}"] = a
        args.append(nc.dram_tensor(f"in_{name}", a.shape, mybir.dt.from_np(a.dtype), kind="ExternalInput").ap())
    out = nc.dram_tensor("out", shape[1:], F32, kind="ExternalOutput").ap()
    layer(nc, *args, out)
    r = run_bass_kernel_spmd(nc, [arrays], core_ids=[0])
    return r.results[0]["out"].reshape(shape)
```

```python
from contextlib import ExitStack
import math

import concourse.bass as bass
from concourse import mybir

F32 = mybir.dt.float32
I32 = mybir.dt.int32
ALU = mybir.AluOpType
ACT = mybir.ActivationFunctionType
AX_X = mybir.AxisListType.X
ds = bass.ds

P = 128
RMS_EPS = 1e-6
GN_EPS = 64e-5
CHUNK = 64
SLOTS = 64
BANK = 512


class Stage:

    def __init__(self, nc, tag):
        self.nc, self.tag, self.stack, self.sems = nc, tag, ExitStack(), []

    def __enter__(self):
        self.stack.__enter__()
        return self

    def __exit__(self, *exc):
        self.stack.__exit__(*exc)
        if exc[0] is None:
            self.nc.clear_and_free_semaphores(self.sems)
            self.nc.all_engine_barrier()

    def sb(self, name, shape, dt=F32):
        return self.stack.enter_context(self.nc.sbuf_tensor(f"{self.tag}_{name}", list(shape), dt))

    def psum(self):
        return self.stack.enter_context(self.nc.psum_tensor(f"{self.tag}_ps", [P, 8, BANK], F32))

    def sem(self, name):
        self.sems.append(self.nc.alloc_semaphore(f"{self.tag}_{name}"))
        return self.sems[-1]

    def block(self):
        return self.stack.enter_context(self.nc.Block())


class Chain:

    def __init__(self, eng, sem, base=0):
        self.eng, self.sem, self.base, self.n = eng, sem, base, 0

    def go(self, ins):
        self.n += 1
        ins.then_inc(self.sem, 1)

    def wait(self):
        self.eng.wait_ge(self.sem, self.base + self.n)

    def __call__(self, ins):
        self.go(ins)
        self.wait()


def signal(eng, ins, sem, value):
    ins.then_inc(sem, 1)
    eng.wait_ge(sem, value)


def wait_apart(eng, sem, value):
    eng.wait_ge(sem, value)
    eng.nop(nofuse=True)


def constants(nc, keep):
    def sb(name, shape, dt=F32):
        return keep.enter_context(nc.sbuf_tensor(f"const_{name}", shape, dt))

    C = {}
    for name in ("ident", "ones", "neg_ones", "later_neg", "after", "head_sum", "head_mean", "tmp", "first_down",
                 "first_up"):
        C[name] = sb(name, [P, P])
    C["levels"] = sb("levels", [P, 5, P])
    C["seen"] = sb("seen", [P, 2, P])
    C["blocks"] = sb("blocks", [P, 6, P])
    C["no_carry"] = sb("no_carry", [P, 512])
    with Stage(nc, "const") as st:
        steps, vsteps, pool_done = st.sem("pool_steps"), st.sem("vector_steps"), st.sem("pool_done")
        block = st.block()

        @block.gpsimd
        def _(pool):
            do = Chain(pool, steps)
            do(pool.memset(C["ident"][:], 0.0))
            do(pool.affine_select(C["ident"][:], C["ident"][:], [[-1, P]], ALU.not_equal, 1.0, base=0,
                                  channel_multiplier=1))
            for name, value in (("ones", 1.0), ("neg_ones", -1.0), ("after", 1.0), ("later_neg", -1.0),
                                ("head_sum", 0.0), ("head_mean", 0.0), ("no_carry", 1.0), ("blocks", 1.0)):
                do(pool.memset(C[name][:], value))
            do(pool.affine_select(C["after"][:], C["after"][:], [[1, P]], ALU.is_gt, 0.0, base=0,
                                  channel_multiplier=-1))
            do(pool.affine_select(C["later_neg"][:], C["later_neg"][:], [[-1, P]], ALU.is_ge, 0.0, base=0,
                                  channel_multiplier=1))
            for h in range(2):
                half = slice(64 * h, 64 * h + 64)
                do(pool.memset(C["head_sum"][half, half], 1.0))
                do(pool.memset(C["head_mean"][half, half], 1.0 / 64))
            do(pool.memset(C["no_carry"][:].rearrange("p (c t) -> p c t", t=CHUNK)[:, :, 0:1], 0.0))
            for n in range(6):
                w = 2 << n
                blk = C["blocks"][:, n, :].rearrange("p (b w) -> p b w", w=w)
                do(pool.affine_select(blk, blk, [[-w, P // w], [0, w]], ALU.is_ge, 0.0, base=0,
                                      channel_multiplier=1))
                do(pool.affine_select(blk, blk, [[w, P // w], [0, w]], ALU.is_ge, 0.0, base=w - 1,
                                      channel_multiplier=-1))
            pool.nop().then_inc(pool_done, 1)

        @block.vector
        def _(v):
            v.wait_ge(pool_done, 1)
            do = Chain(v, vsteps)
            do(v.tensor_tensor(C["seen"][:, 0, :], C["blocks"][:, 5, :], C["after"][:], ALU.mult))
            do(v.tensor_tensor(C["seen"][:, 1, :], C["seen"][:, 0, :], C["ident"][:], ALU.add))
            do(v.tensor_tensor(C["tmp"][:], C["blocks"][:, 0, :], C["ident"][:], ALU.subtract))
            do(v.tensor_tensor(C["first_up"][:], C["tmp"][:], C["after"][:], ALU.mult))
            do(v.tensor_tensor(C["first_down"][:], C["tmp"][:], C["first_up"][:], ALU.subtract))
            for n in range(5):
                do(v.tensor_tensor(C["tmp"][:], C["blocks"][:, n + 1, :], C["blocks"][:, n, :], ALU.subtract))
                do(v.tensor_tensor(C["levels"][:, n, :], C["tmp"][:], C["after"][:], ALU.mult))
    return C


def norm_transpose(nc, tag, C, rows, out_T, gain=None, rows_dram=None, load=None):
    TT, D = rows.shape[1], rows.shape[2]
    KT = D // P
    with Stage(nc, tag) as st:
        sq = st.sb("squares", [P, D])
        normed = st.sb("normed", [P, TT, D])
        ss = st.sb("ss", [P, 3, TT])
        g = st.sb("gain", [P, KT]) if gain is not None else None
        ps = st.psum()
        landed = [st.sem(f"landed{t}") for t in range(TT)]
        gain_in, stored, squared, inverse, rooted = (st.sem(n) for n in ("gain", "stored", "squared", "inverse",
                                                                           "rooted"))
        scaled, turned, vsteps = st.sem("scaled"), st.sem("turned"), st.sem("vector_steps")
        kept = st.sem("kept_vector"), st.sem("kept_scalar")
        block = st.block()

        @block.sync
        def _(sp):
            if load is not None:
                for t in range(TT):
                    sp.dma_start(rows[:, t, :], load[t * P:(t + 1) * P, :]).then_inc(landed[t], 16)
            if g is not None:
                with nc.allow_non_contiguous_dma("a gain per partition"):
                    sp.dma_start(g[:], gain.rearrange("(k p) -> p k", p=P)).then_inc(gain_in, 16)
            if rows_dram is not None:
                for t in range(TT):
                    sp.wait_ge(scaled, t + 1)
                    sp.dma_start(rows_dram[t * P:(t + 1) * P, :], normed[:, t, :]).then_inc(stored, 16)
                sp.wait_ge(stored, 16 * TT)

        @block.scalar
        def _(act):
            for t in range(TT):
                if load is not None:
                    act.wait_ge(landed[t], 16)
                signal(act, act.activation(sq[:], rows[:, t, :], ACT.Square, accum_out=ss[:, 0, t:t + 1]),
                       squared, t + 1)
            act.wait_ge(inverse, 1)
            signal(act, act.activation(ss[:, 2, :], ss[:, 1, :], ACT.Sqrt), rooted, 1)
            if g is not None:
                act.wait_ge(gain_in, 16)
            for k in range(1, KT, 2):
                act.wait_ge(turned, k + 1)
                act.activation(out_T[:, k, :], ps[:, k % 4, :], ACT.Copy,
                               scale=g[:, k:k + 1] if g is not None else 1.0).then_inc(kept[1], 1)

        @block.vector
        def _(v):
            do = Chain(v, vsteps)
            v.wait_ge(squared, TT)
            do(v.tensor_scalar(ss[:, 1, :], ss[:, 0, :], 1.0 / D, RMS_EPS, ALU.mult, ALU.add))
            signal(v, v.reciprocal(ss[:, 1, :], ss[:, 1, :]), inverse, 1)
            v.wait_ge(rooted, 1)
            for t in range(TT):
                v.tensor_scalar(normed[:, t, :], rows[:, t, :], ss[:, 2, t:t + 1], None,
                                ALU.mult).then_inc(scaled, 1)
            if g is not None:
                v.wait_ge(gain_in, 16)
            for k in range(0, KT, 2):
                v.wait_ge(turned, k + 1)
                if g is not None:
                    ins = v.tensor_scalar(out_T[:, k, :], ps[:, k % 4, :], g[:, k:k + 1], None, ALU.mult)
                else:
                    ins = v.tensor_copy(out_T[:, k, :], ps[:, k % 4, :])
                ins.then_inc(kept[0], 1)

        @block.tensor
        def _(pe):
            pe.wait_ge(scaled, TT)
            for k in range(KT):
                if k >= 4:
                    pe.wait_ge(kept[k % 2], (k - 4) // 2 + 1)
                for t in range(TT):
                    ins = pe.transpose(ps[:, k % 4, t * P:(t + 1) * P], normed[:, t, k * P:(k + 1) * P],
                                       C["ident"][:])
                ins.then_inc(turned, 1)


def project_rows(nc, tag, act_T, weights, halves, vector, scalar=None, setup=None, sync=None, finish=None,
                 scalar_first=None):
    KT = act_T.shape[1]
    SLOT, RING = 2, 4
    LOADS = KT // SLOT
    with Stage(nc, tag) as st:
        ring = st.sb("weights", [P, RING, SLOT, 1024])
        ps = st.psum()
        landed = [st.sem(f"landed{r}") for r in range(RING)]
        used, product, taken_v, taken_s = (st.sem(n) for n in ("used", "product", "taken_v", "taken_s"))
        extra = setup(st) if setup else {}
        block = st.block()
        src = weights.rearrange("(k p) n -> p k n", p=P)
        loads = [(half, n) for half in range(halves) for n in range(LOADS)]
        n_s = 4 if scalar else 0
        n_v = 8 - n_s

        @block.sync
        def _(sp):
            if sync:
                sync(sp, extra)
            for i, (half, n) in enumerate(loads):
                r = i % RING
                if i >= RING:
                    before, m = loads[i - RING]
                    if m == LOADS - 1:
                        sp.wait_ge(product, 8 * (before + 1))
                    else:
                        sp.wait_ge(used, before * (LOADS - 1) + m + 1)
                sp.dma_start(ring[:, r, :, :], src[:, n * SLOT:(n + 1) * SLOT, half * 1024:(half + 1) * 1024]
                             ).then_inc(landed[r], 16)

        @block.tensor
        def _(pe):
            for i, (half, n) in enumerate(loads):
                r = i % RING
                pe.wait_ge(landed[r], 16 * (i // RING + 1))
                if n == 0 and half:
                    pe.wait_ge(taken_v, half * n_v)
                    if n_s:
                        pe.wait_ge(taken_s, half * n_s)
                for s in range(SLOT):
                    k = n * SLOT + s
                    for t in range(4):
                        for c in range(2):
                            ins = pe.matmul(ps[:, 2 * t + c, :], act_T[:, k, t * P:(t + 1) * P],
                                            ring[:, r, s, c * BANK:(c + 1) * BANK],
                                            start=(k == 0), stop=(k == KT - 1))
                            if k == KT - 1:
                                ins.then_inc(product, 1)
                if n < LOADS - 1:
                    ins.then_inc(used, 1)

        @block.vector
        def _(v):
            for half in range(halves):
                for b in range(0, 8, 2 if scalar else 1):
                    v.wait_ge(product, half * 8 + b + 1)
                    vector(v, half, b, ps, extra, taken_v)
            if finish:
                finish[0](v, extra, taken_v, taken_s)

        @block.scalar
        def _(act):
            if scalar_first:
                for half in range(halves):
                    for b in range(8):
                        act.wait_ge(product, half * 8 + b + 1)
                        scalar_first(act, half, b, ps, extra, taken_v)
            if scalar:
                for half in range(halves):
                    for b in range(1, 8, 2):
                        act.wait_ge(product, half * 8 + b + 1)
                        scalar(act, half, b, ps, extra, taken_s)
            if finish:
                finish[1](act, extra, taken_v, taken_s)


def value_projection(nc, norm_T, w_v, v_rows):
    def vector(v, half, b, ps, extra, done):
        v.tensor_copy(v_rows[:, b // 2, (b % 2) * BANK:(b % 2 + 1) * BANK], ps[:, b, :]).then_inc(done, 1)

    def scalar(act, half, b, ps, extra, done):
        act.activation(v_rows[:, b // 2, (b % 2) * BANK:(b % 2 + 1) * BANK], ps[:, b, :], ACT.Copy).then_inc(done, 1)

    project_rows(nc, "values", norm_T, w_v, 1, vector, scalar)


def attention(nc, C, norm_T, w_in, v_rows, q_gain, k_gain, out_gain, mixed_T, heads, width):
    KT, S = norm_T.shape[1], norm_T.shape[2]
    HD, NB = P, S // P
    Q, K, OUT = range(3)
    S_STEPS = 8
    EARLY, K_EARLY = KT // 2, KT // 2
    with Stage(nc, "attn") as st:
        w_qk = st.sb("w_qk", [P, 2, KT, HD])
        gains = st.sb("gains", [P, 3])
        eps = st.sb("eps", [P, 1])
        square = st.sb("square", [P, 3, S])
        root = st.sb("root", [P, 3, S])
        qk_T = st.sb("qk_T", [P, 2, S])
        log1p = st.sb("log1p", [P, NB, S])
        softplus = st.sb("softplus", [P, NB, S])
        weight = st.sb("weight", [P, NB, S])
        v_head = st.sb("v_head", [P, NB, HD])
        out_raw = st.sb("out_raw", [P, S])
        ps = st.psum()
        BQ, BO, BN, BZ = 0, 2, 3, 4
        sem = {n: st.sem(n) for n in (
            "gain_in", "eps_set", "scored", "soft_in", "soft", "masked", "exponent", "weighted", "weight_ready",
            "v_ready", "output", "out_copied", "gain_scaled", "s_steps")}
        w_in_sem = [st.sem(n) for n in ("wq_in", "wk_in")]
        projected = [st.sem(n) for n in ("q_projected", "k_projected")]
        squared, summed, logged, rooted, normed = ([st.sem(f"{x}_{n}") for x in ("q", "k", "out")]
                                                   for n in ("squared", "summed", "logged", "rooted", "normed"))
        block = st.block()
        src = w_in.rearrange("(k p) n -> p k n", p=P)

        @block.sync
        def _(sp):
            with nc.allow_non_contiguous_dma("a gain per partition"):
                for n, g in enumerate((q_gain, k_gain, out_gain)):
                    sp.dma_start(gains[:, n:n + 1], g.rearrange("(p o) -> p o", o=1)).then_inc(sem["gain_in"], 16)

            def load(h, first):
                for n in (Q, K):
                    if not first:
                        sp.wait_ge(projected[n], h)
                    sp.dma_start(w_qk[:, n, :, :], src[:, :, ds(h * HD + n * width, HD)]).then_inc(w_in_sem[n], 16)
            load(0, True)
            with sp.Fori(1, heads) as h:
                load(h, False)

        @block.tensor
        def _(pe):
            def project(h, n, first, last):
                if first == 0:
                    pe.wait_ge(w_in_sem[n], (h + 1) * 16)
                    if not isinstance(h, int) or h:
                        pe.wait_ge(normed[n], h)
                for k in range(first, last):
                    ins = pe.matmul(ps[:, BQ + n, :], w_qk[:, n, k, :], norm_T[:, k, :], start=(k == 0),
                                    stop=(k == KT - 1))
                if last == KT:
                    ins.then_inc(projected[n], 1)

            def square_sum(h, n, bank):
                pe.wait_ge(squared[n], h + 1)
                pe.matmul(ps[:, bank, :], C["ones"][:], square[:, n, :], start=True, stop=True).then_inc(summed[n], 1)

            def scores(h):
                pe.wait_ge(normed[Q], h + 1)
                pe.wait_ge(normed[K], h + 1)
                for b in range(NB):
                    pe.matmul(ps[:, BZ + b, b * P:], qk_T[:, 1, b * P:(b + 1) * P], qk_T[:, 0, b * P:],
                              start=True, stop=True).then_inc(sem["scored"], 1)

            def exponents(h):
                pe.wait_ge(sem["masked"], NB * h + NB)
                for b in range(NB):
                    for j in range(b, NB):
                        ins = pe.matmul(ps[:, BZ + b, j * P:], C["later_neg" if j == b else "neg_ones"][:],
                                        softplus[:, j, j * P:], start=False, stop=(j == NB - 1),
                                        skip_group_check=True)
                    ins.then_inc(sem["exponent"], 1)

            def output(h):
                pe.wait_ge(sem["v_ready"], h + 1)
                for b in range(NB):
                    pe.wait_ge(sem["weight_ready"], NB * h + b + 1)
                    ins = pe.matmul(ps[:, BO, b * P:], v_head[:, b, :], weight[:, b, b * P:], start=(b == 0),
                                    stop=(b == NB - 1))
                ins.then_inc(sem["output"], 1)

            def head(h, behind):
                scores(h)
                if behind:
                    project(h + 1, Q, EARLY, KT)
                    project(h + 1, K, 0, K_EARLY)
                exponents(h)
                if behind:
                    square_sum(h + 1, Q, BN)
                    project(h + 1, K, K_EARLY, KT)
                output(h)
                if behind:
                    pe.wait_ge(logged[Q], h + 2)
                    square_sum(h + 1, K, BN)
                if behind > 1:
                    project(h + 2, Q, 0, EARLY // 2)
                square_sum(h, OUT, BO)
                if behind > 1:
                    project(h + 2, Q, EARLY // 2, EARLY)

            project(0, Q, 0, KT)
            square_sum(0, Q, BN)
            project(0, K, 0, KT)
            pe.wait_ge(logged[Q], 1)
            square_sum(0, K, BN)
            project(1, Q, 0, EARLY)
            with pe.Fori(0, heads - 2) as h:
                head(h, 2)
            head(heads - 2, 1)
            head(heads - 1, 0)

        @block.scalar
        def _(act):
            def take_square(h, n):
                act.wait_ge(projected[n], h + 1)
                act.activation(square[:, n, :], ps[:, BQ + n, :], ACT.Square).then_inc(squared[n], 1)

            def take_root(h, n, bank):
                act.wait_ge(summed[n], h + 1)
                signal(act, act.activation(root[:, n, :], ps[:, bank, :], ACT.Ln, scale=1.0 / HD, bias=eps[:]),
                       logged[n], h + 1)
                act.activation(root[:, n, :], root[:, n, :], ACT.Exp, scale=-0.5).then_inc(rooted[n], 1)

            def head(h, last):
                do = Chain(act, sem["s_steps"], h * S_STEPS)
                for b in range(NB):
                    act.wait_ge(sem["scored"], NB * h + b + 1)
                    do.go(act.activation(log1p[:, b, b * P:], ps[:, BZ + b, b * P:], ACT.Abs))
                do.wait()
                for b in range(NB):
                    do.go(act.activation(log1p[:, b, b * P:], log1p[:, b, b * P:], ACT.Exp, scale=-1.0))
                do.wait()
                for b in range(NB):
                    act.activation(log1p[:, b, b * P:], log1p[:, b, b * P:], ACT.Ln, bias=1.0
                                   ).then_inc(sem["soft_in"], 1)
                assert do.n == S_STEPS
                act.activation(v_head[:], v_rows[:, :, ds(h * HD, HD)], ACT.Copy).then_inc(sem["v_ready"], 1)
                if not last:
                    take_square(h + 1, Q)
                for b in range(NB):
                    act.wait_ge(sem["exponent"], NB * h + b + 1)
                    act.activation(weight[:, b, b * P:], ps[:, BZ + b, b * P:], ACT.Exp).then_inc(sem["weighted"], 1)
                if not last:
                    take_root(h + 1, Q, BN)
                    take_square(h + 1, K)
                act.wait_ge(sem["output"], h + 1)
                signal(act, act.activation(out_raw[:], ps[:, BO, :], ACT.Copy), sem["out_copied"], h + 1)
                act.activation(square[:, OUT, :], out_raw[:], ACT.Square).then_inc(squared[OUT], 1)
                if not last:
                    take_root(h + 1, K, BN)
                take_root(h, OUT, BO)

            act.wait_ge(sem["eps_set"], 1)
            take_square(0, Q)
            take_root(0, Q, BN)
            take_square(0, K)
            take_root(0, K, BN)
            with act.Fori(0, heads - 1) as h:
                head(h, False)
            head(heads - 1, True)

        @block.vector
        def _(v):
            def normalise(h, n):
                v.wait_ge(rooted[n], h + 1)
                v.scalar_tensor_tensor(qk_T[:, n, :], ps[:, BQ + n, :], gains[:, n:n + 1], root[:, n, :],
                                       ALU.mult, ALU.mult).then_inc(normed[n], 1)

            def head(h, last):
                for b in range(NB):
                    v.wait_ge(sem["soft_in"], NB * h + b + 1)
                    v.scalar_tensor_tensor(softplus[:, b, b * P:], ps[:, BZ + b, b * P:], 0.0,
                                           log1p[:, b, b * P:], ALU.max, ALU.add).then_inc(sem["soft"], 1)
                if not last:
                    normalise(h + 1, Q)
                    normalise(h + 1, K)
                v.wait_ge(rooted[OUT], h + 1)
                v.scalar_tensor_tensor(mixed_T[:, ds(h, 1), :].rearrange("p o s -> p (o s)"), out_raw[:],
                                       gains[:, 2:3], root[:, OUT, :], ALU.mult, ALU.mult).then_inc(normed[OUT], 1)

            v.memset(eps[:], RMS_EPS).then_inc(sem["eps_set"], 1)
            v.wait_ge(sem["gain_in"], 48)
            signal(v, v.tensor_scalar(gains[:, 0:1], gains[:, 0:1], 1.0 / math.sqrt(HD), None, ALU.mult),
                   sem["gain_scaled"], 1)
            normalise(0, Q)
            normalise(0, K)
            with v.Fori(0, heads - 1) as h:
                head(h, False)
            head(heads - 1, True)

        @block.gpsimd
        def _(pool):
            def head(h):
                for source, tile, done in (("soft", softplus, "masked"), ("weighted", weight, "weight_ready")):
                    for b in range(NB):
                        wait_apart(pool, sem[source], NB * h + b + 1)
                        own = tile[:, b, b * P:(b + 1) * P]
                        pool.affine_select(own, own, [[1, P]], ALU.is_gt, 0.0, base=0,
                                           channel_multiplier=-1).then_inc(sem[done], 1)
            with pool.Fori(0, heads) as h:
                head(h)


def time_mix(nc, C, norm_T, w_u, mu, w0, w2, a0, a2, g2, k_k, k_a, r_k, ln_g, ln_b, mixed_T, first_out, width):
    KT, S = norm_T.shape[1], norm_T.shape[2]
    PAIRS, NT, NC = width // P, S // P, S // CHUNK
    LW = w2.shape[0]
    GA = P
    GB = g2.shape[0] - P
    N_PAR = 10
    MU_R, MU_K, MU_V, W0, A0, KK, KA, RK, LG, LB = range(N_PAR)
    PROJ = 7
    with Stage(nc, "mix") as st:
        w_rkv = st.sb("w_rkv", [P, 3, KT, P])
        w2_s = st.sb("w2", [P, 2, P])
        g2_s = st.sb("g2", [P, 2, P])
        params = st.sb("params", [P, N_PAR, PAIRS])
        par = st.sb("par", [P, N_PAR])
        par_end = st.sb("par_end", [P, 2])
        eps = st.sb("eps", [P, 2])
        lora_mu = st.sb("lora_mu", [P, 3])
        raw = st.sb("raw", [P, 3, S + 1])
        step = st.sb("step", [P, S])
        lora = st.sb("lora", [P, 3, S])
        rkv = st.sb("rkv", [P, 3, S])
        a_t, logw, kk, kmix, cum, e_in, e_out, t1, t2 = (st.sb(n, [P, S]) for n in (
            "a", "logw", "kk", "kmix", "cum", "e_in", "e_out", "t1", "t2"))
        y, bonus, gate_s = (st.sb(n, [P, S]) for n in ("y", "bonus", "gate"))
        ar = st.sb("ar", [P, NT, 2, P])
        b_in, k_in = st.sb("b_in", [P, 2, S]), st.sb("k_in", [P, 2, S])
        e_end, b_end, k_end = t1, logw, a_t
        d_end = st.sb("d_end", [P, NC])
        rows = st.sb("rows", [P, 3, NT, P])
        from_b = st.sb("from_b", [P, 2, NT, 2, P])
        from_k = st.sb("from_k", [P, 2, NT, 2, P])
        inv = st.sb("inv", [P, 2, NT, P])
        inv_T = st.sb("inv_T", [P, 2, NT, P])
        join = st.sb("join", [P, 2, NT, P])
        joined = st.sb("joined", [P, 2, NT, P])
        lv = st.sb("lv", [P, NT, P])
        y_scale = lv[:].rearrange("p t f -> p (t f)")
        x_rows = st.sb("x_rows", [P, P])
        u_rows = st.sb("u_rows", [P, NT, P])
        state = st.sb("state", [P, NC, P])
        ps = st.psum()
        names = ("par_in", "lora_w_in", "r_w_in", "k_w_in", "v_w_in", "w2_in", "g2_in", "lora_mu_in", "zeroed",
                 "lora_product", "lora_raw", "lora_step", "lora_ready", "product", "raw_ready", "shift_steps",
                 "par_ready", "lora_wa", "wa_ready", "kk_ready", "kk_square", "kk_sum", "kk_log", "kk_root", "decays",
                 "exps", "ends_can_start", "ends", "factors", "turned", "rows_kept", "gram", "gram_kept",
                 "first_gram", "inv_start", "join_ready", "join_product", "joined_kept", "level", "level_kept",
                 "lv_product", "lv_kept", "x_product", "x_kept", "u_product", "u_kept", "s_product", "s_kept",
                 "y_product", "y_kept", "mean", "centred", "y_square", "var", "var_log", "var_root", "bonus_in",
                 "bonus_sum", "bonus_steps", "gate", "gate_kept", "v_steps", "end_steps", "inv_kept", "s_half",
                 "pool_steps", "y_ready", "mixed")
        sem = {n: st.sem(n) for n in names}
        w_in_sems = [sem["r_w_in"], sem["k_w_in"], sem["v_w_in"]]
        block = st.block()
        src = w_u.rearrange("(k p) n -> p k n", p=P)
        half = lambda c: slice((c % 2) * CHUNK, (c % 2) * CHUNK + CHUNK)
        head = lambda h: slice(64 * h, 64 * h + 64)
        tiles = lambda x: x.rearrange("p (t s) -> p t s", s=P)
        chunks = lambda x: x.rearrange("p (c s) -> p c s", s=CHUNK)

        @block.sync
        def _(sp):
            lo = 3 * width
            sp.dma_start(w_rkv[:, 0, :, :], src[:, :, lo:lo + P]).then_inc(sem["lora_w_in"], 16)
            sp.dma_start(w_rkv[:, 1, :, :], src[:, :, lo + P:lo + 2 * P]).then_inc(sem["lora_w_in"], 16)
            sp.dma_start(w_rkv[:, 2, :, 0:GB], src[:, :, lo + 2 * P:lo + 2 * P + GB]).then_inc(sem["lora_w_in"], 16)
            with nc.allow_non_contiguous_dma("a parameter per partition"):
                for n in range(2):
                    sp.dma_start(lora_mu[:, n:n + 1], mu[lo + n * P:lo + (n + 1) * P].rearrange("(p o) -> p o", o=1)
                                 ).then_inc(sem["lora_mu_in"], 16)
                sp.dma_start(lora_mu[0:GB, 2:3], mu[lo + 2 * P:lo + 2 * P + GB].rearrange("(p o) -> p o", o=1)
                             ).then_inc(sem["lora_mu_in"], 16)
                for n, a in enumerate((mu[0:width], mu[width:2 * width], mu[2 * width:3 * width], w0, a0, k_k, k_a,
                                       r_k, ln_g, ln_b)):
                    sp.dma_start(params[:, n, :], a.rearrange("(g p) -> p g", p=P)).then_inc(sem["par_in"], 16)

            def load_rkv(g, n):
                sp.dma_start(w_rkv[:, n, :, :], src[:, :, ds(g * P + n * width, P)]).then_inc(w_in_sems[n], 16)

            def load_w2(g):
                sp.dma_start(w2_s[0:LW, 0, :], w2[:, ds(g * P, P)]).then_inc(sem["w2_in"], 16)
                sp.dma_start(w2_s[LW:2 * LW, 1, :], a2[:, ds(g * P, P)]).then_inc(sem["w2_in"], 16)

            def load_g2(g):
                sp.dma_start(g2_s[:, 0, :], g2[0:GA, ds(g * P, P)]).then_inc(sem["g2_in"], 16)
                sp.dma_start(g2_s[0:GB, 1, :], g2[GA:GA + GB, ds(g * P, P)]).then_inc(sem["g2_in"], 16)

            for n in range(3):
                sp.wait_ge(sem["lora_product"], n + 1)
                load_rkv(0, n)
            sp.wait_ge(sem["zeroed"], 1)
            load_w2(0)
            for n in range(3):
                sp.wait_ge(sem["product"], n + 1)
                load_rkv(1, n)
            load_g2(0)
            with sp.Fori(1, PAIRS - 1) as g:
                wait_apart(sp, sem["lora_wa"], 2 * g)
                load_w2(g)
                for n in range(3):
                    wait_apart(sp, sem["product"], 3 * g + n + 1)
                    load_rkv(g + 1, n)
                wait_apart(sp, sem["gate"], g)
                load_g2(g)
            sp.wait_ge(sem["lora_wa"], 2 * (PAIRS - 1))
            load_w2(PAIRS - 1)
            sp.wait_ge(sem["gate"], PAIRS - 1)
            load_g2(PAIRS - 1)

        @block.tensor
        def _(pe):
            pe.wait_ge(sem["lora_w_in"], 48)
            for n, m in ((0, P), (1, P), (2, GB)):
                for k in range(KT):
                    ins = pe.matmul(ps[0:m, n, :], w_rkv[:, n, k, 0:m], norm_T[:, k, :], start=(k == 0),
                                    stop=(k == KT - 1))
                ins.then_inc(sem["lora_product"], 1)
            pe.wait_ge(sem["lora_ready"], 3)

            def project(g, first, last):
                for i in range(first, last):
                    n, k = divmod(i, KT)
                    if k == 0:
                        pe.wait_ge(w_in_sems[n], 16 * (g + 1))
                        if n or not isinstance(g, int) or g:
                            pe.wait_ge(sem["raw_ready"], 3 * g + n)
                    ins = pe.matmul(ps[:, PROJ, :], w_rkv[:, n, k, :], norm_T[:, k, :], start=(k == 0),
                                    stop=(k == KT - 1))
                    if k == KT - 1:
                        ins.then_inc(sem["product"], 1)

            def mean_and_gate(g):
                pe.wait_ge(sem["g2_in"], (g + 1) * 32)
                pe.matmul(ps[:, 5, :], g2_s[:, 0, :], lora[:, 1, :], start=True, stop=False)
                pe.matmul(ps[:, 5, :], g2_s[0:GB, 1, :], lora[0:GB, 2, :], start=False, stop=True
                          ).then_inc(sem["gate"], 1)
                pe.wait_ge(sem["y_kept"], g + 1)
                pe.matmul(ps[:, 0, :], C["head_mean"][:], y[:], start=True, stop=True).then_inc(sem["mean"], 1)

            def variance(g):
                pe.wait_ge(sem["y_square"], g + 1)
                pe.matmul(ps[:, 1, :], C["head_mean"][:], y_scale, start=True, stop=True).then_inc(sem["var"], 1)

            def pair(g, first=False, last=False):
                pe.wait_ge(sem["w2_in"], (g + 1) * 32)
                for n in range(2):
                    pe.matmul(ps[:, 3 + n, :], w2_s[:, n, :], lora[:, 0, :], start=True, stop=True
                              ).then_inc(sem["lora_wa"], 1)
                if not first:
                    mean_and_gate(g - 1)
                pe.wait_ge(sem["wa_ready"], 2 * g + 1)
                pe.wait_ge(sem["kk_square"], g + 1)
                pe.matmul(ps[:, 3, :], C["head_sum"][:], t2[:], start=True, stop=True).then_inc(sem["kk_sum"], 1)
                if not last:
                    project(g + 1, 0, 3)
                if not first:
                    variance(g - 1)
                if not last:
                    project(g + 1, 3, 16)
                for t in range(NT):
                    ins = pe.transpose(ps[:, 0, t * P:(t + 1) * P], rkv[:, 2, t * P:(t + 1) * P], C["ident"][:])
                ins.then_inc(sem["turned"], 1)
                for h in range(2):
                    pe.wait_ge(sem["factors"], 2 * g + h + 1)
                    if h:
                        pe.wait_ge(sem["gram_kept"], 8 * g + 4)
                        pe.wait_ge(sem["rows_kept"], 3 * g + 2)
                    elif not first:
                        pe.wait_ge(sem["gate_kept"], g)
                    for t in range(NT):
                        cols = slice(t * P, (t + 1) * P)
                        for n, source in enumerate((b_in, k_in)):
                            ins = pe.matmul(ps[:, 3 + 2 * n + t // 2, (t % 2) * 2 * P:(t % 2 + 1) * 2 * P],
                                            source[:, h, cols], ar[:, t, :, :].rearrange("p a t -> p (a t)"),
                                            start=True, stop=True)
                            if t % 2:
                                ins.then_inc(sem["gram"], 1)
                        ins = pe.matmul(ps[:, 2 - h, cols], ar[:, t, 0, :], b_in[:, h, cols], start=True, stop=True)
                    ins.then_inc(sem["first_gram"], 1)
                    if h == 0:
                        pe.wait_ge(sem["ends"], 2 * (g + 1))
                        if not first:
                            pe.wait_ge(sem["var_log"], g)
                        for n, source in ((1, b_end), (0, k_end)):
                            if n == 0:
                                pe.wait_ge(sem["rows_kept"], 3 * g + 1)
                            for t in range(NT):
                                ins = pe.transpose(ps[:, n, t * P:(t + 1) * P], source[:, t * P:(t + 1) * P],
                                                   C["ident"][:])
                            ins.then_inc(sem["turned"], 1)
                        if not last:
                            project(g + 1, 16, 18)
                if not last:
                    project(g + 1, 18, 22)
                pe.wait_ge(sem["gram_kept"], 8 * g + 8)
                pe.wait_ge(sem["bonus_in"], g + 1)
                pe.matmul(ps[:, 6, :], C["head_sum"][:], kk[:], start=True, stop=True).then_inc(sem["bonus_sum"], 1)
                pe.wait_ge(sem["rows_kept"], 3 * g + 3)
                pe.wait_ge(sem["inv_start"], 2 * g + 2)
                for n in range(5):
                    for h in range(2):
                        b0 = 3 - 3 * h
                        pe.wait_ge(sem["join_ready"], 10 * g + 2 * n + h + 1)
                        if n:
                            pe.wait_ge(sem["level_kept"], 10 * g + 2 * (n - 1) + h + 1)
                        for t in range(NT):
                            ins = pe.matmul(ps[:, b0, t * P:(t + 1) * P], join[:, h, t, :], inv[:, h, t, :],
                                            start=True, stop=True)
                        ins.then_inc(sem["join_product"], 1)
                    if not last:
                        project(g + 1, 22 + 2 * n, 23 + 2 * n)
                    for h in range(2):
                        b0 = 3 - 3 * h
                        pe.wait_ge(sem["joined_kept"], 10 * g + 2 * n + h + 1)
                        for t in range(NT):
                            cols = slice(t * P, (t + 1) * P)
                            if n < 4:
                                pe.matmul(ps[:, b0 + 1, cols], inv_T[:, h, t, :], joined[:, h, t, :], start=True,
                                          stop=True)
                            ins = pe.matmul(ps[:, b0 + 2, cols], joined[:, h, t, :], inv_T[:, h, t, :], start=True,
                                            stop=True)
                        ins.then_inc(sem["level"], 1)
                    if not last:
                        project(g + 1, 23 + 2 * n, 24 + 2 * n)
                pe.wait_ge(sem["level_kept"], 10 * g + 10)
                for t in range(NT):
                    for h in range(2):
                        ins = pe.matmul(ps[:, 3, t * P + 64 * h:t * P + 64 * h + 64], from_k[:, h, t, 0, :],
                                        rows[:, 0, t, head(h)], start=True, stop=True)
                ins.then_inc(sem["lv_product"], 1)
                for c in range(NC):
                    t, rr = c // 2, half(c)
                    v_at = [2 * KT + min(KT, -(-KT * i // (2 * NC - 2))) for i in (2 * c, 2 * c + 1, 2 * c + 2)]
                    if c:
                        pe.wait_ge(sem["s_kept"], (NC - 1) * g + c)
                    pe.matmul(ps[rr, 4, 0:P], ar[:, t, 0, rr], state[:, c, :], start=True, stop=True
                              ).then_inc(sem["x_product"], 1)
                    pe.matmul(ps[:, 2, c * CHUNK:(c + 1) * CHUNK], state[:, c, :], ar[:, t, 1, rr], start=(c == 0),
                              stop=False, skip_group_check=True)
                    if not last:
                        project(g + 1, v_at[0], v_at[1])
                    pe.wait_ge(sem["x_kept"], NC * g + c + 1)
                    for h in range(2):
                        ins = pe.matmul(ps[rr, 5, head(h)], inv_T[:, h, t, rr], x_rows[:, head(h)], start=True,
                                        stop=True)
                    ins.then_inc(sem["u_product"], 1)
                    pe.wait_ge(sem["u_kept"], NC * g + c + 1)
                    if c < NC - 1:
                        pe.matmul(ps[:, 6, 0:P], rows[rr, 1, t, :], u_rows[rr, t, :], start=True, stop=False)
                        pe.matmul(ps[:, 6, 0:P], rows[rr, 2, t, :], rows[rr, 0, t, :], start=False, stop=True
                                  ).then_inc(sem["s_product"], 1)
                    if c % 2:
                        for h in range(2):
                            f = head(h)
                            pe.matmul(ps[f, 2, t * P:(t + 1) * P], u_rows[:, t, f], from_b[:, h, t, 1, :],
                                      start=False, stop=False, skip_group_check=True)
                            ins = pe.matmul(ps[f, 2, t * P:(t + 1) * P], rows[:, 0, t, f], from_k[:, h, t, 1, :],
                                            start=False, stop=(c == NC - 1), skip_group_check=True)
                    if not last:
                        project(g + 1, v_at[1], v_at[2])
                ins.then_inc(sem["y_product"], 1)

            project(0, 0, 3 * KT)
            pair(0, first=True)
            with pe.Fori(1, PAIRS - 1) as g:
                pair(g)
            pair(PAIRS - 1, last=True)
            mean_and_gate(PAIRS - 1)
            variance(PAIRS - 1)

        @block.scalar
        def _(act):
            act.wait_ge(sem["zeroed"], 1)
            for n, m in ((0, P), (1, P), (2, GB)):
                act.wait_ge(sem["lora_product"], n + 1)
                act.activation(raw[0:m, n, 1:], ps[0:m, n, :], ACT.Copy).then_inc(sem["lora_raw"], 1)
            for n, m, f in ((0, LW, ACT.Tanh), (1, P, ACT.Sigmoid), (2, GB, ACT.Sigmoid)):
                act.wait_ge(sem["lora_step"], n + 1)
                act.activation(lora[0:m, n, :], lora[0:m, n, :], f).then_inc(sem["lora_ready"], 1)

            def keep_raw(g, n, first=False):
                if not first:
                    act.wait_ge(sem["shift_steps"], 6 * (g - 1) + 2 * n + 2)
                act.wait_ge(sem["product"], 3 * g + n + 1)
                act.activation(raw[:, n, 1:], ps[:, PROJ, :], ACT.Copy).then_inc(sem["raw_ready"], 1)

            def keep_y(g):
                act.wait_ge(sem["y_product"], g + 1)
                act.activation(y[:], ps[:, 2, :], ACT.Copy).then_inc(sem["y_kept"], 1)

            def gate_and_square(g):
                act.wait_ge(sem["gate"], g + 1)
                act.activation(gate_s[:], ps[:, 5, :], ACT.Copy).then_inc(sem["gate_kept"], 1)
                act.wait_ge(sem["centred"], g + 1)
                act.activation(y_scale, y[:], ACT.Square).then_inc(sem["y_square"], 1)

            def y_root(g):
                act.wait_ge(sem["var"], g + 1)
                signal(act, act.activation(y_scale, ps[:, 1, :], ACT.Ln, bias=eps[:, 1:2]), sem["var_log"], g + 1)
                act.activation(y_scale, y_scale, ACT.Exp, scale=-0.5).then_inc(sem["var_root"], 1)

            def pair(g, first=False, last=False):
                if not first:
                    keep_y(g - 1)
                act.wait_ge(sem["kk_ready"], g + 1)
                act.activation(t2[:], kk[:], ACT.Square).then_inc(sem["kk_square"], 1)
                for n, (out, bias) in enumerate(((logw, W0), (a_t, A0))):
                    act.wait_ge(sem["lora_wa"], 2 * g + n + 1)
                    act.activation(out[:], ps[:, 3 + n, :], ACT.Sigmoid, bias=par[:, bias:bias + 1]
                                   ).then_inc(sem["wa_ready"], 1)
                if not first:
                    gate_and_square(g - 1)
                act.wait_ge(sem["kk_sum"], g + 1)
                signal(act, act.activation(t1[:], ps[:, 3, :], ACT.Ln, bias=eps[:, 0:1]), sem["kk_log"], g + 1)
                act.activation(t1[:], t1[:], ACT.Exp, scale=-0.5).then_inc(sem["kk_root"], 1)
                act.wait_ge(sem["decays"], g + 1)
                act.activation(e_in[:], e_in[:], ACT.Exp).then_inc(sem["exps"], 1)
                signal(act, act.activation(e_out[:], cum[:], ACT.Exp, scale=-1.0), sem["exps"], 3 * g + 2)
                act.activation(cum[:], cum[:], ACT.Exp).then_inc(sem["exps"], 1)
                if not first:
                    y_root(g - 1)
                if not last:
                    keep_raw(g + 1, 0)
                for n, bank in ((0, 0), (1, 1), (2, 0)):
                    act.wait_ge(sem["turned"], 3 * g + n + 1)
                    act.activation(rows[:, n, :, :].rearrange("p t f -> p (t f)"), ps[:, bank, :], ACT.Copy
                                   ).then_inc(sem["rows_kept"], 1)
                for n in range(5):
                    for h in range(2):
                        act.wait_ge(sem["join_product"], 10 * g + 2 * n + h + 1)
                        act.activation(joined[:, h, :, :].rearrange("p t f -> p (t f)"), ps[:, 3 - 3 * h, :], ACT.Copy
                                       ).then_inc(sem["joined_kept"], 1)
                if not last:
                    keep_raw(g + 1, 1)
                act.wait_ge(sem["lv_product"], g + 1)
                act.activation(lv[:].rearrange("p t f -> p (t f)"), ps[:, 3, :], ACT.Copy).then_inc(sem["lv_kept"], 1)
                for c in range(NC):
                    act.wait_ge(sem["u_product"], NC * g + c + 1)
                    act.activation(u_rows[half(c), c // 2, :], ps[half(c), 5, 0:P], ACT.Copy).then_inc(sem["u_kept"], 1)
                    if c == NC - 2 and not last:
                        keep_raw(g + 1, 2)

            for n in range(3):
                keep_raw(0, n, first=True)
            pair(0, first=True)
            with act.Fori(1, PAIRS - 1) as g:
                pair(g)
            pair(PAIRS - 1, last=True)
            keep_y(PAIRS - 1)
            gate_and_square(PAIRS - 1)
            y_root(PAIRS - 1)

        @block.vector
        def _(v):
            do = Chain(v, sem["v_steps"])
            do.go(v.memset(raw[:, :, 0:1], 0.0))
            do.go(v.memset(state[:], 0.0))
            do.go(v.memset(w2_s[:], 0.0))
            do.go(v.memset(b_in[:], 0.0))
            do.go(v.memset(k_in[:], 0.0))
            do.go(v.memset(eps[:, 0:1], 1e-12))
            do.go(v.memset(eps[:, 1:2], GN_EPS))
            do(v.memset(x_rows[:], 0.0))
            v.nop().then_inc(sem["zeroed"], 1)
            v.wait_ge(sem["lora_mu_in"], 48)
            v.wait_ge(sem["par_in"], 160)
            for n, m in ((0, P), (1, P), (2, GB)):
                v.wait_ge(sem["lora_raw"], n + 1)
                do(v.tensor_tensor(step[0:m, :], raw[0:m, n, 0:S], raw[0:m, n, 1:], ALU.subtract))
                signal(v, v.scalar_tensor_tensor(lora[0:m, n, :], step[0:m, :], lora_mu[0:m, n:n + 1], raw[0:m, n, 1:],
                                                 ALU.mult, ALU.add), sem["lora_step"], n + 1)
            before, V_STEPS = do.n, 11

            def take_params(g):
                signal(v, v.tensor_copy(par[:], params[:, :, ds(g, 1)].rearrange("p n o -> p (n o)")),
                       sem["par_ready"], g + 1)

            def shift_step(g, n):
                v.wait_ge(sem["raw_ready"], 3 * g + n + 1)
                signal(v, v.tensor_tensor(step[:], raw[:, n, 0:S], raw[:, n, 1:], ALU.subtract),
                       sem["shift_steps"], 6 * g + 2 * n + 1)

            def shift(g, n):
                signal(v, v.scalar_tensor_tensor(rkv[:, n, :], step[:], par[:, MU_R + n:MU_R + n + 1],
                                                 raw[:, n, 1:], ALU.mult, ALU.add),
                       sem["shift_steps"], 6 * g + 2 * n + 2)

            def scale_kk(g):
                signal(v, v.tensor_scalar(kk[:], rkv[:, 1, :], par[:, KK:KK + 1], None, ALU.mult), sem["kk_ready"],
                       g + 1)

            def centre(g):
                v.wait_ge(sem["y_kept"], g + 1)
                v.wait_ge(sem["mean"], g + 1)
                v.tensor_tensor(y[:], y[:], ps[:, 0, :], ALU.subtract).then_inc(sem["centred"], 1)

            def scale_y(g):
                v.wait_ge(sem["var_root"], g + 1)
                signal(v, v.scalar_tensor_tensor(y[:], y[:], par_end[:, 0:1], y_scale, ALU.mult,
                                                 ALU.mult), sem["end_steps"], g + 1)
                signal(v, v.scalar_tensor_tensor(y[:], y[:], par_end[:, 1:2], bonus[:], ALU.add,
                                                 ALU.add), sem["y_ready"], g + 1)

            def pair(g, first=False, last=False):
                r, k, val = (rkv[:, n, :] for n in range(3))
                do = Chain(v, sem["v_steps"], before + g * V_STEPS)
                v.wait_ge(sem["wa_ready"], 2 * g + 1)
                do(v.tensor_scalar(logw[:], logw[:], -math.exp(-0.5), None, ALU.mult))
                do(v.tensor_tensor_scan(cum[:], C["no_carry"][:], logw[:], 0.0, ALU.mult, ALU.add))
                v.tensor_tensor(e_in[:], cum[:], logw[:], ALU.subtract).then_inc(sem["decays"], 1)
                if not first:
                    centre(g - 1)
                v.wait_ge(sem["wa_ready"], 2 * g + 2)
                do(v.tensor_scalar(kmix[:], a_t[:], 1.0, par[:, KA:KA + 1], ALU.subtract, ALU.mult))
                do(v.scalar_tensor_tensor(kmix[:], kmix[:], 1.0, k, ALU.add, ALU.mult))
                v.wait_ge(sem["kk_root"], g + 1)
                do(v.tensor_tensor(kk[:], kk[:], t1[:], ALU.mult))
                do(v.tensor_tensor(t2[:], kk[:], a_t[:], ALU.mult))
                v.wait_ge(sem["exps"], 3 * g + 3)
                do(v.tensor_copy(d_end[:], chunks(cum[:])[:, :, CHUNK - 1]))
                v.nop().then_inc(sem["ends_can_start"], 1)
                do.go(v.scalar_tensor_tensor(ar[:, :, 0, :], tiles(kk[:]), -1.0, tiles(e_in[:]), ALU.mult, ALU.mult))
                do.go(v.tensor_tensor(ar[:, :, 1, :], tiles(r), tiles(cum[:]), ALU.mult))
                for h in range(2):
                    f = head(h)
                    do.go(v.tensor_tensor(b_in[f, h, :], t2[f, :], e_out[f, :], ALU.mult))
                    v.tensor_tensor(k_in[f, h, :], kmix[f, :], e_out[f, :], ALU.mult).then_inc(sem["factors"], 1)
                do.wait()
                assert do.n == V_STEPS, do.n
                v.scalar_tensor_tensor(kk[:], r, par[:, RK:RK + 1], kmix[:], ALU.mult, ALU.mult
                                       ).then_inc(sem["bonus_in"], 1)
                if not first:
                    scale_y(g - 1)
                for h in range(2):
                    for i, (bank, kept, t0) in enumerate(((3, from_b, 0), (5, from_k, 0), (4, from_b, 2),
                                                          (6, from_k, 2))):
                        v.wait_ge(sem["gram"], 8 * g + 4 * h + i + 1)
                        v.tensor_tensor(kept[:, h, t0:t0 + 2, :, :].rearrange("p t a s -> p t (a s)"),
                                        ps[:, bank, :].rearrange("p (t s) -> p t s", t=2),
                                        C["seen"][:].rearrange("p a s -> p (a s)").unsqueeze(1
                                                               ).to_broadcast([P, 2, 2 * P]),
                                        ALU.mult).then_inc(sem["gram_kept"], 1)
                    v.wait_ge(sem["first_gram"], 2 * g + h + 1)
                    signal(v, v.tensor_tensor(inv[:, h, :, :], tiles(ps[:, 2 - h, :]),
                                              C["first_down"][:].unsqueeze(1).to_broadcast([P, NT, P]), ALU.mult),
                           sem["inv_kept"], 10 * g + h + 1)
                    v.tensor_tensor(inv[:, h, :, :], inv[:, h, :, :],
                                    C["ident"][:].unsqueeze(1).to_broadcast([P, NT, P]),
                                    ALU.add).then_inc(sem["inv_start"], 1)
                for n in range(5):
                    for h in range(2):
                        flat = lambda x: x[:, h, :, :].rearrange("p t s -> p (t s)")
                        v.wait_ge(sem["level"], 10 * g + 2 * n + h + 1)
                        if n < 4:
                            v.tensor_tensor(flat(inv), flat(inv), ps[:, 4 - 3 * h, :], ALU.add
                                            ).then_inc(sem["inv_kept"], 1)
                        v.tensor_tensor(flat(inv_T), flat(inv_T), ps[:, 5 - 3 * h, :], ALU.add
                                        ).then_inc(sem["level_kept"], 1)
                    if n == 0:
                        v.wait_ge(sem["bonus_sum"], g + 1)
                        signal(v, v.tensor_tensor(bonus[:], val, ps[:, 6, :], ALU.mult), sem["bonus_steps"], 2 * g + 1)
                        signal(v, v.tensor_copy(par_end[:], par[:, LG:LB + 1]), sem["bonus_steps"], 2 * g + 2)
                    if not last:
                        if n == 0:
                            take_params(g + 1)
                        if n == 1:
                            shift_step(g + 1, 0)
                        if n == 2:
                            shift(g + 1, 0)
                v.wait_ge(sem["lv_kept"], g + 1)
                for c in range(NC):
                    rr = half(c)
                    v.wait_ge(sem["x_product"], NC * g + c + 1)
                    v.tensor_tensor(x_rows[rr, :], ps[rr, 4, 0:P], lv[rr, c // 2, :], ALU.add
                                    ).then_inc(sem["x_kept"], 1)
                    if not last:
                        if c == 0:
                            shift_step(g + 1, 1)
                        if c == 1:
                            shift(g + 1, 1)
                        if c == 2:
                            scale_kk(g + 1)
                        if c == NC - 1:
                            shift_step(g + 1, 2)
                            shift(g + 1, 2)
                    if c < NC - 1:
                        v.wait_ge(sem["s_product"], (NC - 1) * g + c + 1)
                        for h in range(2):
                            f = head(h)
                            ins = v.scalar_tensor_tensor(state[f, c + 1, f], state[f, c, f], d_end[f, c:c + 1],
                                                         ps[f, 6, f], ALU.mult, ALU.add)
                            ins.then_inc(sem["s_half" if h == 0 else "s_kept"], 1)

            take_params(0)
            for n in range(3):
                shift_step(0, n)
                shift(0, n)
            scale_kk(0)
            pair(0, first=True)
            with v.Fori(1, PAIRS - 1) as g:
                pair(g)
            pair(PAIRS - 1, last=True)
            centre(PAIRS - 1)
            scale_y(PAIRS - 1)

        @block.gpsimd
        def _(pool):
            bc = lambda m: m.unsqueeze(1).to_broadcast([P, NT, P])

            def open_gate(g):
                pool.wait_ge(sem["gate_kept"], g + 1)
                pool.wait_ge(sem["y_ready"], g + 1)
                pool.tensor_tensor(mixed_T[:, ds(first_out + g, 1), :].rearrange("p o s -> p (o s)"), y[:],
                                   gate_s[:], ALU.mult).then_inc(sem["mixed"], 1)

            def pair(g, first=False):
                do = Chain(pool, sem["pool_steps"], 5 * g)
                pool.wait_ge(sem["ends_can_start"], g + 1)
                do(pool.tensor_tensor(chunks(e_end[:]), chunks(e_out[:]),
                                      d_end[:].unsqueeze(2).to_broadcast([P, NC, CHUNK]), ALU.mult))
                pool.tensor_tensor(b_end[:], t2[:], e_end[:], ALU.mult).then_inc(sem["ends"], 1)
                pool.tensor_tensor(k_end[:], kmix[:], e_end[:], ALU.mult).then_inc(sem["ends"], 1)
                if not first:
                    open_gate(g - 1)
                for h in range(2):
                    pool.wait_ge(sem["gram_kept"], 8 * g + 4 * h + 3)
                    do(pool.tensor_tensor(inv_T[:, h, :, :], from_b[:, h, :, 0, :], bc(C["first_up"][:]), ALU.mult))
                    do(pool.tensor_tensor(inv_T[:, h, :, :], inv_T[:, h, :, :], bc(C["ident"][:]), ALU.add))
                    pool.tensor_tensor(join[:, h, :, :], from_b[:, h, :, 0, :], bc(C["levels"][:, 0, :]),
                                       ALU.mult).then_inc(sem["join_ready"], 1)
                for n in range(1, 5):
                    for h in range(2):
                        pool.wait_ge(sem["join_product"], 10 * g + 2 * (n - 1) + h + 1)
                        pool.tensor_tensor(join[:, h, :, :], from_b[:, h, :, 0, :], bc(C["levels"][:, n, :]),
                                           ALU.mult).then_inc(sem["join_ready"], 1)

            pair(0, first=True)
            with pool.Fori(1, PAIRS) as g:
                pair(g)
            open_gate(PAIRS - 1)


def output_projection(nc, mixed_T, w_out, x, x_rows):
    def setup(st):
        return {"x_in": [st.sem(f"x_in{t}") for t in range(4)]}

    def sync(sp, extra):
        for t in range(4):
            sp.dma_start(x_rows[:, t, :], x[t * P:(t + 1) * P, :]).then_inc(extra["x_in"][t], 16)

    def vector(v, half, b, ps, extra, done):
        t, cols = b // 2, slice(half * 1024 + (b % 2) * BANK, half * 1024 + (b % 2 + 1) * BANK)
        v.wait_ge(extra["x_in"][t], 16)
        v.tensor_tensor(x_rows[:, t, cols], x_rows[:, t, cols], ps[:, b, :], ALU.add).then_inc(done, 1)

    project_rows(nc, "out", mixed_T, w_out, x_rows.shape[2] // 1024, vector, setup=setup, sync=sync)


def route(nc, C, hn_T, router_g, router_g_b, router_e, router_e_b, R, token_table, items_dram):
    KT = hn_T.shape[1]
    G, E = router_g.shape[1], router_e.shape[1]
    EG, NT = E // G, 4
    NB = hn_T.shape[2] // SLOTS - 1
    NL = G + E
    with Stage(nc, "route") as st:
        w = st.sb("w", [P, KT, NL])
        bias = st.sb("bias", [NL, 1])
        logits_T = st.sb("logits_T", [NL, 512])
        lg = st.sb("logits", [P, NT, NL])
        group_at, expert_at = st.sb("group_at", [P, G]), st.sb("expert_at", [P, EG])
        first_at = st.sb("first_at", [P, NB + 1, E])
        later_at = st.sb("later_at", [P, NB, E])
        expert_no = st.sb("expert_no", [P, NB, E])
        edges = st.sb("edges", [P, NB + 2])
        block_min = st.sb("block_min", [P, NB, E])
        own_index = st.sb("own_index", [P, 1])
        token_id = st.sb("token_id", [P, NT, 16], I32)
        g4, g4b = st.sb("g4", [P, NT, G]), st.sb("g4b", [P, NT, G])
        pick = st.sb("pick", [P, NT, G, EG])
        e8, e8b, cand = (st.sb(n, [P, NT, EG]) for n in ("e8", "e8b", "cand"))
        chosen = st.sb("chosen", [P, 2, NT, EG])
        hot = st.sb("hot", [P, 2, NT, G, EG])
        both = st.sb("both", [P, NT, E])
        rank = st.sb("rank", [P, NT, E])
        picked = st.sb("picked", [P, NT, NB + 1, E])
        own_rank = st.sb("own_rank", [P, NT, 1])
        reached = st.sb("reached", [P, NT, NB + 2])
        candidate = st.sb("candidate", [P, NT, NB + 1])
        c1, c2, c3, c4, c5 = (st.sb(n, [P, NT, 1]) for n in ("c1", "c2", "c3", "c4", "c5"))
        slot_f = st.sb("slot_f", [P, 2, NT])
        count = st.sb("count", [P, E])
        over = st.sb("over", [P, NB * E])
        order = st.sb("order", [P, NB * E])
        ones_row = st.sb("ones_row", [P, NB * E])
        item = st.sb("item", [P, 1])
        ps = st.psum()
        sem = {n: st.sem(n) for n in ("w_in", "iota", "logits", "biased", "turned", "v_steps", "difference",
                                      "exp_g", "top", "exp_e", "both_ready", "ranked", "slots_ready", "scattered",
                                      "item_ready", "item_turned", "pool_steps", "items_ready")}
        block = st.block()

        @block.sync
        def _(sp):
            with nc.allow_non_contiguous_dma("router weights"):
                sp.dma_start(w[:, :, 0:G], router_g.rearrange("(k p) n -> p k n", p=P)).then_inc(sem["w_in"], 16)
                sp.dma_start(w[:, :, G:NL], router_e.rearrange("(k p) n -> p k n", p=P)).then_inc(sem["w_in"], 16)
                sp.dma_start(bias[0:G, :], router_g_b.rearrange("(p o) -> p o", o=1)).then_inc(sem["w_in"], 16)
                sp.dma_start(bias[G:NL, :], router_e_b.rearrange("(p o) -> p o", o=1)).then_inc(sem["w_in"], 16)

        @block.tensor
        def _(pe):
            pe.wait_ge(sem["w_in"], 64)
            for k in range(KT):
                ins = pe.matmul(ps[0:NL, 0, :], w[:, k, :], hn_T[:, k, :], start=(k == 0), stop=(k == KT - 1))
            ins.then_inc(sem["logits"], 1)
            pe.wait_ge(sem["biased"], 1)
            for t in range(NT):
                ins = pe.transpose(ps[:, 1, t * NL:(t + 1) * NL], logits_T[:, t * P:(t + 1) * P],
                                   C["ident"][0:NL, 0:NL])
            ins.then_inc(sem["turned"], 1)
            pe.wait_ge(sem["both_ready"], 1)
            for t in range(NT + 1):
                for j in range(min(t, NT - 1) + 1):
                    ins = pe.matmul(ps[:, 2, t * E:(t + 1) * E], C["after" if j == t else "ones"][:], both[:, j, :],
                                    start=(j == 0), stop=(j == min(t, NT - 1)))
            ins.then_inc(sem["ranked"], 1)
            pe.wait_ge(sem["item_ready"], 1)
            pe.matmul(ps[0:1, 3, 0:P], item[:], C["ident"][:], start=True, stop=True).then_inc(sem["item_turned"], 1)

        @block.scalar
        def _(act):
            act.wait_ge(sem["logits"], 1)
            act.wait_ge(sem["w_in"], 64)
            act.activation(logits_T[:], ps[0:NL, 0, :], ACT.Identity, bias=bias[:]).then_inc(sem["biased"], 1)
            act.wait_ge(sem["difference"], 1)
            act.activation(g4b[:], g4b[:], ACT.Exp).then_inc(sem["exp_g"], 1)
            act.wait_ge(sem["top"], 1)
            act.activation(c4[:], c4[:], ACT.Exp).then_inc(sem["exp_e"], 1)

        @block.gpsimd
        def _(pool):
            do = Chain(pool, sem["pool_steps"])
            kw = dict(allow_small_or_imprecise_dtypes=True)
            do.go(pool.iota(group_at[:], [[1, G]], base=-G, channel_multiplier=0, **kw))
            do.go(pool.iota(expert_at[:], [[1, EG]], base=-EG, channel_multiplier=0, **kw))
            do.go(pool.iota(first_at[:, 0, :], [[SLOTS, E]], base=0, channel_multiplier=0, **kw))
            do.go(pool.iota(later_at[:], [[-SLOTS, NB], [0, E]], base=(E - 2) * SLOTS, channel_multiplier=0, **kw))
            do.go(pool.iota(expert_no[:], [[0, NB], [1, E]], base=0, channel_multiplier=0, **kw))
            do.go(pool.iota(edges[:], [[SLOTS, NB + 2]], base=0, channel_multiplier=0, **kw))
            do.go(pool.iota(block_min[:], [[SLOTS, NB], [0, E]], base=SLOTS, channel_multiplier=0, **kw))
            do.go(pool.iota(own_index[:], [[0, 1]], base=0, channel_multiplier=1, **kw))
            do.go(pool.iota(token_id[:], [[P, NT], [0, 16]], base=0, channel_multiplier=1))
            do(pool.memset(ones_row[:], 1.0))
            pool.nop().then_inc(sem["iota"], 1)
            pool.wait_ge(sem["slots_ready"], 2)
            for n in range(2):
                for t in range(NT):
                    pool.indirect_dma_start(
                        out=token_table, out_offset=bass.IndirectOffsetOnAxis(ap=R["slot"][:, n, t:t + 1], axis=0),
                        in_=token_id[:, t, :], in_offset=None).then_inc(sem["scattered"], 16)
            pool.wait_ge(sem["scattered"], 16 * 2 * NT)

        @block.vector
        def _(v):
            do = Chain(v, sem["v_steps"])
            v.wait_ge(sem["iota"], 1)
            v.wait_ge(sem["turned"], 1)
            wide = lambda x, n: x.to_broadcast([P, NT, n])
            do(v.tensor_copy(lg[:], ps[:, 1, 0:NT * NL].rearrange("p (t n) -> p t n", n=NL)))

            def first_top(values, at, n, best, mark, cand):
                do(v.tensor_reduce(best, values, AX_X, ALU.max))
                do(v.tensor_tensor(mark, values, wide(best, n), ALU.is_equal))
                do(v.tensor_tensor(cand, mark, at[:].unsqueeze(1).to_broadcast([P, NT, n]), ALU.mult))
                do(v.tensor_reduce(c5[:], cand, AX_X, ALU.min))
                do(v.tensor_tensor(mark, at[:].unsqueeze(1).to_broadcast([P, NT, n]), wide(c5[:], n), ALU.is_equal))

            first_top(lg[:, :, 0:G], group_at, G, c1[:], g4[:], g4b[:])
            signal(v, v.tensor_tensor(g4b[:], lg[:, :, 0:G], wide(c1[:], G), ALU.subtract), sem["difference"], 1)
            do(v.tensor_tensor(pick[:], lg[:, :, G:NL].rearrange("p t (g e) -> p t g e", g=G),
                               g4[:].unsqueeze(3).to_broadcast([P, NT, G, EG]), ALU.mult))
            do(v.tensor_tensor(e8[:], pick[:, :, 0, :], pick[:, :, 1, :], ALU.add))
            for g in range(2, G):
                do(v.tensor_tensor(e8[:], e8[:], pick[:, :, g, :], ALU.add))
            first_top(e8[:], expert_at, EG, c2[:], chosen[:, 0, :, :], cand[:])
            do(v.scalar_tensor_tensor(e8b[:], chosen[:, 0, :, :], -1e30, e8[:], ALU.mult, ALU.add))
            first_top(e8b[:], expert_at, EG, c3[:], chosen[:, 1, :, :], cand[:])
            signal(v, v.tensor_tensor(c4[:], c3[:], c2[:], ALU.subtract), sem["top"], 1)
            for n in range(2):
                do(v.tensor_tensor(hot[:, n, :, :, :], g4[:].unsqueeze(3).to_broadcast([P, NT, G, EG]),
                                   chosen[:, n, :, :].unsqueeze(2).to_broadcast([P, NT, G, EG]), ALU.mult))
            flat = lambda n: hot[:, n, :, :, :].rearrange("p t g e -> p t (g e)")
            signal(v, v.tensor_tensor(both[:], flat(0), flat(1), ALU.add), sem["both_ready"], 1)
            v.wait_ge(sem["exp_g"], 1)
            do(v.tensor_reduce(c1[:], g4b[:], AX_X, ALU.add))
            v.wait_ge(sem["exp_e"], 1)
            do(v.tensor_scalar(c2[:], c4[:], 1.0, None, ALU.add))
            do(v.tensor_tensor(c2[:], c2[:], c1[:], ALU.mult))
            do(v.reciprocal(R["weight"][:, 0, :].unsqueeze(2), c2[:]))
            do(v.tensor_tensor(R["weight"][:, 1, :].unsqueeze(2), R["weight"][:, 0, :].unsqueeze(2), c4[:], ALU.mult))
            v.wait_ge(sem["ranked"], 1)
            do(v.tensor_copy(rank[:], ps[:, 2, 0:NT * E].rearrange("p (t e) -> p t e", e=E)))
            do(v.tensor_copy(count[:], ps[:, 2, NT * E:(NT + 1) * E]))
            over3 = over[:].rearrange("p (b e) -> p b e", e=E)
            do(v.tensor_tensor(over3, count[:].unsqueeze(1).to_broadcast([P, NB, E]), block_min[:], ALU.is_gt))
            do(v.tensor_tensor_scan(order[:], ones_row[:], over[:], 0.0, ALU.mult, ALU.add))
            do(v.tensor_copy(R["n_items"][:], order[:, NB * E - 1:NB * E]))
            do(v.scalar_tensor_tensor(first_at[:, 1:, :], order[:].rearrange("p (b e) -> p b e", e=E), float(SLOTS),
                                      later_at[:], ALU.mult, ALU.add))
            for n in range(2):
                do(v.tensor_tensor(picked[:, :, 0, :], rank[:], flat(n), ALU.mult))
                do(v.tensor_reduce(own_rank[:], picked[:, :, 0, :], AX_X, ALU.add))
                do(v.tensor_tensor(reached[:], own_rank[:].to_broadcast([P, NT, NB + 2]),
                                   edges[:].unsqueeze(1).to_broadcast([P, NT, NB + 2]), ALU.is_ge))
                do(v.tensor_tensor(reached[:, :, 0:NB + 1], reached[:, :, 0:NB + 1], reached[:, :, 1:NB + 2],
                                   ALU.subtract))
                do(v.tensor_tensor(picked[:], first_at[:].unsqueeze(1).to_broadcast([P, NT, NB + 1, E]),
                                   flat(n).unsqueeze(2).to_broadcast([P, NT, NB + 1, E]), ALU.mult))
                do(v.tensor_reduce(candidate[:].unsqueeze(3), picked[:], AX_X, ALU.add))
                do(v.tensor_tensor(candidate[:], candidate[:], reached[:, :, 0:NB + 1], ALU.mult))
                do(v.tensor_reduce(slot_f[:, n, :].unsqueeze(2), candidate[:], AX_X, ALU.add))
                do(v.tensor_tensor(slot_f[:, n, :].unsqueeze(2), slot_f[:, n, :].unsqueeze(2), own_rank[:], ALU.add))
                signal(v, v.tensor_copy(R["slot"][:, n, :], slot_f[:, n, :]), sem["slots_ready"], n + 1)
            do(v.tensor_tensor(order[:], order[:], over[:], ALU.mult))
            do(v.tensor_scalar(own_index[:], own_index[:], 1.0, None, ALU.add))
            do(v.tensor_scalar(order[:], order[:], own_index[:, 0:1], None, ALU.is_equal))
            do(v.tensor_tensor(over[:], order[:], expert_no[:].rearrange("p b e -> p (b e)"), ALU.mult))
            signal(v, v.tensor_reduce(item[:], over[:], AX_X, ALU.add), sem["item_ready"], 1)
            v.wait_ge(sem["item_turned"], 1)
            do(v.tensor_copy(R["item_expert"][:], ps[0:1, 3, 0:P]))


def experts(nc, C, gain, w_up, w_down, R, token_table, rows_dram, y_dram):
    E, D, F2 = w_up.shape
    F = F2 // 2
    KT, FT, ITEMS = D // P, F // P, R["max_items"]
    UP, DOWN = KT // 4, FT // 2
    with Stage(nc, "moe") as st:
        w_u = st.sb("w_up", [P, UP, 4, F2])
        w_d = st.sb("w_down", [P, DOWN, 2, D])
        g = st.sb("gain", [P, KT])
        ids = st.sb("ids", [SLOTS, 16], I32)
        x_in = st.sb("x_in", [SLOTS, D])
        x_T = st.sb("x_T", [P, KT, SLOTS])
        sig = st.sb("sig", [P, F // 2])
        hid = st.sb("hid", [P, F // 2])
        hid_T = st.sb("hid_T", [P, 2, 2, SLOTS])
        y = st.sb("y", [P, 2, BANK])
        ps = st.psum()
        up_in = [st.sem(f"up_in{n}") for n in range(UP)]
        down_in = [st.sem(f"down_in{n}") for n in range(DOWN)]
        sem = {n: st.sem(n) for n in ("gain_in", "ids_in", "x_in", "x_turned", "x_scaled", "up_used", "up_done",
                                      "sigmoid", "gated", "hidden", "hid_turned", "hid_kept", "down_used",
                                      "y_kept_v", "y_kept_s", "stored")}
        block = st.block()

        def turns(eng, turn):
            turn(0, 0, 0, True)
            with eng.Fori(1, E) as i:
                turn(i, i, i * SLOTS, False)
            n_items = eng.value_load(R["n_items"][0:1, 0:1], min_val=0, max_val=ITEMS)
            with eng.If(n_items > 0):
                with eng.Fori(0, ITEMS) as i:
                    with eng.If(n_items > i):
                        expert = eng.value_load(R["item_expert"][0:1, ds(i, 1)], min_val=0, max_val=E - 1)
                        turn(i + E, expert, (i + E) * SLOTS, False)
                    eng.nop()
            eng.nop()

        @block.sync
        def _(sp):
            with nc.allow_non_contiguous_dma("a gain per partition"):
                sp.dma_start(g[:], gain.rearrange("(k p) -> p k", p=P)).then_inc(sem["gain_in"], 16)
            up = w_up.rearrange("e (n k p) f -> e p n k f", p=P, k=4)
            down = w_down.rearrange("e (n k p) f -> e p n k f", p=P, k=2)

            def turn(i, expert, row, first):
                for n in range(UP):
                    if not first:
                        sp.wait_ge(sem["up_used"], (i - 1) * UP + n + 1)
                    sp.dma_start(w_u[:, n, :, :], up[ds(expert, 1), :, n, :, :].rearrange("e p k f -> (e p) k f")
                                 ).then_inc(up_in[n], 16)
                for n in range(DOWN):
                    if not first:
                        sp.wait_ge(sem["down_used"], (i - 1) * DOWN + n + 1)
                    sp.dma_start(w_d[:, n, :, :], down[ds(expert, 1), :, n, :, :].rearrange("e p k f -> (e p) k f")
                                 ).then_inc(down_in[n], 16)
            turns(sp, turn)

        @block.gpsimd
        def _(pool):
            def turn(i, expert, row, first):
                if not first:
                    pool.wait_ge(sem["x_turned"], i * 2)
                pool.dma_start(ids[:], token_table[ds(row, SLOTS), :]).then_inc(sem["ids_in"], 16)
                wait_apart(pool, sem["ids_in"], (i + 1) * 16)
                pool.indirect_dma_start(out=x_in[:], out_offset=None, in_=rows_dram,
                                        in_offset=bass.IndirectOffsetOnAxis(ap=ids[:, 0:1], axis=0)
                                        ).then_inc(sem["x_in"], 16)
            turns(pool, turn)

        @block.tensor
        def _(pe):
            def turn(i, expert, row, first):
                wait_apart(pe, sem["x_in"], (i + 1) * 16)
                for b in range(2):
                    for k in range(KT // 2):
                        kk = b * KT // 2 + k
                        ins = pe.transpose(ps[:, b, k * SLOTS:(k + 1) * SLOTS], x_in[:, kk * P:(kk + 1) * P],
                                           C["ident"][0:SLOTS, 0:SLOTS])
                    ins.then_inc(sem["x_turned"], 1)
                for n in range(UP):
                    pe.wait_ge(up_in[n], (i + 1) * 16)
                    for s in range(4):
                        k = 4 * n + s
                        if k % (KT // 2) == 0:
                            pe.wait_ge(sem["x_scaled"], i * 2 + k // (KT // 2) + 1)
                        cols = w_u[:, n, s, :].rearrange("p (a c f) -> p a c f", a=2, c=2)
                        for c in range(2):
                            ins = pe.matmul(ps[64 * c:64 * c + 64, 2, :].rearrange("p (a f) -> p a f", a=2),
                                            x_T[:, k, :], cols[:, :, c, :], start=(k == 0), stop=(k == KT - 1))
                            if c == 0 and k == KT - 1:
                                ins.then_inc(sem["up_done"], 1)
                    ins.then_inc(sem["up_used"], 1)
                pe.wait_ge(sem["hidden"], i + 1)
                for c in range(2):
                    ins = pe.transpose(ps[:, 3, c * P:(c + 1) * P], hid[:, c * P:(c + 1) * P], C["ident"][:])
                ins.then_inc(sem["hid_turned"], 1)
                pe.wait_ge(sem["hid_kept"], i + 1)
                if not first:
                    pe.wait_ge(sem["y_kept_v"], i)
                    pe.wait_ge(sem["y_kept_s"], i)
                for n in range(DOWN):
                    pe.wait_ge(down_in[n], (i + 1) * 16)
                    for s in range(2):
                        f = 2 * n + s
                        for b in range(2):
                            for c in range(2):
                                ins = pe.matmul(ps[64 * c:64 * c + 64, 4 + b, :], hid_T[:, f % 2, f // 2, :],
                                                w_d[:, n, s, (2 * c + b) * BANK:(2 * c + b + 1) * BANK],
                                                start=(f == 0), stop=(f == FT - 1))
                    ins.then_inc(sem["down_used"], 1)
            turns(pe, turn)

        @block.scalar
        def _(act):
            def turn(i, expert, row, first):
                act.wait_ge(sem["up_used"], (i + 1) * UP)
                act.activation(sig[:], ps[:, 2, 0:F // 2], ACT.Sigmoid).then_inc(sem["sigmoid"], 1)
                act.wait_ge(sem["down_used"], (i + 1) * DOWN)
                if not first:
                    act.wait_ge(sem["stored"], i * 32)
                signal(act, act.activation(y[:, 1, :], ps[:, 5, :], ACT.Copy), sem["y_kept_s"], i + 1)
                act.wait_ge(sem["y_kept_v"], i + 1)
                for c in range(2):
                    act.dma_start(y_dram[ds(row, SLOTS), c * 1024:(c + 1) * 1024],
                                  y[64 * c:64 * c + 64, :, :].rearrange("p b n -> p (b n)")
                                  ).then_inc(sem["stored"], 16)
            turns(act, turn)
            n_items = act.value_load(R["n_items"][0:1, 0:1], min_val=0, max_val=ITEMS)
            wait_apart(act, sem["stored"], (n_items + E) * 32)

        @block.vector
        def _(v):
            v.wait_ge(sem["gain_in"], 16)

            def turn(i, expert, row, first):
                for b in range(2):
                    v.wait_ge(sem["x_turned"], i * 2 + b + 1)
                    k = slice(b * KT // 2, (b + 1) * KT // 2)
                    v.tensor_tensor(x_T[:, k, :], ps[:, b, :].rearrange("p (k s) -> p k s", s=SLOTS),
                                    g[:, k].unsqueeze(2).to_broadcast([P, KT // 2, SLOTS]),
                                    ALU.mult).then_inc(sem["x_scaled"], 1)
                v.wait_ge(sem["sigmoid"], i + 1)
                signal(v, v.tensor_tensor(hid[:], sig[:], ps[:, 2, 0:F // 2], ALU.mult), sem["gated"], i + 1)
                v.tensor_tensor(hid[:], hid[:], ps[:, 2, F // 2:F], ALU.mult).then_inc(sem["hidden"], 1)
                v.wait_ge(sem["hid_turned"], i + 1)
                v.tensor_copy(hid_T[:].rearrange("p a c s -> p (a c s)"), ps[:, 3, 0:4 * SLOTS]
                              ).then_inc(sem["hid_kept"], 1)
                v.wait_ge(sem["down_used"], (i + 1) * DOWN)
                if not first:
                    v.wait_ge(sem["stored"], i * 32)
                v.tensor_copy(y[:, 0, :], ps[:, 4, :]).then_inc(sem["y_kept_v"], 1)
            turns(v, turn)


def combine(nc, R, y_dram, x_rows):
    NT, D = x_rows.shape[1], x_rows.shape[2]
    with Stage(nc, "combine") as st:
        y = st.sb("y", [P, 4, D])
        landed = [st.sem(f"landed{n}") for n in range(4)]
        added = st.sem("added")
        block = st.block()

        @block.gpsimd
        def _(pool):
            for i in range(2 * NT):
                t, n = i // 2, i % 2
                if i >= 4:
                    pool.wait_ge(added, i - 3)
                pool.indirect_dma_start(out=y[:, i % 4, :], out_offset=None, in_=y_dram,
                                        in_offset=bass.IndirectOffsetOnAxis(ap=R["slot"][:, n, t:t + 1], axis=0)
                                        ).then_inc(landed[i % 4], 16)

        @block.vector
        def _(v):
            for i in range(2 * NT):
                t, n = i // 2, i % 2
                v.wait_ge(landed[i % 4], 16 * (i // 4 + 1))
                signal(v, v.scalar_tensor_tensor(x_rows[:, t, :], y[:, i % 4, :], R["weight"][:, n, t:t + 1],
                                                 x_rows[:, t, :], ALU.mult, ALU.add), added, i + 1)


def layer_embedding(nc, C, p, ple_proj, ple_gate, ple_norm_g, x_rows, x_T, out):
    NT, D, PD = x_rows.shape[1], x_rows.shape[2], p.shape[1]
    KP = PD // P
    with ExitStack() as keep:
        emb = keep.enter_context(nc.sbuf_tensor("embedding", [P, NT, D], F32))
        p_T = keep.enter_context(nc.sbuf_tensor("p_T", [P, KP, 512], F32))
        with Stage(nc, "p_turn") as st:
            rows = st.sb("rows", [P, NT, PD])
            ps = st.psum()
            landed, turned, kept = st.sem("landed"), st.sem("turned"), st.sem("kept")
            block = st.block()

            @block.sync
            def _(sp):
                sp.dma_start(rows[:], p.rearrange("(t q) n -> q t n", q=P)).then_inc(landed, 16)

            @block.tensor
            def _(pe):
                pe.wait_ge(landed, 16)
                for k in range(KP):
                    for t in range(NT):
                        ins = pe.transpose(ps[:, k, t * P:(t + 1) * P], rows[:, t, k * P:(k + 1) * P], C["ident"][:])
                    ins.then_inc(turned, 1)

            @block.vector
            def _(v):
                for k in range(KP):
                    v.wait_ge(turned, k + 1)
                    v.tensor_copy(p_T[:, k, :], ps[:, k, :]).then_inc(kept, 1)

        cols = lambda half, b: slice(half * 1024 + (b % 2) * BANK, half * 1024 + (b % 2 + 1) * BANK)

        def keep_vector(v, half, b, ps, extra, done):
            v.tensor_copy(emb[:, b // 2, cols(half, b)], ps[:, b, :]).then_inc(done, 1)

        def keep_scalar(act, half, b, ps, extra, done):
            act.activation(emb[:, b // 2, cols(half, b)], ps[:, b, :], ACT.Copy).then_inc(done, 1)

        project_rows(nc, "embed", p_T, ple_proj, D // 1024, keep_vector, keep_scalar)

        def setup(st):
            extra = {n: st.sem(n) for n in ("gate", "gated", "g_in", "squared", "inverse", "rooted", "stored",
                                            "steps")}
            extra["sig"] = st.sb("sig", [P, 2, BANK])
            extra["ss"] = st.sb("ss", [P, 2, NT])
            extra["gain_rows"] = st.sb("gain_rows", [P, D])
            extra["square"] = st.sb("square", [P, D])
            return extra

        def sync(sp, X):
            sp.dma_start(X["gain_rows"][:], ple_norm_g.rearrange("(o n) -> o n", o=1).to_broadcast([P, D])
                         ).then_inc(X["g_in"], 16)

        def vector(v, half, b, ps, X, done):
            i = half * 8 + b
            v.wait_ge(X["gate"], i + 1)
            v.tensor_tensor(emb[:, b // 2, cols(half, b)], emb[:, b // 2, cols(half, b)], X["sig"][:, i % 2, :],
                            ALU.mult).then_inc(done, 1)

        def finish_vector(v, X, taken_v, taken_s):
            v.wait_ge(X["squared"], NT)
            do = Chain(v, X["steps"])
            do(v.tensor_scalar(X["ss"][:, 1, :], X["ss"][:, 0, :], 1.0 / D, RMS_EPS, ALU.mult, ALU.add))
            signal(v, v.reciprocal(X["ss"][:, 1, :], X["ss"][:, 1, :]), X["inverse"], 1)
            v.wait_ge(X["rooted"], 1)
            v.wait_ge(X["g_in"], 16)
            for t in range(NT):
                do(v.scalar_tensor_tensor(emb[:, t, :], emb[:, t, :], X["ss"][:, 1, t:t + 1], X["gain_rows"][:],
                                          ALU.mult, ALU.mult))
                signal(v, v.tensor_tensor(emb[:, t, :], emb[:, t, :], x_rows[:, t, :], ALU.add), X["gated"], t + 1)

        def finish_scalar(act, X, taken_v, taken_s):
            act.wait_ge(taken_v, 16)
            for t in range(NT):
                signal(act, act.activation(X["square"][:], emb[:, t, :], ACT.Square,
                                           accum_out=X["ss"][:, 0, t:t + 1]), X["squared"], t + 1)
            act.wait_ge(X["inverse"], 1)
            act.activation(X["ss"][:, 1, :], X["ss"][:, 1, :], ACT.Sqrt).then_inc(X["rooted"], 1)
            for t in range(NT):
                act.wait_ge(X["gated"], t + 1)
                act.dma_start(out[t * P:(t + 1) * P, :], emb[:, t, :]).then_inc(X["stored"], 16)
            act.wait_ge(X["stored"], 16 * NT)

        def gate_scalar(act, half, b, ps, X, taken_v):
            i = half * 8 + b
            if i >= 2:
                act.wait_ge(taken_v, i - 1)
            act.activation(X["sig"][:, i % 2, :], ps[:, b, :], ACT.Sigmoid).then_inc(X["gate"], 1)

        project_rows(nc, "gate", x_T, ple_gate, D // 1024, vector, setup=setup, sync=sync,
                     finish=(finish_vector, finish_scalar), scalar_first=gate_scalar)


def layer(nc, x, p, ln1_g, w_in, sb_q_g, sb_k_g, sb_out_g, rw_mu, rw_w0, rw_w2, rw_a0, rw_a2, rw_g2, rw_k_k,
          rw_k_a, rw_r_k, rw_ln_g, rw_ln_b, w_out, ln2_g, router_g, router_g_b, router_e, router_e_b, w_up, w_down,
          ple_proj, ple_gate, ple_norm_g, out):
    S, D = x.shape
    KT, NT = D // P, S // P
    SB = D // 2
    E = w_up.shape[0]
    max_items = (2 * S - 1) // SLOTS
    slots = (E + max_items) * SLOTS
    rows_dram = nc.dram_tensor("normed_rows", (S, D), F32, kind="Internal").ap()
    y_dram = nc.dram_tensor("expert_rows", (slots, D), F32, kind="Internal").ap()
    token_table = nc.dram_tensor("token_table", (slots, 16), I32, kind="Internal").ap()
    with ExitStack() as keep:
        C = constants(nc, keep)
        hold = lambda stack, name, shape, dt=F32: stack.enter_context(nc.sbuf_tensor(name, shape, dt))
        clear_tables(nc, token_table, y_dram, E * SLOTS)
        with ExitStack() as mixed_life:
            mixed_T = hold(mixed_life, "mixed_T", [P, KT, S])
            with ExitStack() as norm_life:
                norm_T = hold(norm_life, "norm_T", [P, KT, S])
                with ExitStack() as rows_life:
                    rows = hold(rows_life, "rows", [P, NT, D])
                    norm_transpose(nc, "norm1", C, rows, norm_T, gain=ln1_g, load=x)
                with ExitStack() as v_life:
                    v_rows = hold(v_life, "v_rows", [P, NT, SB])
                    value_projection(nc, norm_T, w_in[:, 2 * SB:3 * SB], v_rows)
                    attention(nc, C, norm_T, w_in, v_rows, sb_q_g, sb_k_g, sb_out_g, mixed_T, SB // P, SB)
                time_mix(nc, C, norm_T, w_in[:, 3 * SB:], rw_mu, rw_w0, rw_w2, rw_a0, rw_a2, rw_g2, rw_k_k, rw_k_a,
                         rw_r_k, rw_ln_g, rw_ln_b, mixed_T, SB // P, D - SB)
            x_rows = keep.enter_context(nc.sbuf_tensor("x_rows", [P, NT, D], F32, side="right"))
            output_projection(nc, mixed_T, w_out, x, x_rows)
        R = {"max_items": max_items,
             "slot": hold(keep, "slot", [P, 2, NT], I32), "weight": hold(keep, "weight", [P, 2, NT]),
             "n_items": hold(keep, "n_items", [P, 1], I32),
             "item_expert": hold(keep, "item_expert", [1, P], I32)}
        with ExitStack() as hn_life:
            hn_T = hold(hn_life, "hn_T", [P, KT, S])
            norm_transpose(nc, "norm2", C, x_rows, hn_T, gain=ln2_g, rows_dram=rows_dram)
            route(nc, C, hn_T, router_g, router_g_b, router_e, router_e_b, R, token_table, None)
        experts(nc, C, ln2_g, w_up, w_down, R, token_table, rows_dram, y_dram)
        combine(nc, R, y_dram, x_rows)
        x_T = hold(keep, "x_T", [P, KT, S])
        norm_transpose(nc, "norm3", C, x_rows, x_T)
        layer_embedding(nc, C, p, ple_proj, ple_gate, ple_norm_g, x_rows, x_T, out)


def clear_tables(nc, token_table, y_dram, further):
    (n, w), D, ZR = token_table.shape, y_dram.shape[1], 2
    n_further = n - further
    Q = n_further // 8
    with Stage(nc, "clear") as st:
        zeros = st.sb("zeros", [P, max(n // 64 * w, ZR * D)], I32)
        zeroed, stored = st.sem("zeroed"), st.sem("stored")
        block = st.block()

        @block.vector
        def _(v):
            v.memset(zeros[:], 0).then_inc(zeroed, 1)

        @block.sync
        def _(sp):
            sp.wait_ge(zeroed, 1)
            sp.dma_start(token_table.rearrange("(q r) w -> q (r w)", q=64), zeros[0:64, 0:n // 64 * w]
                         ).then_inc(stored, 16)
            rows = y_dram[further:n, :].rearrange("(q r) n -> q (r n)", r=8)
            for i in range(8 // ZR):
                sp.dma_start(rows[:, i * ZR * D:(i + 1) * ZR * D], zeros[0:Q, 0:ZR * D].bitcast(F32)
                             ).then_inc(stored, 16)
            sp.wait_ge(stored, 16 * (8 // ZR + 1))


def kernel(**inputs):
    import numpy as np
    import concourse.bacc as bacc
    from concourse.bass_utils import run_bass_kernel_spmd

    names = ["x", "p", "ln1_g", "w_in", "sb_q_g", "sb_k_g", "sb_out_g", "rw_mu", "rw_w0", "rw_w2", "rw_a0", "rw_a2",
             "rw_g2", "rw_k_k", "rw_k_a", "rw_r_k", "rw_ln_g", "rw_ln_b", "w_out", "ln2_g", "router_g", "router_g_b",
             "router_e", "router_e_b", "w_up", "w_down", "ple_proj", "ple_gate", "ple_norm_g"]
    shape = inputs["x"].shape
    nc = bacc.Bacc("TRN2", target_bir_lowering=False, num_devices=1)
    arrays, args = {}, []
    for name in names:
        a = np.ascontiguousarray(inputs[name])[0]
        if name == "p":
            a = a[0]
        if name == "rw_r_k":
            a = a.reshape(-1)
        a = np.ascontiguousarray(a)
        arrays[f"in_{name}"] = a
        args.append(nc.dram_tensor(f"in_{name}", a.shape, mybir.dt.from_np(a.dtype), kind="ExternalInput").ap())
    out = nc.dram_tensor("out", shape[1:], F32, kind="ExternalOutput").ap()
    layer(nc, *args, out)
    r = run_bass_kernel_spmd(nc, [arrays], core_ids=[0])
    return r.results[0]["out"].reshape(shape)
```

```python
from contextlib import ExitStack
import math

import concourse.bass as bass
from concourse import mybir

F32 = mybir.dt.float32
F32R = mybir.dt.float32r
I32 = mybir.dt.int32
ALU = mybir.AluOpType
ACT = mybir.ActivationFunctionType
AX_X = mybir.AxisListType.X
ds = bass.ds

P = 128
RMS_EPS = 1e-6
GN_EPS = 64e-5
CHUNK = 64
SLOTS = 64
BANK = 512


class Stage:

    def __init__(self, nc, tag):
        self.nc, self.tag, self.stack, self.sems = nc, tag, ExitStack(), []

    def __enter__(self):
        self.stack.__enter__()
        return self

    def __exit__(self, *exc):
        self.stack.__exit__(*exc)
        if exc[0] is None:
            self.nc.clear_and_free_semaphores(self.sems)
            self.nc.all_engine_barrier()

    def sb(self, name, shape, dt=F32):
        return self.stack.enter_context(self.nc.sbuf_tensor(f"{self.tag}_{name}", list(shape), dt))

    def psum(self):
        return self.stack.enter_context(self.nc.psum_tensor(f"{self.tag}_ps", [P, 8, BANK], F32))

    def sem(self, name):
        self.sems.append(self.nc.alloc_semaphore(f"{self.tag}_{name}"))
        return self.sems[-1]

    def block(self):
        return self.stack.enter_context(self.nc.Block())


class Chain:

    def __init__(self, eng, sem, base=0):
        self.eng, self.sem, self.base, self.n = eng, sem, base, 0

    def go(self, ins):
        self.n += 1
        ins.then_inc(self.sem, 1)

    def wait(self):
        self.eng.wait_ge(self.sem, self.base + self.n)

    def __call__(self, ins):
        self.go(ins)
        self.wait()


def signal(eng, ins, sem, value):
    ins.then_inc(sem, 1)
    eng.wait_ge(sem, value)


def wait_apart(eng, sem, value):
    eng.wait_ge(sem, value)
    eng.nop(nofuse=True)


def constant_tensors(nc, keep):
    def sb(name, shape, dt=F32):
        return keep.enter_context(nc.sbuf_tensor(f"const_{name}", shape, dt))

    C = {}
    for name in ("ident", "ones", "neg_ones", "later_neg", "after", "head_sum", "head_mean", "first_down",
                 "first_up"):
        C[name] = sb(name, [P, P])
    C["levels"] = sb("levels", [P, 5, P])
    C["seen"] = sb("seen", [P, 2, P])
    C["blocks"] = sb("blocks", [P, 6, P])
    C["no_carry"] = sb("no_carry", [P, 512])
    return C


def constants(nc, C, x, rows, sums, scratch, ahead):
    with Stage(nc, "const") as st:
        steps, vsteps, pool_done, squared = (st.sem(n) for n in ("pool_steps", "vector_steps", "pool_done", "squared"))
        rows_in = [st.sem(f"rows_in{t}") for t in range(rows.shape[1])]
        tmp = st.sb("tmp", [P, P])
        block = st.block()

        @block.sync
        def _(sp):
            for t in range(rows.shape[1]):
                sp.dma_start(rows[:, t, :], x[t * P:(t + 1) * P, :]).then_inc(rows_in[t], 16)
            ahead(sp)

        @block.scalar
        def _(act):
            for t in range(rows.shape[1]):
                act.wait_ge(rows_in[t], 16)
                signal(act, act.activation(scratch, rows[:, t, :], ACT.Square, accum_out=sums[:, t, :]), squared, t + 1)

        @block.gpsimd
        def _(pool):
            do = Chain(pool, steps)
            do(pool.memset(C["ident"][:], 0.0))
            do(pool.affine_select(C["ident"][:], C["ident"][:], [[-1, P]], ALU.not_equal, 1.0, base=0,
                                  channel_multiplier=1))
            for name, value in (("ones", 1.0), ("neg_ones", -1.0), ("after", 1.0), ("later_neg", -1.0),
                                ("head_sum", 0.0), ("head_mean", 0.0), ("no_carry", 1.0), ("blocks", 1.0)):
                do(pool.memset(C[name][:], value))
            do(pool.affine_select(C["after"][:], C["after"][:], [[1, P]], ALU.is_gt, 0.0, base=0,
                                  channel_multiplier=-1))
            do(pool.affine_select(C["later_neg"][:], C["later_neg"][:], [[-1, P]], ALU.is_ge, 0.0, base=0,
                                  channel_multiplier=1))
            for h in range(2):
                half = slice(64 * h, 64 * h + 64)
                do(pool.memset(C["head_sum"][half, half], 1.0))
                do(pool.memset(C["head_mean"][half, half], 1.0 / 64))
            do(pool.memset(C["no_carry"][:].rearrange("p (c t) -> p c t", t=CHUNK)[:, :, 0:1], 0.0))
            for n in range(6):
                w = 2 << n
                blk = C["blocks"][:, n, :].rearrange("p (b w) -> p b w", w=w)
                do(pool.affine_select(blk, blk, [[-w, P // w], [0, w]], ALU.is_ge, 0.0, base=0,
                                      channel_multiplier=1))
                do(pool.affine_select(blk, blk, [[w, P // w], [0, w]], ALU.is_ge, 0.0, base=w - 1,
                                      channel_multiplier=-1))
            pool.nop().then_inc(pool_done, 1)

        @block.vector
        def _(v):
            v.wait_ge(pool_done, 1)
            do = Chain(v, vsteps)
            do(v.tensor_tensor(C["seen"][:, 0, :], C["blocks"][:, 5, :], C["after"][:], ALU.mult))
            do(v.tensor_tensor(C["seen"][:, 1, :], C["seen"][:, 0, :], C["ident"][:], ALU.add))
            do(v.tensor_tensor(tmp[:], C["blocks"][:, 0, :], C["ident"][:], ALU.subtract))
            do(v.tensor_tensor(C["first_up"][:], tmp[:], C["after"][:], ALU.mult))
            do(v.tensor_tensor(C["first_down"][:], tmp[:], C["first_up"][:], ALU.subtract))
            for n in range(5):
                do(v.tensor_tensor(tmp[:], C["blocks"][:, n + 1, :], C["blocks"][:, n, :], ALU.subtract))
                do(v.tensor_tensor(C["levels"][:, n, :], tmp[:], C["after"][:], ALU.mult))


def norm_transpose(nc, tag, C, rows, sums, out_T, gain=None, rows_dram=None, ahead=None,
                   out_low=None):
    TT, D = rows.shape[1], rows.shape[2]
    KT = D // P
    with Stage(nc, tag) as st:
        normed = st.sb("normed", [P, TT, D]) if rows_dram is not None else None
        diag = st.sb("diag", [P, TT, P]) if rows_dram is None else None
        ss = st.sb("ss", [P, 3, TT])
        g = st.sb("gain", [P, KT]) if gain is not None else None
        ps = st.psum()
        gain_in, stored, inverse, rooted = (st.sem(n) for n in ("gain", "stored", "inverse", "rooted"))
        scaled, turned, vsteps = st.sem("scaled"), st.sem("turned"), st.sem("vector_steps")
        kept = st.sem("kept_vector"), st.sem("kept_scalar")
        block = st.block()

        @block.sync
        def _(sp):
            if g is not None:
                with nc.allow_non_contiguous_dma("a gain per partition"):
                    sp.dma_start(g[:], gain.rearrange("(k p) -> p k", p=P)).then_inc(gain_in, 16)
            if ahead:
                ahead(sp)
            if rows_dram is not None:
                for t in range(TT):
                    sp.wait_ge(scaled, t + 1)
                    sp.dma_start(rows_dram[t * P:(t + 1) * P, :], normed[:, t, :]).then_inc(stored, 16)
                sp.wait_ge(stored, 16 * TT)

        @block.scalar
        def _(act):
            act.wait_ge(inverse, 1)
            signal(act, act.activation(ss[:, 2, :], ss[:, 1, :], ACT.Sqrt), rooted, 1)
            if g is not None:
                act.wait_ge(gain_in, 16)
            for k in range(0 if out_low else 1, KT, 1 if out_low else 2):
                act.wait_ge(turned, k + 1)
                act.activation(out_T[:, k, :], ps[:, k % 4, :], ACT.Copy,
                               scale=g[:, k:k + 1] if g is not None else 1.0).then_inc(kept[1], 1)

        @block.vector
        def _(v):
            do = Chain(v, vsteps)
            do(v.tensor_reduce(ss[:, 0, :].unsqueeze(2), sums[:], AX_X, ALU.add))
            do(v.tensor_scalar(ss[:, 1, :], ss[:, 0, :], 1.0 / D, RMS_EPS, ALU.mult, ALU.add))
            signal(v, v.reciprocal(ss[:, 1, :], ss[:, 1, :]), inverse, 1)
            v.wait_ge(rooted, 1)
            for t in range(TT):
                source, target = (C["ident"][:], diag[:, t, :]) if normed is None else (rows[:, t, :], normed[:, t, :])
                v.tensor_scalar(target, source, ss[:, 2, t:t + 1], None, ALU.mult).then_inc(scaled, 1)
            if g is not None:
                v.wait_ge(gain_in, 16)
            for k in range(0, KT, 1 if out_low else 2):
                if out_low:
                    v.wait_ge(kept[1], k + 1)
                    high = out_T[:, k, :].bitcast(F32)
                    if g is not None:
                        ins = v.scalar_tensor_tensor(out_low[:, k, :], ps[:, k % 4, :], g[:, k:k + 1], high,
                                                     ALU.mult, ALU.subtract)
                    else:
                        ins = v.tensor_tensor(out_low[:, k, :], ps[:, k % 4, :], high, ALU.subtract)
                    ins.then_inc(kept[0], 1)
                    continue
                v.wait_ge(turned, k + 1)
                if g is not None:
                    ins = v.tensor_scalar(out_T[:, k, :], ps[:, k % 4, :], g[:, k:k + 1], None, ALU.mult)
                else:
                    ins = v.tensor_copy(out_T[:, k, :], ps[:, k % 4, :])
                ins.then_inc(kept[0], 1)

        @block.tensor
        def _(pe):
            pe.wait_ge(scaled, TT)
            for k in range(KT):
                if k >= 4 and out_low:
                    pe.wait_ge(kept[0], k - 3)
                elif k >= 4:
                    pe.wait_ge(kept[k % 2], (k - 4) // 2 + 1)
                for t in range(TT):
                    bank = ps[:, k % 4, t * P:(t + 1) * P]
                    if normed is None:
                        ins = pe.matmul(bank, rows[:, t, k * P:(k + 1) * P], diag[:, t, :], start=True, stop=True)
                    else:
                        ins = pe.transpose(bank, normed[:, t, k * P:(k + 1) * P], C["ident"][:])
                ins.then_inc(turned, 1)


class Ring:
    SLOT, COUNT = 2, 4

    def __init__(self, nc, keep, tag, weights, first=0):
        self.first = first
        self.tensor = keep.enter_context(nc.sbuf_tensor(f"{tag}_weights", [P, self.COUNT, self.SLOT, 1024], F32))
        self.landed = [nc.alloc_semaphore(f"{tag}_landed{r}") for r in range(self.COUNT)]
        self.src = weights.rearrange("(k p) n -> p k n", p=P)
        self.per_half = self.src.shape[1] // self.SLOT
        self.loads = [(half, n) for half in range(weights.shape[1] // 1024) for n in range(self.per_half)]
        self.started = 0

    def load(self, sp, i):
        half, n = self.loads[i]
        n, r = (n + self.first) % self.per_half, i % self.COUNT
        sp.dma_start(self.tensor[:, r, :, :], self.src[:, n * self.SLOT:(n + 1) * self.SLOT,
                                                       half * 1024:(half + 1) * 1024]).then_inc(self.landed[r], 16)

    def ahead(self, sp):
        self.started = min(self.COUNT, len(self.loads))
        for i in range(self.started):
            self.load(sp, i)


def project_rows(nc, tag, act_T, ring, vector, scalar=None, setup=None, sync=None, finish=None, scalar_first=None,
                 pool=None, ahead=None, sync_end=None, split=False, parts=None):
    KT = ring.src.shape[1]
    SLOT, RING, LOADS, loads, landed = ring.SLOT, ring.COUNT, ring.per_half, ring.loads, ring.landed
    halves = len(loads) // LOADS
    TILES = halves * KT
    AHEAD = 2
    with Stage(nc, tag) as st:
        if split:
            cut_act = parts is None
            act_h, act_l = parts or (st.sb("act_high", [P, KT, 4 * P], F32R), st.sb("act_low", [P, KT, 4 * P], F32R))
            w_h, w_l = st.sb("w_high", [P, 2, 1024], F32R), st.sb("w_low", [P, 2, 1024], F32R)
        ps = st.psum()
        used, product, taken_v, taken_s = (st.sem(n) for n in ("used", "product", "taken_v", "taken_s"))
        act_high, act_low, high, low, multiplied = (st.sem(n) for n in ("act_high", "act_low", "high", "low",
                                                                        "multiplied"))
        extra = setup(st) if setup else {}
        block = st.block()
        n_s = 4 if scalar else 0

        @block.sync
        def _(sp):
            for i in range(ring.started, len(loads)):
                if i == RING and sync:
                    sync(sp, extra)
                if i >= RING:
                    before, m = loads[i - RING]
                    if split:
                        sp.wait_ge(low, (i - RING + 1) * SLOT)
                    elif m == LOADS - 1:
                        sp.wait_ge(product, 8 * (before + 1))
                    else:
                        sp.wait_ge(used, before * (LOADS - 1) + m + 1)
                ring.load(sp, i)
            if ahead:
                ahead(sp)
            if sync_end:
                sync_end(sp, extra)

        @block.tensor
        def _(pe):
            for i, (half, n) in enumerate(loads):
                r = i % RING
                if not split:
                    pe.wait_ge(landed[r], 16 * (i // RING + 1))
                for s in range(SLOT):
                    k = n * SLOT + s
                    j = half * KT + k
                    if split:
                        pe.wait_ge(low, j + 1)
                        if cut_act and half == 0:
                            pe.wait_ge(act_low, k + 1)
                    for t in range(4):
                        for c in range(2):
                            b = 2 * t + c
                            if half and k == 0:
                                if n_s:
                                    pe.wait_ge((taken_v, taken_s)[b % 2], (half - 1) * 4 + b // 2 + 1)
                                else:
                                    pe.wait_ge(taken_v, (half - 1) * 8 + b + 1)
                            toks, cols = slice(t * P, (t + 1) * P), slice(c * BANK, (c + 1) * BANK)
                            if split:
                                pairs = [(act_h[:, k, toks], w_h[:, j % 2, cols]),
                                         (act_h[:, k, toks], w_l[:, j % 2, cols]),
                                         (act_l[:, k, toks], w_h[:, j % 2, cols])]
                            else:
                                pairs = [(act_T[:, k, toks], ring.tensor[:, r, s, cols])]
                            for m, (x, w) in enumerate(pairs):
                                ins = pe.matmul(ps[:, b, :], x, w, start=(k == 0 and m == 0),
                                                stop=(k == KT - 1 and m == len(pairs) - 1))
                            if k == KT - 1:
                                ins.then_inc(product, 1)
                    if split and k < KT - 1:
                        ins.then_inc(multiplied, 1)
                if not split and n < LOADS - 1:
                    ins.then_inc(used, 1)

        if pool:
            @block.gpsimd
            def _(eng):
                pool(eng, extra)

        def cut(eng, first, last, make_high):
            for j in range(first, min(last, TILES)):
                half, k = divmod(j, KT)
                i, s = divmod(j, SLOT)
                if make_high:
                    eng.wait_ge(landed[i % RING], 16 * (i // RING + 1))
                    if j >= 2:
                        before, m = divmod(j - 2, KT)
                        if m == KT - 1:
                            eng.wait_ge(product, 8 * (before + 1))
                        else:
                            eng.wait_ge(multiplied, before * (KT - 1) + m + 1)
                    if cut_act and half == 0:
                        eng.activation(act_h[:, k, :], act_T(eng, k, extra), ACT.Copy).then_inc(act_high, 1)
                    eng.activation(w_h[:, j % 2, :], ring.tensor[:, i % RING, s, :], ACT.Copy).then_inc(high, 1)
                else:
                    if cut_act and half == 0:
                        eng.wait_ge(act_high, k + 1)
                        eng.tensor_tensor(act_l[:, k, :], act_T(eng, k, extra), act_h[:, k, :].bitcast(F32),
                                          ALU.subtract).then_inc(act_low, 1)
                    eng.wait_ge(high, j + 1)
                    eng.tensor_tensor(w_l[:, j % 2, :], ring.tensor[:, i % RING, s, :],
                                      w_h[:, j % 2, :].bitcast(F32), ALU.subtract).then_inc(low, 1)

        @block.vector
        def _(v):
            for half in range(halves):
                if split:
                    cut(v, half * KT + (AHEAD if half else 0), (half + 1) * KT + AHEAD, False)
                for b in range(0, 8, 2 if scalar else 1):
                    v.wait_ge(product, half * 8 + b + 1)
                    vector(v, half, b, ps, extra, taken_v)
            if finish:
                finish[0](v, extra, taken_v, taken_s)

        @block.scalar
        def _(act):
            for half in range(halves):
                if split:
                    cut(act, half * KT + (AHEAD if half else 0), (half + 1) * KT + AHEAD, True)
                for b in range(8):
                    if scalar_first or (scalar and b % 2):
                        act.wait_ge(product, half * 8 + b + 1)
                        (scalar_first or scalar)(act, half, b, ps, extra, taken_v if scalar_first else taken_s)
            if finish:
                finish[1](act, extra, taken_v, taken_s)


def value_projection(nc, norm_parts, ring, v_rows, token_table, y_dram, further, ahead):
    (n, w), D, ZR = token_table.shape, y_dram.shape[1], 2
    Q = (n - further) // 8

    def setup(st):
        return {"zeros": st.sb("zeros", [P, max(n // 64 * w, ZR * D)], I32), "zeroed": st.sem("zeroed"),
                "stored": st.sem("stored")}

    def pool(eng, X):
        signal(eng, eng.memset(X["zeros"][:], 0), X["zeroed"], 1)
        eng.dma_start(token_table.rearrange("(q r) w -> q (r w)", q=64), X["zeros"][0:64, 0:n // 64 * w]
                      ).then_inc(X["stored"], 16)
        rows = y_dram[further:n, :].rearrange("(q r) n -> q (r n)", r=8)
        for i in range(8 // ZR):
            eng.dma_start(rows[:, i * ZR * D:(i + 1) * ZR * D], X["zeros"][0:Q, 0:ZR * D].bitcast(F32)
                          ).then_inc(X["stored"], 16)
        eng.wait_ge(X["stored"], 16 * (8 // ZR + 1))

    def vector(v, half, b, ps, extra, done):
        v.tensor_copy(v_rows[:, b // 2, (b % 2) * BANK:(b % 2 + 1) * BANK], ps[:, b, :]).then_inc(done, 1)

    def scalar(act, half, b, ps, extra, done):
        act.activation(v_rows[:, b // 2, (b % 2) * BANK:(b % 2 + 1) * BANK], ps[:, b, :], ACT.Copy).then_inc(done, 1)

    project_rows(nc, "values", None, ring, vector, scalar, setup=setup, pool=pool, ahead=ahead, split=True,
                 parts=norm_parts)


class HeadWeights:

    def __init__(self, nc, keep, w_in, KT, width):
        self.tensor = keep.enter_context(nc.sbuf_tensor("attn_w_qk", [P, 2, KT, P], F32))
        self.landed = [nc.alloc_semaphore(f"attn_w{n}_in") for n in "qk"]
        self.src, self.width = w_in.rearrange("(k p) n -> p k n", p=P), width

    def load(self, sp, h, n):
        sp.dma_start(self.tensor[:, n, :, :], self.src[:, :, ds(h * P + n * self.width, P)]
                     ).then_inc(self.landed[n], 16)

    def ahead(self, sp):
        for n in range(2):
            self.load(sp, 0, n)


def attention(nc, C, norm_parts, weights, v_rows, q_gain, k_gain, out_gain, mixed_dram, heads, ahead):
    norm_h, norm_l = norm_parts
    KT, S = norm_h.shape[1], norm_h.shape[2]
    CUT, CUTS = 4, 4
    GQ = KT // CUT
    HD, NB = P, S // P
    Q, K, OUT = range(3)
    S_STEPS = 8
    EARLY = GQ // 2
    with Stage(nc, "attn") as st:
        mixed = st.sb("mixed", [P, heads, S])
        gains = st.sb("gains", [P, 3])
        eps = st.sb("eps", [P, 1])
        square = st.sb("square", [P, 2, S])
        root = square
        place = (0, 1, 0)
        qk_T = st.sb("qk_T", [P, 2, S])
        log1p = st.sb("log1p", [P, NB, S])
        softplus = st.sb("softplus", [P, NB, S])
        weight = log1p
        w_h, w_l = st.sb("w_high", [P, CUTS, CUT, HD], F32R), st.sb("w_low", [P, CUTS, CUT, HD], F32R)
        v_head = st.sb("v_head", [P, NB, HD])
        ps = st.psum()
        BQ, BO, BN, BZ = 0, 2, 3, 4
        sem = {n: st.sem(n) for n in (
            "gain_in", "eps_set", "scored", "soft_in", "soft", "masked", "exponent", "weighted", "weight_ready",
            "v_ready", "output", "gain_scaled", "s_steps", "high", "low", "multiplied", "stored")}
        w_qk, w_in_sem = weights.tensor, weights.landed
        projected = [st.sem(n) for n in ("q_projected", "k_projected")]
        squared, summed, logged, rooted, normed = ([st.sem(f"{x}_{n}") for x in ("q", "k", "out")]
                                                   for n in ("squared", "summed", "logged", "rooted", "normed"))
        block = st.block()

        @block.sync
        def _(sp):
            with nc.allow_non_contiguous_dma("a gain per partition"):
                for n, g in enumerate((q_gain, k_gain, out_gain)):
                    sp.dma_start(gains[:, n:n + 1], g.rearrange("(p o) -> p o", o=1)).then_inc(sem["gain_in"], 16)

            def load(h, n):
                wait_apart(sp, sem["low"], (2 * h - 1 + n) * GQ)
                weights.load(sp, h, n)

            def store(h):
                wait_apart(sp, normed[OUT], h + 1)
                sp.dma_start(mixed_dram[:, ds(h, 1), :], mixed[:, ds(h, 1), :]).then_inc(sem["stored"], 16)

            load(1, Q)
            load(1, K)
            load(2, Q)
            with sp.Fori(0, heads - 3) as h:
                load(h + 2, K)
                store(h)
                load(h + 3, Q)
            load(heads - 1, K)
            ahead(sp)
            store(heads - 3)
            store(heads - 2)
            store(heads - 1)
            sp.wait_ge(sem["stored"], 16 * heads)

        @block.tensor
        def _(pe):
            def project(h, n, first, last):
                if first == 0 and (not isinstance(h, int) or h):
                    pe.wait_ge(normed[n], h)
                for j in range(first, last):
                    pe.wait_ge(sem["low"], (2 * h + n) * GQ + j + 1)
                    for s in range(CUT):
                        k = CUT * j + s
                        for w, x in ((w_h, norm_h), (w_l, norm_h), (w_h, norm_l)):
                            ins = pe.matmul(ps[:, BQ + n, :], w[:, j % CUTS, s, :], x[:, k, :],
                                            start=(k == 0 and w is w_h and x is norm_h),
                                            stop=(k == KT - 1 and x is norm_l))
                    ins.then_inc(projected[n] if j == GQ - 1 else sem["multiplied"], 1)

            def square_sum(h, n, bank):
                pe.wait_ge(squared[n], h + 1)
                pe.matmul(ps[:, bank, :], C["ones"][:], square[:, place[n], :], start=True, stop=True).then_inc(summed[n], 1)

            def scores(h):
                pe.wait_ge(normed[Q], h + 1)
                pe.wait_ge(normed[K], h + 1)
                for b in range(NB):
                    pe.matmul(ps[:, BZ + b, b * P:], qk_T[:, 1, b * P:(b + 1) * P], qk_T[:, 0, b * P:],
                              start=True, stop=True).then_inc(sem["scored"], 1)

            def exponents(h):
                pe.wait_ge(sem["masked"], NB * h + NB)
                for b in range(NB):
                    for j in range(b, NB):
                        ins = pe.matmul(ps[:, BZ + b, j * P:], C["later_neg" if j == b else "neg_ones"][:],
                                        softplus[:, j, j * P:], start=False, stop=(j == NB - 1),
                                        skip_group_check=True)
                    ins.then_inc(sem["exponent"], 1)

            def output(h):
                pe.wait_ge(sem["v_ready"], h + 1)
                for b in range(NB):
                    pe.wait_ge(sem["weight_ready"], NB * h + b + 1)
                    ins = pe.matmul(ps[:, BO, b * P:], v_head[:, b, :], weight[:, b, b * P:], start=(b == 0),
                                    stop=(b == NB - 1))
                ins.then_inc(sem["output"], 1)

            def head(h, behind):
                scores(h)
                if behind:
                    project(h + 1, Q, EARLY, GQ)
                    project(h + 1, K, 0, EARLY)
                exponents(h)
                if behind:
                    square_sum(h + 1, Q, BN)
                    project(h + 1, K, EARLY, GQ)
                output(h)
                if behind:
                    pe.wait_ge(logged[Q], h + 2)
                    square_sum(h + 1, K, BN)
                if behind > 1:
                    project(h + 2, Q, 0, 1)
                if behind:
                    pe.wait_ge(logged[K], h + 2)
                square_sum(h, OUT, BN)
                if behind > 1:
                    project(h + 2, Q, 1, EARLY)

            project(0, Q, 0, GQ)
            square_sum(0, Q, BN)
            project(0, K, 0, GQ)
            pe.wait_ge(logged[Q], 1)
            square_sum(0, K, BN)
            project(1, Q, 0, EARLY)
            with pe.Fori(0, heads - 2) as h:
                head(h, 2)
            head(heads - 2, 1)
            head(heads - 1, 0)

        @block.scalar
        def _(act):
            def take_square(h, n):
                act.wait_ge(projected[n], h + 1)
                act.activation(square[:, n, :], ps[:, BQ + n, :], ACT.Square).then_inc(squared[n], 1)

            def take_root(h, n, bank):
                act.wait_ge(summed[n], h + 1)
                signal(act, act.activation(root[:, place[n], :], ps[:, bank, :], ACT.Ln, scale=1.0 / HD, bias=eps[:]),
                       logged[n], h + 1)
                act.activation(root[:, place[n], :], root[:, place[n], :], ACT.Exp, scale=-0.5).then_inc(rooted[n], 1)

            def head(h, last):
                do = Chain(act, sem["s_steps"], h * S_STEPS)
                for b in range(NB):
                    act.wait_ge(sem["scored"], NB * h + b + 1)
                    do.go(act.activation(log1p[:, b, b * P:], ps[:, BZ + b, b * P:], ACT.Abs))
                do.wait()
                for b in range(NB):
                    do.go(act.activation(log1p[:, b, b * P:], log1p[:, b, b * P:], ACT.Exp, scale=-1.0))
                do.wait()
                for b in range(NB):
                    act.activation(log1p[:, b, b * P:], log1p[:, b, b * P:], ACT.Ln, bias=1.0
                                   ).then_inc(sem["soft_in"], 1)
                assert do.n == S_STEPS
                act.activation(v_head[:], v_rows[:, :, ds(h * HD, HD)], ACT.Copy).then_inc(sem["v_ready"], 1)
                if not last:
                    act.wait_ge(sem["exponent"], NB * h + 1)
                    take_square(h + 1, Q)
                for b in range(NB):
                    act.wait_ge(sem["exponent"], NB * h + b + 1)
                    act.activation(weight[:, b, b * P:], ps[:, BZ + b, b * P:], ACT.Exp).then_inc(sem["weighted"], 1)
                if not last:
                    take_root(h + 1, Q, BN)
                    take_square(h + 1, K)
                act.wait_ge(sem["output"], h + 1)
                if not last:
                    act.wait_ge(normed[Q], h + 2)
                act.activation(square[:, place[OUT], :], ps[:, BO, :], ACT.Square).then_inc(squared[OUT], 1)
                if not last:
                    take_root(h + 1, K, BN)
                take_root(h, OUT, BN)

            act.wait_ge(sem["eps_set"], 1)
            take_square(0, Q)
            take_root(0, Q, BN)
            take_square(0, K)
            take_root(0, K, BN)
            with act.Fori(0, heads - 1) as h:
                head(h, False)
            head(heads - 1, True)

        @block.vector
        def _(v):
            def normalise(h, n):
                v.wait_ge(rooted[n], h + 1)
                v.scalar_tensor_tensor(qk_T[:, n, :], ps[:, BQ + n, :], gains[:, n:n + 1], root[:, n, :],
                                       ALU.mult, ALU.mult).then_inc(normed[n], 1)

            def cut_low(h, n, first, last):
                for j in range(first, last):
                    v.wait_ge(sem["high"], (2 * h + n) * GQ + j + 1)
                    v.tensor_tensor(w_l[:, j % CUTS, :, :], w_qk[:, n, CUT * j:CUT * j + CUT, :],
                                    w_h[:, j % CUTS, :, :].bitcast(F32), ALU.subtract).then_inc(sem["low"], 1)

            def head(h, behind):
                if behind:
                    cut_low(h + 1, Q, EARLY, GQ)
                    cut_low(h + 1, K, 0, EARLY)
                for b in range(NB):
                    v.wait_ge(sem["soft_in"], NB * h + b + 1)
                    v.scalar_tensor_tensor(softplus[:, b, b * P:], ps[:, BZ + b, b * P:], 0.0,
                                           log1p[:, b, b * P:], ALU.max, ALU.add).then_inc(sem["soft"], 1)
                if behind:
                    cut_low(h + 1, K, EARLY, GQ)
                    normalise(h + 1, Q)
                    if behind > 1:
                        cut_low(h + 2, Q, 0, EARLY)
                    normalise(h + 1, K)
                v.wait_ge(rooted[OUT], h + 1)
                v.scalar_tensor_tensor(mixed[:, ds(h, 1), :].rearrange("p o s -> p (o s)"), ps[:, BO, :],
                                       gains[:, 2:3], root[:, place[OUT], :], ALU.mult, ALU.mult).then_inc(normed[OUT], 1)

            v.memset(eps[:], RMS_EPS).then_inc(sem["eps_set"], 1)
            v.wait_ge(sem["gain_in"], 48)
            signal(v, v.tensor_scalar(gains[:, 0:1], gains[:, 0:1], 1.0 / math.sqrt(HD), None, ALU.mult),
                   sem["gain_scaled"], 1)
            cut_low(0, Q, 0, GQ)
            cut_low(0, K, 0, 1)
            normalise(0, Q)
            cut_low(0, K, 1, GQ)
            cut_low(1, Q, 0, EARLY)
            normalise(0, K)
            with v.Fori(0, heads - 2) as h:
                head(h, 2)
            head(heads - 2, 1)
            head(heads - 1, 0)

        @block.gpsimd
        def _(pool):
            def cut_high(h, n, first, last):
                for j in range(first, last):
                    if j == 0:
                        wait_apart(pool, w_in_sem[n], 16 * (h + 1))
                    if j == GQ - 1:
                        if n or not isinstance(h, int) or h:
                            wait_apart(pool, projected[1 - n], h + n)
                    elif n or not isinstance(h, int) or h:
                        wait_apart(pool, sem["multiplied"], (2 * h + n - 1) * (GQ - 1) + j + 1)
                    pool.tensor_copy(w_h[:, j % CUTS, :, :], w_qk[:, n, CUT * j:CUT * j + CUT, :]
                                     ).then_inc(sem["high"], 1)

            def select(h, source, tile, done):
                for b in range(NB):
                    wait_apart(pool, sem[source], NB * h + b + 1)
                    own = tile[:, b, b * P:(b + 1) * P]
                    pool.affine_select(own, own, [[1, P]], ALU.is_gt, 0.0, base=0,
                                       channel_multiplier=-1).then_inc(sem[done], 1)

            def head(h, behind):
                if behind:
                    cut_high(h + 1, Q, EARLY, GQ)
                    cut_high(h + 1, K, 0, EARLY)
                select(h, "soft", softplus, "masked")
                if behind:
                    cut_high(h + 1, K, EARLY, GQ)
                if behind > 1:
                    cut_high(h + 2, Q, 0, 1)
                select(h, "weighted", weight, "weight_ready")
                if behind > 1:
                    cut_high(h + 2, Q, 1, EARLY)

            cut_high(0, Q, 0, GQ)
            cut_high(0, K, 0, GQ)
            cut_high(1, Q, 0, EARLY)
            with pool.Fori(0, heads - 2) as h:
                head(h, 2)
            head(heads - 2, 1)
            head(heads - 1, 0)


class MixWeights:
    COUNT = 3

    def __init__(self, nc, keep, w_u, mu, w0, a0, k_k, k_a, r_k, ln_g, ln_b, width, GB):
        def sb(name, shape):
            return keep.enter_context(nc.sbuf_tensor(f"mix_{name}", shape, F32))
        self.nc, self.src = nc, w_u.rearrange("(k p) n -> p k n", p=P)
        self.HALF = self.src.shape[1] // 2
        self.tensor = sb("w_rkv", [P, self.COUNT, self.HALF, P])
        self.landed = [nc.alloc_semaphore(f"mix_w_landed{n}") for n in range(self.COUNT)]
        self.vectors = (mu[0:width], mu[width:2 * width], mu[2 * width:3 * width], w0, a0, k_k, k_a, r_k, ln_g, ln_b)
        self.params = sb("params", [P, len(self.vectors), width // P])
        self.lora_mu = sb("lora_mu", [P, 3])
        self.mu, self.GB, self.width = mu, GB, width
        self.mu_in, self.par_in = (nc.alloc_semaphore(f"mix_{n}") for n in ("lora_mu_in", "par_in"))

    def columns(self, n, lora):
        return self.GB if lora and n == 2 else P

    def load(self, sp, turn, i, lora=False):
        n, m, cols = i // 2, i % 2, self.columns(i // 2, lora)
        start = 3 * self.width + n * P if lora else (turn - 1) * P + n * self.width
        sp.dma_start(self.tensor[:, i % self.COUNT, :, 0:cols],
                     self.src[:, m * self.HALF:(m + 1) * self.HALF, ds(start, cols)]
                     ).then_inc(self.landed[i % self.COUNT], 16)

    def landed_value(self, turn, i):
        return 16 * (turn * (6 // self.COUNT) + i // self.COUNT + 1)

    def ahead(self, sp):
        lo = 3 * self.width
        for i in range(self.COUNT):
            self.load(sp, 0, i, lora=True)
        with self.nc.allow_non_contiguous_dma("a parameter per partition"):
            for n, m in ((0, P), (1, P), (2, self.GB)):
                sp.dma_start(self.lora_mu[0:m, n:n + 1],
                             self.mu[lo + n * P:lo + n * P + m].rearrange("(p o) -> p o", o=1)
                             ).then_inc(self.mu_in, 16)
            for n, a in enumerate(self.vectors):
                sp.dma_start(self.params[:, n, :], a.rearrange("(g p) -> p g", p=P)).then_inc(self.par_in, 16)


def time_mix(nc, C, norm_parts, weights, w2, a2, g2, mixed_T, width):
    norm_h, norm_l = norm_parts
    KT, S = norm_h.shape[1], norm_h.shape[2]
    CUT, CUTS = 4, 2
    GN = KT // CUT
    PAIRS, NT, NC = width // P, S // P, S // CHUNK
    LW = w2.shape[0]
    GA = P
    GB = g2.shape[0] - P
    N_PAR = 10
    MU_R, MU_K, MU_V, W0, A0, KK, KA, RK, LG, LB = range(N_PAR)
    PROJ = 7
    with Stage(nc, "mix") as st:
        params, lora_mu = weights.params, weights.lora_mu
        w_h, w_l = st.sb("w_high", [P, CUTS, CUT, P], F32R), st.sb("w_low", [P, CUTS, CUT, P], F32R)
        w2_s = st.sb("w2", [P, 2, P])
        g2_s = st.sb("g2", [P, 2, P])
        par = st.sb("par", [P, N_PAR])
        par_end = st.sb("par_end", [P, 2])
        eps = st.sb("eps", [P, 2])
        raw = st.sb("raw", [P, 3, S + 1])
        step = st.sb("step", [P, S])
        lora = st.sb("lora", [P, 3, S])
        rkv = st.sb("rkv", [P, 3, S])
        a_t, logw, kk, kmix, t1, bonus = (st.sb(n, [P, S]) for n in ("a", "logw", "kk", "kmix", "t1", "bonus"))
        ar = st.sb("ar", [P, NT, 2, P])
        b_in, k_in = st.sb("b_in", [P, 2, S]), st.sb("k_in", [P, 2, S])
        e_end, b_end, k_end = t1, logw, a_t
        d_end = st.sb("d_end", [P, NC])
        rows = st.sb("rows", [P, 3, NT, P])
        from_b = st.sb("from_b", [P, 2, NT, 2, P])
        from_k = st.sb("from_k", [P, 2, NT, 2, P])
        inv = st.sb("inv", [P, 2, NT, P])
        inv_T = st.sb("inv_T", [P, 2, NT, P])
        join = st.sb("join", [P, 2, NT, P])
        joined = st.sb("joined", [P, 2, NT, P])
        cum, t2, e_in, e_out, y, gate_s = (x[:, h, :, :].rearrange("p t s -> p (t s)") for x in (inv, joined, join)
                                           for h in range(2))
        lv = st.sb("lv", [P, NT, P])
        y_scale = lv[:].rearrange("p t f -> p (t f)")
        x_rows = st.sb("x_rows", [P, P])
        u_rows = st.sb("u_rows", [P, NT, P])
        state = st.sb("state", [P, NC, P])
        ps = st.psum()
        names = ("high", "low", "multiplied", "w2_in", "g2_in", "zeroed",
                 "lora_raw", "lora_step", "lora_ready", "raw_ready", "shift_steps",
                 "par_ready", "lora_wa", "wa_ready", "kk_ready", "kk_square", "kk_sum", "kk_log", "kk_root", "decays",
                 "exps", "ends_can_start", "ends", "factors", "turned", "rows_kept", "gram", "gram_kept",
                 "first_gram", "inv_start", "join_ready", "join_product", "joined_kept", "level", "level_kept",
                 "lv_product", "lv_kept", "x_product", "x_kept", "u_product", "u_kept", "s_product", "s_kept",
                 "y_product", "y_kept", "mean", "centred", "y_square", "var", "var_log", "var_root", "bonus_in",
                 "bonus_sum", "bonus_steps", "gate", "gate_kept", "v_steps", "end_steps", "inv_kept", "s_half",
                 "pool_steps", "y_ready", "mixed")
        sem = {n: st.sem(n) for n in names}
        block = st.block()
        half = lambda c: slice((c % 2) * CHUNK, (c % 2) * CHUNK + CHUNK)
        head = lambda h: slice(64 * h, 64 * h + 64)
        tiles = lambda x: x.rearrange("p (t s) -> p t s", s=P)
        chunks = lambda x: x.rearrange("p (c s) -> p c s", s=CHUNK)

        @block.sync
        def _(sp):
            def load(turn, first, last, lora=False):
                for i in range(first, last):
                    wait_apart(sp, sem["low"], 2 * (6 * turn + i - weights.COUNT + 1))
                    weights.load(sp, turn, i, lora)

            def load_w2(g):
                sp.dma_start(w2_s[0:LW, 0, :], w2[:, ds(g * P, P)]).then_inc(sem["w2_in"], 16)
                sp.dma_start(w2_s[LW:2 * LW, 1, :], a2[:, ds(g * P, P)]).then_inc(sem["w2_in"], 16)

            def load_g2(g):
                sp.dma_start(g2_s[:, 0, :], g2[0:GA, ds(g * P, P)]).then_inc(sem["g2_in"], 16)
                sp.dma_start(g2_s[0:GB, 1, :], g2[GA:GA + GB, ds(g * P, P)]).then_inc(sem["g2_in"], 16)

            load(0, weights.COUNT, 6, lora=True)
            load(1, 0, 6)
            sp.wait_ge(sem["zeroed"], 1)
            load_w2(0)
            load(2, 0, 6)
            load_g2(0)
            with sp.Fori(1, PAIRS - 1) as g:
                wait_apart(sp, sem["lora_wa"], 2 * g)
                load_w2(g)
                load(g + 2, 0, 6)
                wait_apart(sp, sem["gate"], g)
                load_g2(g)
            sp.wait_ge(sem["lora_wa"], 2 * (PAIRS - 1))
            load_w2(PAIRS - 1)
            sp.wait_ge(sem["gate"], PAIRS - 1)
            load_g2(PAIRS - 1)

        @block.tensor
        def _(pe):
            def multiply(turn, first, last, bank):
                for i in range(first, last):
                    n, k = divmod(i, KT)
                    if k % CUT == 0:
                        pe.wait_ge(sem["low"], 3 * GN * turn + i // CUT + 1)
                    for w, x in ((w_h, norm_h), (w_l, norm_h), (w_h, norm_l)):
                        ins = pe.matmul(ps[:, bank, :], w[:, i // CUT % CUTS, k % CUT, :], x[:, k, :],
                                        start=(k == 0 and w is w_h and x is norm_h),
                                        stop=(k == KT - 1 and x is norm_l))
                    if k % CUT == CUT - 1:
                        ins.then_inc(sem["multiplied"], 1)

            def project(g, first, last):
                for n in range(3):
                    start, end = max(first, n * KT), min(last, (n + 1) * KT)
                    if start == n * KT and start < end and (n or not isinstance(g, int) or g):
                        pe.wait_ge(sem["raw_ready"], 3 * g + n)
                    multiply(g + 1, start, end, PROJ)

            for n in range(3):
                multiply(0, n * KT, (n + 1) * KT, n)

            def mean_and_gate(g):
                pe.wait_ge(sem["g2_in"], (g + 1) * 32)
                pe.matmul(ps[:, 5, :], g2_s[:, 0, :], lora[:, 1, :], start=True, stop=False)
                pe.matmul(ps[:, 5, :], g2_s[0:GB, 1, :], lora[0:GB, 2, :], start=False, stop=True
                          ).then_inc(sem["gate"], 1)
                pe.wait_ge(sem["y_kept"], g + 1)
                pe.matmul(ps[:, 0, :], C["head_mean"][:], y, start=True, stop=True).then_inc(sem["mean"], 1)

            def variance(g):
                pe.wait_ge(sem["y_square"], g + 1)
                pe.matmul(ps[:, 1, :], C["head_mean"][:], y_scale, start=True, stop=True).then_inc(sem["var"], 1)

            def pair(g, first=False, last=False):
                pe.wait_ge(sem["w2_in"], (g + 1) * 32)
                for n in range(2):
                    pe.matmul(ps[:, 3 + n, :], w2_s[:, n, :], lora[:, 0, :], start=True, stop=True
                              ).then_inc(sem["lora_wa"], 1)
                if not first:
                    mean_and_gate(g - 1)
                pe.wait_ge(sem["wa_ready"], 2 * g + 1)
                pe.wait_ge(sem["kk_square"], g + 1)
                pe.matmul(ps[:, 3, :], C["head_sum"][:], t2, start=True, stop=True).then_inc(sem["kk_sum"], 1)
                if not last:
                    project(g + 1, 0, 10)
                if not first:
                    variance(g - 1)
                if not last:
                    project(g + 1, 10, 16)
                for t in range(NT):
                    ins = pe.transpose(ps[:, 0, t * P:(t + 1) * P], rkv[:, 2, t * P:(t + 1) * P], C["ident"][:])
                ins.then_inc(sem["turned"], 1)
                for h in range(2):
                    pe.wait_ge(sem["factors"], 2 * g + h + 1)
                    if h:
                        pe.wait_ge(sem["gram_kept"], 8 * g + 4)
                        pe.wait_ge(sem["rows_kept"], 3 * g + 2)
                    elif not first:
                        pe.wait_ge(sem["gate_kept"], g)
                    for t in range(NT):
                        cols = slice(t * P, (t + 1) * P)
                        for n, source in enumerate((b_in, k_in)):
                            ins = pe.matmul(ps[:, 3 + 2 * n + t // 2, (t % 2) * 2 * P:(t % 2 + 1) * 2 * P],
                                            source[:, h, cols], ar[:, t, :, :].rearrange("p a t -> p (a t)"),
                                            start=True, stop=True)
                            if t % 2:
                                ins.then_inc(sem["gram"], 1)
                        ins = pe.matmul(ps[:, 2 - h, cols], ar[:, t, 0, :], b_in[:, h, cols], start=True, stop=True)
                    ins.then_inc(sem["first_gram"], 1)
                    if h == 0:
                        pe.wait_ge(sem["ends"], 2 * (g + 1))
                        if not first:
                            pe.wait_ge(sem["var_log"], g)
                        for n, source in ((1, b_end), (0, k_end)):
                            if n == 0:
                                pe.wait_ge(sem["rows_kept"], 3 * g + 1)
                            for t in range(NT):
                                ins = pe.transpose(ps[:, n, t * P:(t + 1) * P], source[:, t * P:(t + 1) * P],
                                                   C["ident"][:])
                            ins.then_inc(sem["turned"], 1)
                        if not last:
                            project(g + 1, 16, 18)
                if not last:
                    project(g + 1, 18, 22)
                pe.wait_ge(sem["gram_kept"], 8 * g + 8)
                pe.wait_ge(sem["bonus_in"], g + 1)
                pe.matmul(ps[:, 6, :], C["head_sum"][:], kk[:], start=True, stop=True).then_inc(sem["bonus_sum"], 1)
                pe.wait_ge(sem["rows_kept"], 3 * g + 3)
                pe.wait_ge(sem["inv_start"], 2 * g + 2)
                for n in range(5):
                    for h in range(2):
                        b0 = 3 - 3 * h
                        pe.wait_ge(sem["join_ready"], 10 * g + 2 * n + h + 1)
                        if n:
                            pe.wait_ge(sem["level_kept"], 10 * g + 2 * (n - 1) + h + 1)
                        for t in range(NT):
                            ins = pe.matmul(ps[:, b0, t * P:(t + 1) * P], join[:, h, t, :], inv[:, h, t, :],
                                            start=True, stop=True)
                        ins.then_inc(sem["join_product"], 1)
                    if not last:
                        project(g + 1, 22 + 2 * n, 23 + 2 * n)
                    for h in range(2):
                        b0 = 3 - 3 * h
                        pe.wait_ge(sem["joined_kept"], 10 * g + 2 * n + h + 1)
                        for t in range(NT):
                            cols = slice(t * P, (t + 1) * P)
                            if n < 4:
                                pe.matmul(ps[:, b0 + 1, cols], inv_T[:, h, t, :], joined[:, h, t, :], start=True,
                                          stop=True)
                            ins = pe.matmul(ps[:, b0 + 2, cols], joined[:, h, t, :], inv_T[:, h, t, :], start=True,
                                            stop=True)
                        ins.then_inc(sem["level"], 1)
                    if not last:
                        project(g + 1, 23 + 2 * n, 24 + 2 * n)
                pe.wait_ge(sem["level_kept"], 10 * g + 10)
                for t in range(NT):
                    for h in range(2):
                        ins = pe.matmul(ps[:, 3, t * P + 64 * h:t * P + 64 * h + 64], from_k[:, h, t, 0, :],
                                        rows[:, 0, t, head(h)], start=True, stop=True)
                ins.then_inc(sem["lv_product"], 1)
                for c in range(NC):
                    t, rr = c // 2, half(c)
                    v_at = [2 * KT + min(KT, -(-KT * i // (2 * NC - 2))) for i in (2 * c, 2 * c + 1, 2 * c + 2)]
                    if c:
                        pe.wait_ge(sem["s_kept"], (NC - 1) * g + c)
                    pe.matmul(ps[rr, 4, 0:P], ar[:, t, 0, rr], state[:, c, :], start=True, stop=True
                              ).then_inc(sem["x_product"], 1)
                    pe.matmul(ps[:, 2, c * CHUNK:(c + 1) * CHUNK], state[:, c, :], ar[:, t, 1, rr], start=(c == 0),
                              stop=False, skip_group_check=True)
                    if not last:
                        project(g + 1, v_at[0], v_at[1])
                    pe.wait_ge(sem["x_kept"], NC * g + c + 1)
                    for h in range(2):
                        ins = pe.matmul(ps[rr, 5, head(h)], inv_T[:, h, t, rr], x_rows[:, head(h)], start=True,
                                        stop=True)
                    ins.then_inc(sem["u_product"], 1)
                    pe.wait_ge(sem["u_kept"], NC * g + c + 1)
                    if c < NC - 1:
                        pe.matmul(ps[:, 6, 0:P], rows[rr, 1, t, :], u_rows[rr, t, :], start=True, stop=False)
                        pe.matmul(ps[:, 6, 0:P], rows[rr, 2, t, :], rows[rr, 0, t, :], start=False, stop=True
                                  ).then_inc(sem["s_product"], 1)
                    if c % 2:
                        for h in range(2):
                            f = head(h)
                            pe.matmul(ps[f, 2, t * P:(t + 1) * P], u_rows[:, t, f], from_b[:, h, t, 1, :],
                                      start=False, stop=False, skip_group_check=True)
                            ins = pe.matmul(ps[f, 2, t * P:(t + 1) * P], rows[:, 0, t, f], from_k[:, h, t, 1, :],
                                            start=False, stop=(c == NC - 1), skip_group_check=True)
                    if not last:
                        project(g + 1, v_at[1], v_at[2])
                ins.then_inc(sem["y_product"], 1)

            project(0, 0, 3 * KT)
            pe.wait_ge(sem["lora_ready"], 3)
            pair(0, first=True)
            with pe.Fori(1, PAIRS - 1) as g:
                pair(g)
            pair(PAIRS - 1, last=True)
            mean_and_gate(PAIRS - 1)
            variance(PAIRS - 1)

        @block.scalar
        def _(act):
            act.wait_ge(sem["zeroed"], 1)
            for n, m in ((0, P), (1, P), (2, GB)):
                act.wait_ge(sem["multiplied"], GN * (n + 1))
                act.activation(raw[0:m, n, 1:], ps[0:m, n, :], ACT.Copy).then_inc(sem["lora_raw"], 1)
            for n, m, f in ((0, LW, ACT.Tanh), (1, P, ACT.Sigmoid), (2, GB, ACT.Sigmoid)):
                act.wait_ge(sem["lora_step"], n + 1)
                act.activation(lora[0:m, n, :], lora[0:m, n, :], f).then_inc(sem["lora_ready"], 1)

            def keep_raw(g, n, first=False):
                if not first:
                    act.wait_ge(sem["shift_steps"], 6 * (g - 1) + 2 * n + 2)
                act.wait_ge(sem["multiplied"], GN * (3 * g + 3 + n + 1))
                act.activation(raw[:, n, 1:], ps[:, PROJ, :], ACT.Copy).then_inc(sem["raw_ready"], 1)

            def keep_y(g):
                act.wait_ge(sem["y_product"], g + 1)
                act.activation(y, ps[:, 2, :], ACT.Copy).then_inc(sem["y_kept"], 1)

            def gate_and_square(g):
                act.wait_ge(sem["gate"], g + 1)
                act.activation(gate_s, ps[:, 5, :], ACT.Copy).then_inc(sem["gate_kept"], 1)
                act.wait_ge(sem["centred"], g + 1)
                act.activation(y_scale, y, ACT.Square).then_inc(sem["y_square"], 1)

            def y_root(g):
                act.wait_ge(sem["var"], g + 1)
                signal(act, act.activation(y_scale, ps[:, 1, :], ACT.Ln, bias=eps[:, 1:2]), sem["var_log"], g + 1)
                act.activation(y_scale, y_scale, ACT.Exp, scale=-0.5).then_inc(sem["var_root"], 1)

            def pair(g, first=False, last=False):
                if not first:
                    keep_y(g - 1)
                act.wait_ge(sem["kk_ready"], g + 1)
                act.activation(t2, kk[:], ACT.Square).then_inc(sem["kk_square"], 1)
                for n, (out, bias) in enumerate(((logw, W0), (a_t, A0))):
                    act.wait_ge(sem["lora_wa"], 2 * g + n + 1)
                    act.activation(out[:], ps[:, 3 + n, :], ACT.Sigmoid, bias=par[:, bias:bias + 1]
                                   ).then_inc(sem["wa_ready"], 1)
                act.wait_ge(sem["kk_sum"], g + 1)
                signal(act, act.activation(t1[:], ps[:, 3, :], ACT.Ln, bias=eps[:, 0:1]), sem["kk_log"], g + 1)
                act.activation(t1[:], t1[:], ACT.Exp, scale=-0.5).then_inc(sem["kk_root"], 1)
                act.wait_ge(sem["decays"], g + 1)
                act.activation(e_in, e_in, ACT.Exp).then_inc(sem["exps"], 1)
                signal(act, act.activation(e_out, cum, ACT.Exp, scale=-1.0), sem["exps"], 3 * g + 2)
                act.activation(cum, cum, ACT.Exp).then_inc(sem["exps"], 1)
                if not first:
                    gate_and_square(g - 1)
                    y_root(g - 1)
                if not last:
                    keep_raw(g + 1, 0)
                for n, bank in ((0, 0), (1, 1), (2, 0)):
                    act.wait_ge(sem["turned"], 3 * g + n + 1)
                    act.activation(rows[:, n, :, :].rearrange("p t f -> p (t f)"), ps[:, bank, :], ACT.Copy
                                   ).then_inc(sem["rows_kept"], 1)
                for n in range(5):
                    for h in range(2):
                        act.wait_ge(sem["join_product"], 10 * g + 2 * n + h + 1)
                        act.activation(joined[:, h, :, :].rearrange("p t f -> p (t f)"), ps[:, 3 - 3 * h, :], ACT.Copy
                                       ).then_inc(sem["joined_kept"], 1)
                if not last:
                    keep_raw(g + 1, 1)
                act.wait_ge(sem["lv_product"], g + 1)
                act.activation(lv[:].rearrange("p t f -> p (t f)"), ps[:, 3, :], ACT.Copy).then_inc(sem["lv_kept"], 1)
                for c in range(NC):
                    act.wait_ge(sem["u_product"], NC * g + c + 1)
                    act.activation(u_rows[half(c), c // 2, :], ps[half(c), 5, 0:P], ACT.Copy).then_inc(sem["u_kept"], 1)
                    if c == NC - 2 and not last:
                        keep_raw(g + 1, 2)

            for n in range(3):
                keep_raw(0, n, first=True)
            pair(0, first=True)
            with act.Fori(1, PAIRS - 1) as g:
                pair(g)
            pair(PAIRS - 1, last=True)
            keep_y(PAIRS - 1)
            gate_and_square(PAIRS - 1)
            y_root(PAIRS - 1)

        @block.vector
        def _(v):
            do = Chain(v, sem["v_steps"])
            do.go(v.memset(raw[:, :, 0:1], 0.0))
            do.go(v.memset(state[:], 0.0))
            do.go(v.memset(w2_s[:], 0.0))
            do.go(v.memset(b_in[:], 0.0))
            do.go(v.memset(k_in[:], 0.0))
            do.go(v.memset(eps[:, 0:1], 1e-12))
            do.go(v.memset(eps[:, 1:2], GN_EPS))
            do(v.memset(x_rows[:], 0.0))
            v.nop().then_inc(sem["zeroed"], 1)
            v.wait_ge(weights.mu_in, 48)
            v.wait_ge(weights.par_in, 16 * N_PAR)
            for n, m in ((0, P), (1, P), (2, GB)):
                v.wait_ge(sem["lora_raw"], n + 1)
                do(v.tensor_tensor(step[0:m, :], raw[0:m, n, 0:S], raw[0:m, n, 1:], ALU.subtract))
                signal(v, v.scalar_tensor_tensor(lora[0:m, n, :], step[0:m, :], lora_mu[0:m, n:n + 1], raw[0:m, n, 1:],
                                                 ALU.mult, ALU.add), sem["lora_step"], n + 1)
            before, V_STEPS = do.n, 11

            def take_params(g):
                signal(v, v.tensor_copy(par[:], params[:, :, ds(g, 1)].rearrange("p n o -> p (n o)")),
                       sem["par_ready"], g + 1)

            def shift_step(g, n):
                v.wait_ge(sem["raw_ready"], 3 * g + n + 1)
                signal(v, v.tensor_tensor(step[:], raw[:, n, 0:S], raw[:, n, 1:], ALU.subtract),
                       sem["shift_steps"], 6 * g + 2 * n + 1)

            def shift(g, n):
                signal(v, v.scalar_tensor_tensor(rkv[:, n, :], step[:], par[:, MU_R + n:MU_R + n + 1],
                                                 raw[:, n, 1:], ALU.mult, ALU.add),
                       sem["shift_steps"], 6 * g + 2 * n + 2)

            def scale_kk(g):
                signal(v, v.tensor_scalar(kk[:], rkv[:, 1, :], par[:, KK:KK + 1], None, ALU.mult), sem["kk_ready"],
                       g + 1)

            def centre(g):
                v.wait_ge(sem["y_kept"], g + 1)
                v.wait_ge(sem["mean"], g + 1)
                v.tensor_tensor(y, y, ps[:, 0, :], ALU.subtract).then_inc(sem["centred"], 1)

            def scale_y(g):
                v.wait_ge(sem["var_root"], g + 1)
                signal(v, v.scalar_tensor_tensor(y, y, par_end[:, 0:1], y_scale, ALU.mult,
                                                 ALU.mult), sem["end_steps"], g + 1)
                signal(v, v.scalar_tensor_tensor(y, y, par_end[:, 1:2], bonus[:], ALU.add,
                                                 ALU.add), sem["y_ready"], g + 1)

            def pair(g, first=False, last=False):
                r, k, val = (rkv[:, n, :] for n in range(3))
                do = Chain(v, sem["v_steps"], before + g * V_STEPS)
                v.wait_ge(sem["wa_ready"], 2 * g + 1)
                do(v.tensor_scalar(logw[:], logw[:], -math.exp(-0.5), None, ALU.mult))
                do(v.tensor_tensor_scan(cum, C["no_carry"][:], logw[:], 0.0, ALU.mult, ALU.add))
                v.tensor_tensor(e_in, cum, logw[:], ALU.subtract).then_inc(sem["decays"], 1)
                if not first:
                    centre(g - 1)
                v.wait_ge(sem["wa_ready"], 2 * g + 2)
                do(v.tensor_scalar(kmix[:], a_t[:], 1.0, par[:, KA:KA + 1], ALU.subtract, ALU.mult))
                do(v.scalar_tensor_tensor(kmix[:], kmix[:], 1.0, k, ALU.add, ALU.mult))
                v.wait_ge(sem["kk_root"], g + 1)
                do(v.tensor_tensor(kk[:], kk[:], t1[:], ALU.mult))
                do(v.tensor_tensor(t2, kk[:], a_t[:], ALU.mult))
                v.wait_ge(sem["exps"], 3 * g + 3)
                do(v.tensor_copy(d_end[:], chunks(cum)[:, :, CHUNK - 1]))
                v.nop().then_inc(sem["ends_can_start"], 1)
                do.go(v.scalar_tensor_tensor(ar[:, :, 0, :], tiles(kk[:]), -1.0, tiles(e_in), ALU.mult, ALU.mult))
                do.go(v.tensor_tensor(ar[:, :, 1, :], tiles(r), tiles(cum), ALU.mult))
                for h in range(2):
                    f = head(h)
                    do.go(v.tensor_tensor(b_in[f, h, :], t2[f, :], e_out[f, :], ALU.mult))
                    v.tensor_tensor(k_in[f, h, :], kmix[f, :], e_out[f, :], ALU.mult).then_inc(sem["factors"], 1)
                do.wait()
                assert do.n == V_STEPS, do.n
                v.scalar_tensor_tensor(kk[:], r, par[:, RK:RK + 1], kmix[:], ALU.mult, ALU.mult
                                       ).then_inc(sem["bonus_in"], 1)
                if not first:
                    scale_y(g - 1)
                for h in range(2):
                    for i, (bank, kept, t0) in enumerate(((3, from_b, 0), (5, from_k, 0), (4, from_b, 2),
                                                          (6, from_k, 2))):
                        v.wait_ge(sem["gram"], 8 * g + 4 * h + i + 1)
                        v.tensor_tensor(kept[:, h, t0:t0 + 2, :, :].rearrange("p t a s -> p t (a s)"),
                                        ps[:, bank, :].rearrange("p (t s) -> p t s", t=2),
                                        C["seen"][:].rearrange("p a s -> p (a s)").unsqueeze(1
                                                               ).to_broadcast([P, 2, 2 * P]),
                                        ALU.mult).then_inc(sem["gram_kept"], 1)
                    v.wait_ge(sem["first_gram"], 2 * g + h + 1)
                    signal(v, v.tensor_tensor(inv[:, h, :, :], tiles(ps[:, 2 - h, :]),
                                              C["first_down"][:].unsqueeze(1).to_broadcast([P, NT, P]), ALU.mult),
                           sem["inv_kept"], 10 * g + h + 1)
                    v.tensor_tensor(inv[:, h, :, :], inv[:, h, :, :],
                                    C["ident"][:].unsqueeze(1).to_broadcast([P, NT, P]),
                                    ALU.add).then_inc(sem["inv_start"], 1)
                for n in range(5):
                    for h in range(2):
                        flat = lambda x: x[:, h, :, :].rearrange("p t s -> p (t s)")
                        v.wait_ge(sem["level"], 10 * g + 2 * n + h + 1)
                        if n < 4:
                            v.tensor_tensor(flat(inv), flat(inv), ps[:, 4 - 3 * h, :], ALU.add
                                            ).then_inc(sem["inv_kept"], 1)
                        v.tensor_tensor(flat(inv_T), flat(inv_T), ps[:, 5 - 3 * h, :], ALU.add
                                        ).then_inc(sem["level_kept"], 1)
                    if n == 0:
                        v.wait_ge(sem["bonus_sum"], g + 1)
                        signal(v, v.tensor_tensor(bonus[:], val, ps[:, 6, :], ALU.mult), sem["bonus_steps"], 2 * g + 1)
                        signal(v, v.tensor_copy(par_end[:], par[:, LG:LB + 1]), sem["bonus_steps"], 2 * g + 2)
                    if not last:
                        if n == 0:
                            take_params(g + 1)
                        if n == 1:
                            shift_step(g + 1, 0)
                        if n == 2:
                            shift(g + 1, 0)
                v.wait_ge(sem["lv_kept"], g + 1)
                for c in range(NC):
                    rr = half(c)
                    v.wait_ge(sem["x_product"], NC * g + c + 1)
                    v.tensor_tensor(x_rows[rr, :], ps[rr, 4, 0:P], lv[rr, c // 2, :], ALU.add
                                    ).then_inc(sem["x_kept"], 1)
                    if not last:
                        if c == 0:
                            shift_step(g + 1, 1)
                        if c == 1:
                            shift(g + 1, 1)
                        if c == 2:
                            scale_kk(g + 1)
                        if c == NC - 1:
                            shift_step(g + 1, 2)
                            shift(g + 1, 2)
                    if c < NC - 1:
                        v.wait_ge(sem["s_product"], (NC - 1) * g + c + 1)
                        for h in range(2):
                            f = head(h)
                            ins = v.scalar_tensor_tensor(state[f, c + 1, f], state[f, c, f], d_end[f, c:c + 1],
                                                         ps[f, 6, f], ALU.mult, ALU.add)
                            ins.then_inc(sem["s_half" if h == 0 else "s_kept"], 1)

            take_params(0)
            for n in range(3):
                shift_step(0, n)
                shift(0, n)
            scale_kk(0)
            pair(0, first=True)
            with v.Fori(1, PAIRS - 1) as g:
                pair(g)
            pair(PAIRS - 1, last=True)
            centre(PAIRS - 1)
            scale_y(PAIRS - 1)

        @block.gpsimd
        def _(pool):
            bc = lambda m: m.unsqueeze(1).to_broadcast([P, NT, P])

            def open_gate(g):
                pool.wait_ge(sem["gate_kept"], g + 1)
                pool.wait_ge(sem["y_ready"], g + 1)
                pool.tensor_tensor(mixed_T[:, ds(g, 1), :].rearrange("p o s -> p (o s)"), y,
                                   gate_s, ALU.mult).then_inc(sem["mixed"], 1)

            def cut(turn, first, last, lora=False):
                for i in range(first, last):
                    load, part = i // (GN // 2), i % (GN // 2)
                    cols = weights.columns(i // GN, lora)
                    wait_apart(pool, weights.landed[load % weights.COUNT], weights.landed_value(turn, load))
                    if not lora or i >= CUTS:
                        wait_apart(pool, sem["multiplied"], 3 * GN * turn + i - CUTS + 1)
                    whole = weights.tensor[:, load % weights.COUNT, part * CUT:(part + 1) * CUT, 0:cols]
                    high, low = w_h[:, i % CUTS, :, 0:cols], w_l[:, i % CUTS, :, 0:cols]
                    pool.tensor_copy(high, whole).then_inc(sem["high"], 1)
                    wait_apart(pool, sem["high"], 3 * GN * turn + i + 1)
                    pool.tensor_tensor(low, whole, high.bitcast(F32), ALU.subtract).then_inc(sem["low"], 1)

            def pair(g, behind, first=False):
                K0, K1, K2, K3, V0, V1, V2 = range(GN, 2 * GN + 3)
                do = Chain(pool, sem["pool_steps"], 5 * g)
                if behind:
                    cut(g + 2, CUTS, K0)
                pool.wait_ge(sem["ends_can_start"], g + 1)
                do(pool.tensor_tensor(chunks(e_end[:]), chunks(e_out),
                                      d_end[:].unsqueeze(2).to_broadcast([P, NC, CHUNK]), ALU.mult))
                pool.tensor_tensor(b_end[:], t2, e_end[:], ALU.mult).then_inc(sem["ends"], 1)
                pool.tensor_tensor(k_end[:], kmix[:], e_end[:], ALU.mult).then_inc(sem["ends"], 1)
                if behind:
                    cut(g + 2, K0, K1)
                if not first:
                    open_gate(g - 1)
                for h in range(2):
                    pool.wait_ge(sem["gram_kept"], 8 * g + 4 * h + 3)
                    do(pool.tensor_tensor(inv_T[:, h, :, :], from_b[:, h, :, 0, :], bc(C["first_up"][:]), ALU.mult))
                    do(pool.tensor_tensor(inv_T[:, h, :, :], inv_T[:, h, :, :], bc(C["ident"][:]), ALU.add))
                    pool.tensor_tensor(join[:, h, :, :], from_b[:, h, :, 0, :], bc(C["levels"][:, 0, :]),
                                       ALU.mult).then_inc(sem["join_ready"], 1)
                    if behind and h == 0:
                        cut(g + 2, K1, K2)
                for n in range(1, 5):
                    for h in range(2):
                        pool.wait_ge(sem["join_product"], 10 * g + 2 * (n - 1) + h + 1)
                        pool.tensor_tensor(join[:, h, :, :], from_b[:, h, :, 0, :], bc(C["levels"][:, n, :]),
                                           ALU.mult).then_inc(sem["join_ready"], 1)
                    if behind:
                        cut(g + 2, K1 + n, K2 + n)
                if behind:
                    cut(g + 2, V2, 3 * GN)
                if behind > 1:
                    cut(g + 3, 0, CUTS)

            cut(0, 0, 3 * GN, lora=True)
            cut(1, 0, 3 * GN)
            cut(2, 0, CUTS)
            pair(0, 2, first=True)
            with pool.Fori(1, PAIRS - 2) as g:
                pair(g, 2)
            pair(PAIRS - 2, 1)
            pair(PAIRS - 1, 0)
            open_gate(PAIRS - 1)


def output_projection(nc, mixed_dram, mixed_T, ring, x, x_rows, sums):
    H = mixed_T.shape[1]

    def setup(st):
        return {"first": st.sb("first", [P, H, mixed_T.shape[2]]), "first_in": st.sem("first_in"), "x_in": [st.sem(f"x_in{t}") for t in range(4)], "squared": st.sem("squared"),
                "square": st.sb("square", [P, BANK])}

    def sync(sp, extra):
        sp.dma_start(extra["first"][:], mixed_dram).then_inc(extra["first_in"], 16)
        for t in range(4):
            sp.dma_start(x_rows[:, t, :], x[t * P:(t + 1) * P, :]).then_inc(extra["x_in"][t], 16)

    def vector(v, half, b, ps, extra, done):
        t, cols = b // 2, slice(half * 1024 + (b % 2) * BANK, half * 1024 + (b % 2 + 1) * BANK)
        v.wait_ge(extra["x_in"][t], 16)
        v.tensor_tensor(x_rows[:, t, cols], x_rows[:, t, cols], ps[:, b, :], ALU.add).then_inc(done, 1)

    def scalar(act, half, b, ps, extra, taken_v):
        t, cols = b // 2, slice(half * 1024 + (b % 2) * BANK, half * 1024 + (b % 2 + 1) * BANK)
        act.wait_ge(taken_v, half * 8 + b + 1)
        part = 2 * half + b % 2
        signal(act, act.activation(extra["square"][:], x_rows[:, t, cols], ACT.Square,
                                   accum_out=sums[:, t, part:part + 1]), extra["squared"], half * 8 + b + 1)

    def tile(eng, k, extra):
        if k == H:
            eng.wait_ge(extra["first_in"], 16)
        return mixed_T[:, k, :] if k < H else extra["first"][:, k - H, :]

    project_rows(nc, "out", tile, ring, vector, setup=setup, sync=sync, split=True,
                 scalar_first=scalar)


def route(nc, C, hn_T, router_g, router_g_b, router_e, router_e_b, R, token_table, ahead):
    KT = hn_T.shape[1]
    G, E = router_g.shape[1], router_e.shape[1]
    EG, NT = E // G, 4
    NB = hn_T.shape[2] // SLOTS - 1
    NL = G + E
    with Stage(nc, "route") as st:
        w = st.sb("w", [P, KT, NL])
        bias = st.sb("bias", [NL, 1])
        logits_T = st.sb("logits_T", [NL, 512])
        lg = st.sb("logits", [P, NT, NL])
        group_at, expert_at = st.sb("group_at", [P, G]), st.sb("expert_at", [P, EG])
        first_at = st.sb("first_at", [P, NB + 1, E])
        later_at = st.sb("later_at", [P, NB, E])
        expert_no = st.sb("expert_no", [P, NB, E])
        edges = st.sb("edges", [P, NB + 2])
        block_min = st.sb("block_min", [P, NB, E])
        own_index = st.sb("own_index", [P, 1])
        token_id = st.sb("token_id", [P, NT, 16], I32)
        g4, g4b = st.sb("g4", [P, NT, G]), st.sb("g4b", [P, NT, G])
        pick = st.sb("pick", [P, NT, G, EG])
        e8, e8b, cand = (st.sb(n, [P, NT, EG]) for n in ("e8", "e8b", "cand"))
        chosen = st.sb("chosen", [P, 2, NT, EG])
        hot = st.sb("hot", [P, 2, NT, G, EG])
        both = st.sb("both", [P, NT, E])
        rank = st.sb("rank", [P, NT, E])
        picked = st.sb("picked", [P, NT, NB + 1, E])
        own_rank = st.sb("own_rank", [P, NT, 1])
        reached = st.sb("reached", [P, NT, NB + 2])
        candidate = st.sb("candidate", [P, NT, NB + 1])
        c1, c2, c3, c4, c5 = (st.sb(n, [P, NT, 1]) for n in ("c1", "c2", "c3", "c4", "c5"))
        slot_f = st.sb("slot_f", [P, 2, NT])
        count = st.sb("count", [P, E])
        over = st.sb("over", [P, NB * E])
        order = st.sb("order", [P, NB * E])
        ones_row = st.sb("ones_row", [P, NB * E])
        item = st.sb("item", [P, 1])
        ps = st.psum()
        sem = {n: st.sem(n) for n in ("w_in", "iota", "logits", "biased", "turned", "v_steps", "difference",
                                      "exp_g", "top", "exp_e", "both_ready", "ranked", "slots_ready", "scattered",
                                      "item_ready", "item_turned", "pool_steps", "items_ready")}
        block = st.block()

        @block.sync
        def _(sp):
            with nc.allow_non_contiguous_dma("router weights"):
                sp.dma_start(w[:, :, 0:G], router_g.rearrange("(k p) n -> p k n", p=P)).then_inc(sem["w_in"], 16)
                sp.dma_start(w[:, :, G:NL], router_e.rearrange("(k p) n -> p k n", p=P)).then_inc(sem["w_in"], 16)
                sp.dma_start(bias[0:G, :], router_g_b.rearrange("(p o) -> p o", o=1)).then_inc(sem["w_in"], 16)
                sp.dma_start(bias[G:NL, :], router_e_b.rearrange("(p o) -> p o", o=1)).then_inc(sem["w_in"], 16)
            ahead(sp)

        @block.tensor
        def _(pe):
            pe.wait_ge(sem["w_in"], 64)
            for k in range(KT):
                ins = pe.matmul(ps[0:NL, 0, :], w[:, k, :], hn_T[:, k, :], start=(k == 0), stop=(k == KT - 1))
            ins.then_inc(sem["logits"], 1)
            pe.wait_ge(sem["biased"], 1)
            for t in range(NT):
                ins = pe.transpose(ps[:, 1, t * NL:(t + 1) * NL], logits_T[:, t * P:(t + 1) * P],
                                   C["ident"][0:NL, 0:NL])
            ins.then_inc(sem["turned"], 1)
            pe.wait_ge(sem["both_ready"], 1)
            for t in range(NT + 1):
                for j in range(min(t, NT - 1) + 1):
                    ins = pe.matmul(ps[:, 2, t * E:(t + 1) * E], C["after" if j == t else "ones"][:], both[:, j, :],
                                    start=(j == 0), stop=(j == min(t, NT - 1)))
            ins.then_inc(sem["ranked"], 1)
            pe.wait_ge(sem["item_ready"], 1)
            pe.matmul(ps[0:1, 3, 0:P], item[:], C["ident"][:], start=True, stop=True).then_inc(sem["item_turned"], 1)

        @block.scalar
        def _(act):
            act.wait_ge(sem["logits"], 1)
            act.wait_ge(sem["w_in"], 64)
            act.activation(logits_T[:], ps[0:NL, 0, :], ACT.Identity, bias=bias[:]).then_inc(sem["biased"], 1)
            act.wait_ge(sem["difference"], 1)
            act.activation(g4b[:], g4b[:], ACT.Exp).then_inc(sem["exp_g"], 1)
            act.wait_ge(sem["top"], 1)
            act.activation(c4[:], c4[:], ACT.Exp).then_inc(sem["exp_e"], 1)

        @block.gpsimd
        def _(pool):
            do = Chain(pool, sem["pool_steps"])
            kw = dict(allow_small_or_imprecise_dtypes=True)
            do.go(pool.iota(group_at[:], [[1, G]], base=-G, channel_multiplier=0, **kw))
            do.go(pool.iota(expert_at[:], [[1, EG]], base=-EG, channel_multiplier=0, **kw))
            do.go(pool.iota(first_at[:, 0, :], [[SLOTS, E]], base=0, channel_multiplier=0, **kw))
            do.go(pool.iota(later_at[:], [[-SLOTS, NB], [0, E]], base=(E - 2) * SLOTS, channel_multiplier=0, **kw))
            do.go(pool.iota(expert_no[:], [[0, NB], [1, E]], base=0, channel_multiplier=0, **kw))
            do.go(pool.iota(edges[:], [[SLOTS, NB + 2]], base=0, channel_multiplier=0, **kw))
            do.go(pool.iota(block_min[:], [[SLOTS, NB], [0, E]], base=SLOTS, channel_multiplier=0, **kw))
            do.go(pool.iota(own_index[:], [[0, 1]], base=0, channel_multiplier=1, **kw))
            do.go(pool.iota(token_id[:], [[P, NT], [0, 16]], base=0, channel_multiplier=1))
            do(pool.memset(ones_row[:], 1.0))
            pool.nop().then_inc(sem["iota"], 1)
            pool.wait_ge(sem["slots_ready"], 2)
            for n in range(2):
                for t in range(NT):
                    pool.indirect_dma_start(
                        out=token_table, out_offset=bass.IndirectOffsetOnAxis(ap=R["slot"][:, n, t:t + 1], axis=0),
                        in_=token_id[:, t, :], in_offset=None).then_inc(sem["scattered"], 16)
            pool.wait_ge(sem["scattered"], 16 * 2 * NT)

        @block.vector
        def _(v):
            do = Chain(v, sem["v_steps"])
            v.wait_ge(sem["iota"], 1)
            v.wait_ge(sem["turned"], 1)
            wide = lambda x, n: x.to_broadcast([P, NT, n])
            do(v.tensor_copy(lg[:], ps[:, 1, 0:NT * NL].rearrange("p (t n) -> p t n", n=NL)))

            def first_top(values, at, n, best, mark, cand):
                do(v.tensor_reduce(best, values, AX_X, ALU.max))
                do(v.tensor_tensor(mark, values, wide(best, n), ALU.is_equal))
                do(v.tensor_tensor(cand, mark, at[:].unsqueeze(1).to_broadcast([P, NT, n]), ALU.mult))
                do(v.tensor_reduce(c5[:], cand, AX_X, ALU.min))
                do(v.tensor_tensor(mark, at[:].unsqueeze(1).to_broadcast([P, NT, n]), wide(c5[:], n), ALU.is_equal))

            first_top(lg[:, :, 0:G], group_at, G, c1[:], g4[:], g4b[:])
            signal(v, v.tensor_tensor(g4b[:], lg[:, :, 0:G], wide(c1[:], G), ALU.subtract), sem["difference"], 1)
            do(v.tensor_tensor(pick[:], lg[:, :, G:NL].rearrange("p t (g e) -> p t g e", g=G),
                               g4[:].unsqueeze(3).to_broadcast([P, NT, G, EG]), ALU.mult))
            do(v.tensor_tensor(e8[:], pick[:, :, 0, :], pick[:, :, 1, :], ALU.add))
            for g in range(2, G):
                do(v.tensor_tensor(e8[:], e8[:], pick[:, :, g, :], ALU.add))
            first_top(e8[:], expert_at, EG, c2[:], chosen[:, 0, :, :], cand[:])
            do(v.scalar_tensor_tensor(e8b[:], chosen[:, 0, :, :], -1e30, e8[:], ALU.mult, ALU.add))
            first_top(e8b[:], expert_at, EG, c3[:], chosen[:, 1, :, :], cand[:])
            signal(v, v.tensor_tensor(c4[:], c3[:], c2[:], ALU.subtract), sem["top"], 1)
            for n in range(2):
                do(v.tensor_tensor(hot[:, n, :, :, :], g4[:].unsqueeze(3).to_broadcast([P, NT, G, EG]),
                                   chosen[:, n, :, :].unsqueeze(2).to_broadcast([P, NT, G, EG]), ALU.mult))
            flat = lambda n: hot[:, n, :, :, :].rearrange("p t g e -> p t (g e)")
            signal(v, v.tensor_tensor(both[:], flat(0), flat(1), ALU.add), sem["both_ready"], 1)
            v.wait_ge(sem["exp_g"], 1)
            do(v.tensor_reduce(c1[:], g4b[:], AX_X, ALU.add))
            v.wait_ge(sem["exp_e"], 1)
            do(v.tensor_scalar(c2[:], c4[:], 1.0, None, ALU.add))
            do(v.tensor_tensor(c2[:], c2[:], c1[:], ALU.mult))
            do(v.reciprocal(R["weight"][:, 0, :].unsqueeze(2), c2[:]))
            do(v.tensor_tensor(R["weight"][:, 1, :].unsqueeze(2), R["weight"][:, 0, :].unsqueeze(2), c4[:], ALU.mult))
            v.wait_ge(sem["ranked"], 1)
            do(v.tensor_copy(rank[:], ps[:, 2, 0:NT * E].rearrange("p (t e) -> p t e", e=E)))
            do(v.tensor_copy(count[:], ps[:, 2, NT * E:(NT + 1) * E]))
            over3 = over[:].rearrange("p (b e) -> p b e", e=E)
            do(v.tensor_tensor(over3, count[:].unsqueeze(1).to_broadcast([P, NB, E]), block_min[:], ALU.is_gt))
            do(v.tensor_tensor_scan(order[:], ones_row[:], over[:], 0.0, ALU.mult, ALU.add))
            do(v.tensor_copy(R["n_items"][:], order[:, NB * E - 1:NB * E]))
            do(v.scalar_tensor_tensor(first_at[:, 1:, :], order[:].rearrange("p (b e) -> p b e", e=E), float(SLOTS),
                                      later_at[:], ALU.mult, ALU.add))
            for n in range(2):
                do(v.tensor_tensor(picked[:, :, 0, :], rank[:], flat(n), ALU.mult))
                do(v.tensor_reduce(own_rank[:], picked[:, :, 0, :], AX_X, ALU.add))
                do(v.tensor_tensor(reached[:], own_rank[:].to_broadcast([P, NT, NB + 2]),
                                   edges[:].unsqueeze(1).to_broadcast([P, NT, NB + 2]), ALU.is_ge))
                do(v.tensor_tensor(reached[:, :, 0:NB + 1], reached[:, :, 0:NB + 1], reached[:, :, 1:NB + 2],
                                   ALU.subtract))
                do(v.tensor_tensor(picked[:], first_at[:].unsqueeze(1).to_broadcast([P, NT, NB + 1, E]),
                                   flat(n).unsqueeze(2).to_broadcast([P, NT, NB + 1, E]), ALU.mult))
                do(v.tensor_reduce(candidate[:].unsqueeze(3), picked[:], AX_X, ALU.add))
                do(v.tensor_tensor(candidate[:], candidate[:], reached[:, :, 0:NB + 1], ALU.mult))
                do(v.tensor_reduce(slot_f[:, n, :].unsqueeze(2), candidate[:], AX_X, ALU.add))
                do(v.tensor_tensor(slot_f[:, n, :].unsqueeze(2), slot_f[:, n, :].unsqueeze(2), own_rank[:], ALU.add))
                signal(v, v.tensor_copy(R["slot"][:, n, :], slot_f[:, n, :]), sem["slots_ready"], n + 1)
            do(v.tensor_tensor(order[:], order[:], over[:], ALU.mult))
            do(v.tensor_scalar(own_index[:], own_index[:], 1.0, None, ALU.add))
            do(v.tensor_scalar(order[:], order[:], own_index[:, 0:1], None, ALU.is_equal))
            do(v.tensor_tensor(over[:], order[:], expert_no[:].rearrange("p b e -> p (b e)"), ALU.mult))
            signal(v, v.tensor_reduce(item[:], over[:], AX_X, ALU.add), sem["item_ready"], 1)
            v.wait_ge(sem["item_turned"], 1)
            do(v.tensor_copy(R["item_expert"][:], ps[0:1, 3, 0:P]))


class ExpertWeights:

    def __init__(self, nc, keep, w_up, w_down):
        E, D, F2 = w_up.shape
        self.UP, self.DOWN = D // P // 4, F2 // 2 // P // 2
        self.w_u = keep.enter_context(nc.sbuf_tensor("moe_w_up", [P, self.UP, 4, F2], F32))
        self.w_d = keep.enter_context(nc.sbuf_tensor("moe_w_down", [P, self.DOWN, 2, D], F32))
        self.up_in = [nc.alloc_semaphore(f"moe_up_in{n}") for n in range(self.UP)]
        self.down_in = [nc.alloc_semaphore(f"moe_down_in{n}") for n in range(self.DOWN)]
        self.up = w_up.rearrange("e (n k p) f -> e p n k f", p=P, k=4)
        self.down = w_down.rearrange("e (n k p) f -> e p n k f", p=P, k=2)

    def load_up(self, sp, expert, n):
        sp.dma_start(self.w_u[:, n, :, :], self.up[ds(expert, 1), :, n, :, :].rearrange("e p k f -> (e p) k f")
                     ).then_inc(self.up_in[n], 16)

    def load_down(self, sp, expert, n):
        sp.dma_start(self.w_d[:, n, :, :], self.down[ds(expert, 1), :, n, :, :].rearrange("e p k f -> (e p) k f")
                     ).then_inc(self.down_in[n], 16)

    def ahead(self, sp):
        for n in range(self.UP):
            self.load_up(sp, 0, n)
        for n in range(self.DOWN):
            self.load_down(sp, 0, n)


def experts(nc, C, gain, W, E, D, F2, R, token_table, rows_dram, y_dram, ahead):
    F = F2 // 2
    KT, FT, ITEMS = D // P, F // P, R["max_items"]
    UP, DOWN, w_u, w_d, up_in, down_in = W.UP, W.DOWN, W.w_u, W.w_d, W.up_in, W.down_in
    with Stage(nc, "moe") as st:
        g = st.sb("gain", [P, KT])
        ids = st.sb("ids", [SLOTS, 16], I32)
        x_in = st.sb("x_in", [SLOTS, D])
        x_T = st.sb("x_T", [P, KT, SLOTS])
        sig = st.sb("sig", [P, F // 2])
        hid = st.sb("hid", [P, F // 2])
        hid_T = st.sb("hid_T", [P, 2, 2, SLOTS])
        y = st.sb("y", [P, 2, BANK])
        ps = st.psum()
        sem = {n: st.sem(n) for n in ("gain_in", "ids_in", "x_in", "x_turned", "x_scaled", "up_used", "up_done",
                                      "sigmoid", "gated", "hidden", "hid_turned", "hid_kept", "down_used",
                                      "y_kept_v", "y_kept_s", "stored")}
        block = st.block()

        def turns(eng, turn):
            turn(0, 0, 0, True)
            with eng.Fori(1, E) as i:
                turn(i, i, i * SLOTS, False)
            n_items = eng.value_load(R["n_items"][0:1, 0:1], min_val=0, max_val=ITEMS)
            with eng.If(n_items > 0):
                with eng.Fori(0, ITEMS) as i:
                    with eng.If(n_items > i):
                        expert = eng.value_load(R["item_expert"][0:1, ds(i, 1)], min_val=0, max_val=E - 1)
                        turn(i + E, expert, (i + E) * SLOTS, False)
                    eng.nop()
            eng.nop()

        @block.sync
        def _(sp):
            with nc.allow_non_contiguous_dma("a gain per partition"):
                sp.dma_start(g[:], gain.rearrange("(k p) -> p k", p=P)).then_inc(sem["gain_in"], 16)
            ahead(sp)

            def turn(i, expert, row, first):
                if first:
                    return
                for n in range(UP):
                    sp.wait_ge(sem["up_used"], (i - 1) * UP + n + 1)
                    W.load_up(sp, expert, n)
                for n in range(DOWN):
                    sp.wait_ge(sem["down_used"], (i - 1) * DOWN + n + 1)
                    W.load_down(sp, expert, n)
            turns(sp, turn)

        @block.gpsimd
        def _(pool):
            def turn(i, expert, row, first):
                if not first:
                    pool.wait_ge(sem["x_turned"], i * 2)
                pool.dma_start(ids[:], token_table[ds(row, SLOTS), :]).then_inc(sem["ids_in"], 16)
                wait_apart(pool, sem["ids_in"], (i + 1) * 16)
                pool.indirect_dma_start(out=x_in[:], out_offset=None, in_=rows_dram,
                                        in_offset=bass.IndirectOffsetOnAxis(ap=ids[:, 0:1], axis=0)
                                        ).then_inc(sem["x_in"], 16)
            turns(pool, turn)

        @block.tensor
        def _(pe):
            def turn(i, expert, row, first):
                wait_apart(pe, sem["x_in"], (i + 1) * 16)
                for b in range(2):
                    for k in range(KT // 2):
                        kk = b * KT // 2 + k
                        ins = pe.transpose(ps[:, b, k * SLOTS:(k + 1) * SLOTS], x_in[:, kk * P:(kk + 1) * P],
                                           C["ident"][0:SLOTS, 0:SLOTS])
                    ins.then_inc(sem["x_turned"], 1)
                for n in range(UP):
                    pe.wait_ge(up_in[n], (i + 1) * 16)
                    for s in range(4):
                        k = 4 * n + s
                        if k % (KT // 2) == 0:
                            pe.wait_ge(sem["x_scaled"], i * 2 + k // (KT // 2) + 1)
                        cols = w_u[:, n, s, :].rearrange("p (a c f) -> p a c f", a=2, c=2)
                        for c in range(2):
                            ins = pe.matmul(ps[64 * c:64 * c + 64, 2, :].rearrange("p (a f) -> p a f", a=2),
                                            x_T[:, k, :], cols[:, :, c, :], start=(k == 0), stop=(k == KT - 1))
                            if c == 0 and k == KT - 1:
                                ins.then_inc(sem["up_done"], 1)
                    ins.then_inc(sem["up_used"], 1)
                pe.wait_ge(sem["hidden"], i + 1)
                for c in range(2):
                    ins = pe.transpose(ps[:, 3, c * P:(c + 1) * P], hid[:, c * P:(c + 1) * P], C["ident"][:])
                ins.then_inc(sem["hid_turned"], 1)
                pe.wait_ge(sem["hid_kept"], i + 1)
                if not first:
                    pe.wait_ge(sem["y_kept_v"], i)
                    pe.wait_ge(sem["y_kept_s"], i)
                for n in range(DOWN):
                    pe.wait_ge(down_in[n], (i + 1) * 16)
                    for s in range(2):
                        f = 2 * n + s
                        for b in range(2):
                            for c in range(2):
                                ins = pe.matmul(ps[64 * c:64 * c + 64, 4 + b, :], hid_T[:, f % 2, f // 2, :],
                                                w_d[:, n, s, (2 * c + b) * BANK:(2 * c + b + 1) * BANK],
                                                start=(f == 0), stop=(f == FT - 1))
                    ins.then_inc(sem["down_used"], 1)
            turns(pe, turn)

        @block.scalar
        def _(act):
            def turn(i, expert, row, first):
                act.wait_ge(sem["up_used"], (i + 1) * UP)
                act.activation(sig[:], ps[:, 2, 0:F // 2], ACT.Sigmoid).then_inc(sem["sigmoid"], 1)
                act.wait_ge(sem["down_used"], (i + 1) * DOWN)
                if not first:
                    act.wait_ge(sem["stored"], i * 32)
                signal(act, act.activation(y[:, 1, :], ps[:, 5, :], ACT.Copy), sem["y_kept_s"], i + 1)
                act.wait_ge(sem["y_kept_v"], i + 1)
                for c in range(2):
                    act.dma_start(y_dram[ds(row, SLOTS), c * 1024:(c + 1) * 1024],
                                  y[64 * c:64 * c + 64, :, :].rearrange("p b n -> p (b n)")
                                  ).then_inc(sem["stored"], 16)
            turns(act, turn)
            n_items = act.value_load(R["n_items"][0:1, 0:1], min_val=0, max_val=ITEMS)
            wait_apart(act, sem["stored"], (n_items + E) * 32)

        @block.vector
        def _(v):
            v.wait_ge(sem["gain_in"], 16)

            def turn(i, expert, row, first):
                for b in range(2):
                    v.wait_ge(sem["x_turned"], i * 2 + b + 1)
                    k = slice(b * KT // 2, (b + 1) * KT // 2)
                    v.tensor_tensor(x_T[:, k, :], ps[:, b, :].rearrange("p (k s) -> p k s", s=SLOTS),
                                    g[:, k].unsqueeze(2).to_broadcast([P, KT // 2, SLOTS]),
                                    ALU.mult).then_inc(sem["x_scaled"], 1)
                v.wait_ge(sem["sigmoid"], i + 1)
                signal(v, v.tensor_tensor(hid[:], sig[:], ps[:, 2, 0:F // 2], ALU.mult), sem["gated"], i + 1)
                v.tensor_tensor(hid[:], hid[:], ps[:, 2, F // 2:F], ALU.mult).then_inc(sem["hidden"], 1)
                v.wait_ge(sem["hid_turned"], i + 1)
                v.tensor_copy(hid_T[:].rearrange("p a c s -> p (a c s)"), ps[:, 3, 0:4 * SLOTS]
                              ).then_inc(sem["hid_kept"], 1)
                v.wait_ge(sem["down_used"], (i + 1) * DOWN)
                if not first:
                    v.wait_ge(sem["stored"], i * 32)
                v.tensor_copy(y[:, 0, :], ps[:, 4, :]).then_inc(sem["y_kept_v"], 1)
            turns(v, turn)


class EmbeddingLoads:

    def __init__(self, nc, keep, p, ple_proj):
        self.p, self.proj, self.KP = p, ple_proj, p.shape[1] // P
        self.rows = keep.enter_context(nc.sbuf_tensor("embed_p_rows", [P, p.shape[0] // P, p.shape[1]], F32,
                                                       side="right"))
        self.weights = keep.enter_context(nc.sbuf_tensor("embed_weights", [P, self.KP, ple_proj.shape[1]], F32,
                                                          side="right"))
        self.rows_in, self.weights_in = nc.alloc_semaphore("embed_rows_in"), nc.alloc_semaphore("embed_weights_in")

    def ahead(self, sp):
        sp.dma_start(self.rows[:], self.p.rearrange("(t q) n -> q t n", q=P)).then_inc(self.rows_in, 16)
        sp.dma_start(self.weights[:], self.proj.rearrange("(k p) n -> p k n", p=P)).then_inc(self.weights_in, 16)


def combine(nc, C, R, y_dram, x_rows, sums, loads, emb):
    NT, D = x_rows.shape[1], x_rows.shape[2]
    KP, CB, BANKS = loads.KP, D // BANK, 6
    with Stage(nc, "combine") as st:
        y = st.sb("y", [P, 4, D])
        p_T = st.sb("p_T", [P, KP, NT * P])
        ps = st.psum()
        landed = [st.sem(f"landed{n}") for n in range(4)]
        square = st.sb("square", [P, D])
        added, turned, kept, product, taken, squared = (st.sem(n) for n in ("added", "turned", "kept", "product",
                                                                            "taken", "squared"))
        block = st.block()

        @block.gpsimd
        def _(pool):
            for i in range(2 * NT):
                t, n = i // 2, i % 2
                if i >= 4:
                    pool.wait_ge(added, i - 3)
                pool.indirect_dma_start(out=y[:, i % 4, :], out_offset=None, in_=y_dram,
                                        in_offset=bass.IndirectOffsetOnAxis(ap=R["slot"][:, n, t:t + 1], axis=0)
                                        ).then_inc(landed[i % 4], 16)

        @block.vector
        def _(v):
            for i in range(2 * NT):
                t, n = i // 2, i % 2
                v.wait_ge(landed[i % 4], 16 * (i // 4 + 1))
                signal(v, v.scalar_tensor_tensor(x_rows[:, t, :], y[:, i % 4, :], R["weight"][:, n, t:t + 1],
                                                 x_rows[:, t, :], ALU.mult, ALU.add), added, i + 1)

        @block.tensor
        def _(pe):
            pe.wait_ge(loads.rows_in, 16)
            for k in range(KP):
                for t in range(NT):
                    ins = pe.transpose(ps[:, k, t * P:(t + 1) * P], loads.rows[:, t, k * P:(k + 1) * P],
                                       C["ident"][:])
                ins.then_inc(turned, 1)
            pe.wait_ge(loads.weights_in, 16)
            pe.wait_ge(kept, KP)
            for i in range(NT * CB):
                t, c = i // CB, i % CB
                if i >= BANKS:
                    pe.wait_ge(taken, i - BANKS + 1)
                for k in range(KP):
                    ins = pe.matmul(ps[:, 2 + i % BANKS, :], p_T[:, k, t * P:(t + 1) * P],
                                    loads.weights[:, k, c * BANK:(c + 1) * BANK], start=(k == 0), stop=(k == KP - 1))
                ins.then_inc(product, 1)

        @block.scalar
        def _(act):
            for k in range(KP):
                act.wait_ge(turned, k + 1)
                act.activation(p_T[:, k, :], ps[:, k, :], ACT.Copy).then_inc(kept, 1)
            for i in range(NT * CB):
                t, c = i // CB, i % CB
                act.wait_ge(product, i + 1)
                act.activation(emb[:, t, c * BANK:(c + 1) * BANK], ps[:, 2 + i % BANKS, :], ACT.Copy
                               ).then_inc(taken, 1)
                if c == CB - 1:
                    act.wait_ge(added, 2 * t + 2)
                    signal(act, act.activation(square[:], x_rows[:, t, :], ACT.Square, accum_out=sums[:, t, :]),
                           squared, t + 1)


def layer_embedding(nc, C, gate_ring, ple_norm_g, x_rows, x_parts, emb, out):
    NT, D = x_rows.shape[1], x_rows.shape[2]
    N_SIG = 3
    HALVES = D // 1024
    TILES = 8 * HALVES
    cols = lambda half, b: slice(half * 1024 + (b % 2) * BANK, half * 1024 + (b % 2 + 1) * BANK)

    def setup(st):
        extra = {n: st.sem(n) for n in ("gate", "g_in", "squared", "gained", "inverse", "rooted", "done", "stored",
                                        "steps")}
        extra["sig"] = st.sb("sig", [P, N_SIG, BANK])
        extra["ss"] = st.sb("ss", [P, NT, 2 * HALVES])
        extra["rs"] = st.sb("rs", [P, NT])
        extra["gain_rows"] = st.sb("gain_rows", [P, D])
        extra["square"] = st.sb("square", [P, BANK])
        return extra

    def sync(sp, X):
        sp.dma_start(X["gain_rows"][:], ple_norm_g.rearrange("(o n) -> o n", o=1).to_broadcast([P, D])
                     ).then_inc(X["g_in"], 16)

    def gate_scalar(act, half, b, ps, X, taken_v):
        i = half * 8 + b
        if i >= N_SIG:
            act.wait_ge(taken_v, i - N_SIG + 1)
        act.activation(X["sig"][:, i % N_SIG, :], ps[:, b, :], ACT.Sigmoid).then_inc(X["gate"], 1)
        if i:
            take_square(act, i - 1, X, taken_v)

    def take_square(act, i, X, taken_v):
        half, b = divmod(i, 8)
        act.wait_ge(taken_v, i + 1)
        signal(act, act.activation(X["square"][:], emb[:, b // 2, cols(half, b)], ACT.Square,
                                   accum_out=X["ss"][:, b // 2, 2 * half + b % 2:2 * half + b % 2 + 1]),
               X["squared"], i + 1)

    def vector(v, half, b, ps, X, done):
        i = half * 8 + b
        v.wait_ge(X["gate"], i + 1)
        v.tensor_tensor(emb[:, b // 2, cols(half, b)], emb[:, b // 2, cols(half, b)], X["sig"][:, i % N_SIG, :],
                        ALU.mult).then_inc(done, 1)

    def pool(eng, X):
        eng.wait_ge(X["g_in"], 16)
        for i in range(TILES):
            half, b = divmod(i, 8)
            eng.wait_ge(X["squared"], i + 1)
            tile = emb[:, b // 2, cols(half, b)]
            eng.tensor_tensor(tile, tile, X["gain_rows"][:, cols(half, b)], ALU.mult).then_inc(X["gained"], 1)

    def finish_vector(v, X, taken_v, taken_s):
        v.wait_ge(X["squared"], TILES)
        do = Chain(v, X["steps"])
        do(v.tensor_reduce(X["rs"][:].unsqueeze(2), X["ss"][:], AX_X, ALU.add))
        do(v.tensor_scalar(X["rs"][:], X["rs"][:], 1.0 / D, RMS_EPS, ALU.mult, ALU.add))
        signal(v, v.reciprocal(X["rs"][:], X["rs"][:]), X["inverse"], 1)
        v.wait_ge(X["rooted"], 1)
        for t in range(NT):
            v.wait_ge(X["gained"], TILES - 8 + 2 * t + 2)
            v.scalar_tensor_tensor(emb[:, t, :], emb[:, t, :], X["rs"][:, t:t + 1], x_rows[:, t, :],
                                   ALU.mult, ALU.add).then_inc(X["done"], 1)

    def finish_scalar(act, X, taken_v, taken_s):
        take_square(act, TILES - 1, X, taken_v)
        act.wait_ge(X["inverse"], 1)
        act.activation(X["rs"][:], X["rs"][:], ACT.Sqrt).then_inc(X["rooted"], 1)

    def store(sp, X):
        for t in range(NT):
            sp.wait_ge(X["done"], t + 1)
            sp.dma_start(out[t * P:(t + 1) * P, :], emb[:, t, :]).then_inc(X["stored"], 16)
        sp.wait_ge(X["stored"], 16 * NT)

    project_rows(nc, "gate", None, gate_ring, vector, split=True, parts=x_parts, setup=setup, sync=sync, finish=(finish_vector, finish_scalar),
                 scalar_first=gate_scalar, pool=pool, sync_end=store)


def layer(nc, x, p, ln1_g, w_in, sb_q_g, sb_k_g, sb_out_g, rw_mu, rw_w0, rw_w2, rw_a0, rw_a2, rw_g2, rw_k_k,
          rw_k_a, rw_r_k, rw_ln_g, rw_ln_b, w_out, ln2_g, router_g, router_g_b, router_e, router_e_b, w_up, w_down,
          ple_proj, ple_gate, ple_norm_g, out):
    S, D = x.shape
    KT, NT = D // P, S // P
    SB = D // 2
    E = w_up.shape[0]
    max_items = (2 * S - 1) // SLOTS
    slots = (E + max_items) * SLOTS
    rows_dram = nc.dram_tensor("normed_rows", (S, D), F32, kind="Internal").ap()
    y_dram = nc.dram_tensor("expert_rows", (slots, D), F32, kind="Internal").ap()
    token_table = nc.dram_tensor("token_table", (slots, 16), I32, kind="Internal").ap()
    mixed_dram = nc.dram_tensor("attention_out", (P, SB // P, S), F32, kind="Internal").ap()
    with ExitStack() as keep:
        C = constant_tensors(nc, keep)
        sums, sums_out = (keep.enter_context(nc.sbuf_tensor(n, [P, S // P, m], F32)) for n, m in (
            ("row_sums", 1), ("row_sums_out", D // BANK)))
        hold = lambda stack, name, shape, dt=F32: stack.enter_context(nc.sbuf_tensor(name, shape, dt))
        with ExitStack() as mixed_life:
            with ExitStack() as norm_life:
                mix_w = MixWeights(nc, norm_life, w_in[:, 3 * SB:], rw_mu, rw_w0, rw_a0, rw_k_k, rw_k_a, rw_r_k,
                                   rw_ln_g, rw_ln_b, D - SB, rw_g2.shape[0] - P)
                with ExitStack() as parts_life:
                    norm_parts = [hold(parts_life, f"norm_{n}", [P, KT, S], F32R) for n in ("high", "low")]
                    with ExitStack() as v_life:
                        v_rows = hold(v_life, "v_rows", [P, NT, SB])
                        head_w = HeadWeights(nc, v_life, w_in, KT, SB)
                        with ExitStack() as ring_life:
                            value_ring = Ring(nc, ring_life, "values", w_in[:, 2 * SB:3 * SB])
                            with ExitStack() as rows_life:
                                rows = hold(rows_life, "rows", [P, NT, D])
                                constants(nc, C, x, rows, sums,
                                          norm_parts[0][:, 0:D // S, :].rearrange("p k s -> p (k s)"),
                                          value_ring.ahead)
                                norm_transpose(nc, "norm1", C, rows, sums, norm_parts[0], gain=ln1_g,
                                               out_low=norm_parts[1])
                            value_projection(nc, norm_parts, value_ring, v_rows, token_table, y_dram, E * SLOTS,
                                             head_w.ahead)
                        attention(nc, C, norm_parts, head_w, v_rows, sb_q_g, sb_k_g, sb_out_g, mixed_dram, SB // P,
                                  mix_w.ahead)
                    mixed_T = mixed_life.enter_context(nc.sbuf_tensor("mixed_T", [P, (D - SB) // P, S], F32,
                                                                      side="right"))
                    time_mix(nc, C, norm_parts, mix_w, rw_w2, rw_a2, rw_g2, mixed_T, D - SB)
            x_rows = hold(keep, "x_rows", [P, NT, D])
            out_ring = Ring(nc, mixed_life, "out", w_out, first=SB // P // Ring.SLOT)
            output_projection(nc, mixed_dram, mixed_T, out_ring, x, x_rows, sums_out)
        R = {"max_items": max_items,
             "slot": hold(keep, "slot", [P, 2, NT], I32), "weight": hold(keep, "weight", [P, 2, NT]),
             "n_items": hold(keep, "n_items", [P, 1], I32),
             "item_expert": hold(keep, "item_expert", [1, P], I32)}
        with ExitStack() as embed_life:
            with ExitStack() as moe_life:
                expert_w = ExpertWeights(nc, moe_life, w_up, w_down)
                with ExitStack() as hn_life:
                    hn_T = hold(hn_life, "hn_T", [P, KT, S])
                    norm_transpose(nc, "norm2", C, x_rows, sums_out, hn_T, gain=ln2_g, rows_dram=rows_dram)
                    route(nc, C, hn_T, router_g, router_g_b, router_e, router_e_b, R, token_table, expert_w.ahead)
                embedding = EmbeddingLoads(nc, embed_life, p, ple_proj)
                experts(nc, C, ln2_g, expert_w, E, D, w_up.shape[2], R, token_table, rows_dram, y_dram,
                        embedding.ahead)
            emb = hold(keep, "emb", [P, NT, D])
            gate_ring = Ring(nc, keep, "gate", ple_gate)
            combine(nc, C, R, y_dram, x_rows, sums, embedding, emb)
        x_parts = hold(keep, "x_high", [P, KT, S], F32R), hold(keep, "x_low", [P, KT, S], F32R)
        norm_transpose(nc, "norm3", C, x_rows, sums, x_parts[0], out_low=x_parts[1],
                       ahead=gate_ring.ahead)
        layer_embedding(nc, C, gate_ring, ple_norm_g, x_rows, x_parts, emb, out)


def kernel(**inputs):
    import numpy as np
    import concourse.bacc as bacc
    from concourse.bass_utils import run_bass_kernel_spmd

    names = ["x", "p", "ln1_g", "w_in", "sb_q_g", "sb_k_g", "sb_out_g", "rw_mu", "rw_w0", "rw_w2", "rw_a0", "rw_a2",
             "rw_g2", "rw_k_k", "rw_k_a", "rw_r_k", "rw_ln_g", "rw_ln_b", "w_out", "ln2_g", "router_g", "router_g_b",
             "router_e", "router_e_b", "w_up", "w_down", "ple_proj", "ple_gate", "ple_norm_g"]
    shape = inputs["x"].shape
    nc = bacc.Bacc("TRN2", target_bir_lowering=False, num_devices=1)
    arrays, args = {}, []
    for name in names:
        a = np.ascontiguousarray(inputs[name])[0]
        if name == "p":
            a = a[0]
        if name == "rw_r_k":
            a = a.reshape(-1)
        a = np.ascontiguousarray(a)
        arrays[f"in_{name}"] = a
        args.append(nc.dram_tensor(f"in_{name}", a.shape, mybir.dt.from_np(a.dtype), kind="ExternalInput").ap())
    out = nc.dram_tensor("out", shape[1:], F32, kind="ExternalOutput").ap()
    layer(nc, *args, out)
    r = run_bass_kernel_spmd(nc, [arrays], core_ids=[0])
    return r.results[0]["out"].reshape(shape)
```
